# Optimizing a Trainium2 kernel written in Bass

```python
import math
import jax
import jax.numpy as jnp
from jax import lax
import numpy as np

D_MODEL = 1024
BATCH = 1
SEQ = 512
DEPTH = 2
DEC_BATCH = 1
DEC_SEQ = 64
PAST_LEN = 1024

CHUNK = 64
N_A = DEPTH // 2
N_B = DEPTH - N_A
GROUP = 16
N_GROUPS = D_MODEL // GROUP
P_STATE = 64
HEAD_DIM = 64
V_DIM = 2 * HEAD_DIM
N_HEADS = D_MODEL // V_DIM
D_FF = ((8 * D_MODEL // 3 + 127) // 128) * 128
ROPE_THETA = 10000.0
Q_BLOCK = 128
ALPHA = (2 * DEPTH) ** 0.25
BETA = (8 * DEPTH) ** -0.25
LN_EPS = 1e-5
RMS_EPS = 1e-5

kernel_name = 'yoco_s5_diffattn_streaming_step'

def layer_norm(x, g, b):
    xf = x.astype(jnp.float32)
    mu = jnp.mean(xf, axis=-1, keepdims=True)
    var = jnp.mean(jnp.square(xf - mu), axis=-1, keepdims=True)
    return ((xf - mu) * lax.rsqrt(var + LN_EPS) * g + b).astype(x.dtype)

def swiglu(x, w_in, w_out):
    a, gate = jnp.split(x @ w_in, 2, axis=-1)
    return (jax.nn.silu(a) * gate) @ w_out

def rope(x, pos):
    half = HEAD_DIM // 2
    inv = ROPE_THETA ** (-jnp.arange(half, dtype=jnp.float32) / half)
    ang = pos.astype(jnp.float32)[:, None] * inv[None, :]
    cos = jnp.cos(ang)[:, None, :]
    sin = jnp.sin(ang)[:, None, :]
    xf = x.astype(jnp.float32)
    x1, x2 = xf[..., :half], xf[..., half:]
    return jnp.concatenate([x1 * cos - x2 * sin, x1 * sin + x2 * cos], axis=-1).astype(x.dtype)

def s5_discretise(a_re, a_im, log_dt, b_re, b_im):
    f32 = jnp.float32
    lam_re = jnp.minimum(a_re.astype(f32), -1e-4)
    lam_im = a_im.astype(f32)
    dt = jnp.exp(log_dt.astype(f32))[:, None]
    mag = jnp.exp(lam_re * dt)
    lb_re = mag * jnp.cos(lam_im * dt)
    lb_im = mag * jnp.sin(lam_im * dt)
    den = lam_re * lam_re + lam_im * lam_im
    n_re = lb_re - 1.0
    c_re = (n_re * lam_re + lb_im * lam_im) / den
    c_im = (lb_im * lam_re - n_re * lam_im) / den
    b_re = b_re.astype(f32)
    b_im = b_im.astype(f32)
    bb_re = c_re[..., None] * b_re - c_im[..., None] * b_im
    bb_im = c_re[..., None] * b_im + c_im[..., None] * b_re
    return lb_re, lb_im, bb_re, bb_im

def complex_affine_combine(e1, e2):
    a1r, a1i, b1r, b1i = e1
    a2r, a2i, b2r, b2i = e2
    return (a2r * a1r - a2i * a1i,
            a2r * a1i + a2i * a1r,
            a2r * b1r - a2i * b1i + b2r,
            a2r * b1i + a2i * b1r + b2i)

def s5_mixer(x, h0_re, h0_im, a_re, a_im, log_dt, b_re, b_im, c_re, c_im, d_skip, w_glu):
    B, L, _ = x.shape
    f32 = jnp.float32
    lb_re, lb_im, bb_re, bb_im = s5_discretise(a_re, a_im, log_dt, b_re, b_im)
    c_re = c_re.astype(f32)
    c_im = c_im.astype(f32)
    blk = min(CHUNK, L)
    n_blk = L // blk
    u = x.astype(f32)
    u_blocks = u.reshape(B, n_blk, blk, N_GROUPS, GROUP).transpose(1, 0, 2, 3, 4)

    def block_step(carry, u_blk):
        h_re, h_im = carry
        bu_re = jnp.einsum('gpc,btgc->btgp', bb_re, u_blk)
        bu_im = jnp.einsum('gpc,btgc->btgp', bb_im, u_blk)
        bu_re = bu_re.at[:, 0].add(lb_re * h_re - lb_im * h_im)
        bu_im = bu_im.at[:, 0].add(lb_re * h_im + lb_im * h_re)
        a_r = jnp.broadcast_to(lb_re, bu_re.shape)
        a_i = jnp.broadcast_to(lb_im, bu_im.shape)
        _, _, hs_re, hs_im = lax.associative_scan(complex_affine_combine, (a_r, a_i, bu_re, bu_im), axis=1)
        y_blk = jnp.einsum('gcp,btgp->btgc', c_re, hs_re) - jnp.einsum('gcp,btgp->btgc', c_im, hs_im)
        return (hs_re[:, -1], hs_im[:, -1]), y_blk

    (h_re, h_im), y = lax.scan(block_step, (h0_re.astype(f32), h0_im.astype(f32)), u_blocks)
    y = y.transpose(1, 0, 2, 3, 4).reshape(B, L, D_MODEL) + d_skip.astype(f32) * u
    z = jax.nn.gelu(y).astype(x.dtype)
    out, gate = jnp.split(z @ w_glu, 2, axis=-1)
    return out * jax.nn.sigmoid(gate), h_re, h_im

def shared_kv(h, pos, w_kv):
    B, L, _ = h.shape
    k, v = jnp.split(h @ w_kv, 2, axis=-1)
    k = rope(k.reshape(B, L, 2 * N_HEADS, HEAD_DIM), pos).reshape(B, L, N_HEADS, 2, HEAD_DIM)
    return k, v.reshape(B, L, N_HEADS, V_DIM)

def diff_attend(q, q_pos, segments, lam):
    scale = HEAD_DIM ** -0.5
    scores = []
    for k, _, k_pos in segments:
        s = jnp.einsum('bqhmd,bkhmd->bhmqk', q, k).astype(jnp.float32) * scale
        visible = (k_pos[None, :] // CHUNK) <= (q_pos[:, None] // CHUNK)
        scores.append(jnp.where(visible, s, -1e30))
    p = jax.nn.softmax(jnp.concatenate(scores, axis=-1), axis=-1)
    p = p[:, :, 0] - lam * p[:, :, 1]
    out = 0.0
    start = 0
    for k, v, _ in segments:
        n = k.shape[1]
        out = out + jnp.einsum('bhqk,bkhe->bqhe', p[..., start:start + n].astype(v.dtype), v)
        start += n
    return out

def diff_attention(x, pos, k_sh, v_sh, k_past, v_past, pos_past, w_q, lam_vec, subln_g, w_o, layer_idx):
    B, L, _ = x.shape
    q = rope((x @ w_q).reshape(B, L, 2 * N_HEADS, HEAD_DIM), pos).reshape(B, L, N_HEADS, 2, HEAD_DIM)
    lam_init = 0.8 - 0.6 * math.exp(-0.3 * layer_idx)
    lv = lam_vec.astype(jnp.float32)
    lam = jnp.exp(jnp.sum(lv[0] * lv[1])) - jnp.exp(jnp.sum(lv[2] * lv[3])) + lam_init
    segments = [(k_sh, v_sh, pos)]
    if k_past is not None:
        segments = [(k_past, v_past, pos_past)] + segments
    if L <= Q_BLOCK:
        o = diff_attend(q, pos, segments, lam)
    else:
        n_qb = L // Q_BLOCK
        q_blocks = q.reshape(B, n_qb, Q_BLOCK, N_HEADS, 2, HEAD_DIM).transpose(1, 0, 2, 3, 4, 5)
        pos_blocks = pos.reshape(n_qb, Q_BLOCK)
        o = lax.map(lambda qp: diff_attend(qp[0], qp[1], segments, lam), (q_blocks, pos_blocks))
        o = o.transpose(1, 0, 2, 3, 4).reshape(B, L, N_HEADS, V_DIM)
    of = o.astype(jnp.float32)
    of = of * lax.rsqrt(jnp.mean(of * of, axis=-1, keepdims=True) + RMS_EPS) * subln_g * (1.0 - lam_init)
    return of.astype(x.dtype).reshape(B, L, D_MODEL) @ w_o

def run_trunk(x, pos, h0_re, h0_im, k_past, v_past, pos_past, w):
    new_re, new_im = [], []
    k_sh = v_sh = None
    for l in range(DEPTH):
        if l == N_A:
            k_sh, v_sh = shared_kv(x, pos, w['attn_w_kv'])
        g, b = w['ln_g'][l], w['ln_b'][l]
        x = layer_norm(ALPHA * x + 0.5 * swiglu(x, w['ffn_w_in'][l, 0], w['ffn_w_out'][l, 0]), g[0], b[0])
        if l < N_A:
            y, hr, hi = s5_mixer(x, h0_re[l], h0_im[l], w['ssm_a_re'][l], w['ssm_a_im'][l], w['ssm_log_dt'][l],
                                 w['ssm_b_re'][l], w['ssm_b_im'][l], w['ssm_c_re'][l], w['ssm_c_im'][l],
                                 w['ssm_d'][l], w['ssm_w_glu'][l])
            new_re.append(hr)
            new_im.append(hi)
        else:
            j = l - N_A
            y = diff_attention(x, pos, k_sh, v_sh, k_past, v_past, pos_past, w['attn_w_q'][j], w['attn_lam'][j],
                               w['attn_subln_g'][j], w['attn_w_o'][j], l)
        x = layer_norm(ALPHA * x + y, g[1], b[1])
        x = layer_norm(ALPHA * x + 0.5 * swiglu(x, w['ffn_w_in'][l, 1], w['ffn_w_out'][l, 1]), g[2], b[2])
    return x, jnp.stack(new_re), jnp.stack(new_im), k_sh, v_sh

def setup_inputs(seed: int = 0) -> dict:
    key = jax.random.key(seed)
    ks = jax.random.split(key, 24)
    f32 = jnp.float32

    def nrm(k, shape, s):
        return jax.random.normal(k, shape, f32) * s

    D = D_MODEL
    x_prompt = nrm(ks[0], (BATCH, SEQ, D), 1.0)
    x_sample = nrm(ks[1], (DEC_BATCH, DEC_SEQ, D), 1.0)
    cache_k = nrm(ks[2], (DEC_BATCH, PAST_LEN, N_HEADS, 2, HEAD_DIM), 1.0)
    cache_v = nrm(ks[3], (DEC_BATCH, PAST_LEN, N_HEADS, V_DIM), 1.0)
    state_ssm_re = nrm(ks[4], (N_A, DEC_BATCH, N_GROUPS, P_STATE), 0.1)
    state_ssm_im = nrm(ks[5], (N_A, DEC_BATCH, N_GROUPS, P_STATE), 0.1)
    ln_g = 1.0 + nrm(ks[6], (DEPTH, 3, D), 0.01)
    ln_b = nrm(ks[7], (DEPTH, 3, D), 0.01)
    ffn_w_in = nrm(ks[8], (DEPTH, 2, D, 2 * D_FF), D ** -0.5)
    ffn_w_out = nrm(ks[9], (DEPTH, 2, D_FF, D), (D_FF ** -0.5) * BETA)
    ssm_a_re = -0.5 + nrm(ks[10], (N_A, N_GROUPS, P_STATE), 0.01)
    ssm_a_im = math.pi * jnp.arange(P_STATE, dtype=f32) + nrm(ks[11], (N_A, N_GROUPS, P_STATE), 0.01)
    ssm_log_dt = jax.random.uniform(ks[12], (N_A, N_GROUPS), f32, math.log(1e-3), math.log(1e-1))
    ssm_b_re = nrm(ks[13], (N_A, N_GROUPS, P_STATE, GROUP), (2 * GROUP) ** -0.5)
    ssm_b_im = nrm(ks[14], (N_A, N_GROUPS, P_STATE, GROUP), (2 * GROUP) ** -0.5)
    ssm_c_re = nrm(ks[15], (N_A, N_GROUPS, GROUP, P_STATE), P_STATE ** -0.5)
    ssm_c_im = nrm(ks[16], (N_A, N_GROUPS, GROUP, P_STATE), P_STATE ** -0.5)
    ssm_d = nrm(ks[17], (N_A, D), 1.0)
    glu_scale = jnp.concatenate([jnp.full((D,), BETA, f32), jnp.ones((D,), f32)])
    ssm_w_glu = nrm(ks[18], (N_A, D, 2 * D), D ** -0.5) * glu_scale
    attn_w_q = nrm(ks[19], (N_B, D, D), D ** -0.5)
    kv_scale = jnp.concatenate([jnp.ones((D,), f32), jnp.full((D,), BETA, f32)])
    attn_w_kv = nrm(ks[20], (D, 2 * D), D ** -0.5) * kv_scale
    attn_lam = nrm(ks[21], (N_B, 4, HEAD_DIM), 0.1)
    attn_subln_g = 1.0 + nrm(ks[22], (N_B, V_DIM), 0.01)
    attn_w_o = nrm(ks[23], (N_B, D, D), (D ** -0.5) * BETA)
    return {'x_prompt': x_prompt, 'x_sample': x_sample, 'cache_k': cache_k, 'cache_v': cache_v,
            'state_ssm_re': state_ssm_re, 'state_ssm_im': state_ssm_im,
            'ln_g': ln_g, 'ln_b': ln_b, 'ffn_w_in': ffn_w_in, 'ffn_w_out': ffn_w_out,
            'ssm_a_re': ssm_a_re, 'ssm_a_im': ssm_a_im, 'ssm_log_dt': ssm_log_dt,
            'ssm_b_re': ssm_b_re, 'ssm_b_im': ssm_b_im, 'ssm_c_re': ssm_c_re, 'ssm_c_im': ssm_c_im,
            'ssm_d': ssm_d, 'ssm_w_glu': ssm_w_glu,
            'attn_w_q': attn_w_q, 'attn_w_kv': attn_w_kv, 'attn_lam': attn_lam,
            'attn_subln_g': attn_subln_g, 'attn_w_o': attn_w_o}

def reference(x_prompt, x_sample, cache_k, cache_v, state_ssm_re, state_ssm_im,
              ln_g, ln_b, ffn_w_in, ffn_w_out,
              ssm_a_re, ssm_a_im, ssm_log_dt, ssm_b_re, ssm_b_im, ssm_c_re, ssm_c_im, ssm_d, ssm_w_glu,
              attn_w_q, attn_w_kv, attn_lam, attn_subln_g, attn_w_o):
    w = {'ln_g': ln_g, 'ln_b': ln_b, 'ffn_w_in': ffn_w_in, 'ffn_w_out': ffn_w_out,
         'ssm_a_re': ssm_a_re, 'ssm_a_im': ssm_a_im, 'ssm_log_dt': ssm_log_dt,
         'ssm_b_re': ssm_b_re, 'ssm_b_im': ssm_b_im, 'ssm_c_re': ssm_c_re, 'ssm_c_im': ssm_c_im,
         'ssm_d': ssm_d, 'ssm_w_glu': ssm_w_glu,
         'attn_w_q': attn_w_q, 'attn_w_kv': attn_w_kv, 'attn_lam': attn_lam,
         'attn_subln_g': attn_subln_g, 'attn_w_o': attn_w_o}
    b_p, l_p, _ = x_prompt.shape
    pos_p = jnp.arange(l_p, dtype=jnp.int32)
    h0 = jnp.zeros((N_A, b_p, N_GROUPS, P_STATE), jnp.float32)
    y_prompt, p_ssm_re, p_ssm_im, p_k, p_v = run_trunk(x_prompt, pos_p, h0, h0, None, None, None, w)
    past = cache_k.shape[1]
    pos_past = jnp.arange(past, dtype=jnp.int32)
    pos_s = past + jnp.arange(x_sample.shape[1], dtype=jnp.int32)
    y_sample, s_ssm_re, s_ssm_im, s_k, s_v = run_trunk(x_sample, pos_s, state_ssm_re, state_ssm_im,
                                                       cache_k, cache_v, pos_past, w)
    return (y_prompt, y_sample, p_ssm_re, p_ssm_im, p_k, p_v, s_ssm_re, s_ssm_im, s_k, s_v)


_drawn_inputs = setup_inputs


def setup_inputs(seed=0):
    import zlib

    import numpy as np

    out = dict(_drawn_inputs(seed))
    spreads = {}
    factors = {'ssm_a_re': 3.982, 'ssm_c_re': 5.007, 'ssm_c_im': 5.048, 'attn_subln_g': 8.0}
    for name, (base, spread) in spreads.items():
        noise = np.random.default_rng([zlib.crc32(name.encode()), seed]).standard_normal(out[name].shape)
        drawn = base * np.exp(spread * noise) if base else spread * noise
        out[name] = jnp.asarray(drawn.astype(out[name].dtype))
    for name, factor in factors.items():
        out[name] = (out[name] * factor).astype(out[name].dtype)
    return out
```

```python
import math
from contextlib import ExitStack

import numpy as np

import concourse.bass as bass
from concourse import mybir

F32 = mybir.dt.float32
F32R = mybir.dt.float32r
I32 = mybir.dt.int32
ALU = mybir.AluOpType
ACT = mybir.ActivationFunctionType
AX = mybir.AxisListType

P = 128
D = 1024
DT = D // P
SEQ, DEC, PAST = 512, 64, 1024
T = SEQ + DEC
HALF = T // 2
DEPTH = 2
FF = ((8 * D // 3 + 127) // 128) * 128
FT = FF // P
FH = FT // 2
CHUNK = 64
HD, NH = 64, 8
GROUPS, GC, PS = 64, 16, 64
NPAIR = GROUPS // 2
BLK = 8
NB = T // BLK
NBP = SEQ // BLK
ALPHA = (2 * DEPTH) ** 0.25
LN_EPS = RMS_EPS = 1e-5
SCALE = HD ** -0.5
TT = [(i * P, min(P, T - i * P)) for i in range(5)]
NCEN = 6

FFN_TILES = 2 * (2 * FH + DT)
N_FFN00 = 0
N_GLU = N_FFN00 + FFN_TILES
N_FFN01 = N_GLU + 2 * DT
N_KV = N_FFN01 + FFN_TILES
N_FFN10 = N_KV + 2 * DT
N_Q = N_FFN10 + FFN_TILES
N_O = N_Q + DT
N_FFN11 = N_O + DT
N_TILES = N_FFN11 + FFN_TILES

X_IN, X_GELU, X_LN1, X_LN2, X_LN3, X_ATT, X_LN4 = (8 * i for i in range(7))
TWO_PI_1 = 6.28125
TWO_PI_2 = float(np.float32(2 * math.pi - TWO_PI_1))
TWO_PI_3 = float(2 * math.pi - TWO_PI_1 - TWO_PI_2)
LN2_1 = 0.693359375
LN2_2 = math.log(2) - LN2_1
ROUND = 1.5 * 2.0 ** 23
LAM_INIT = 0.8 - 0.6 * math.exp(-0.3 * 1)


def unit_rows(n):
    for base in (N_FFN00, N_FFN01, N_FFN10, N_FFN11):
        if base <= n < base + FFN_TILES:
            return DT if (n - base) % (2 * FH + DT) < 2 * FH else FH
    return DT


def pairs(eng, count, body, peel_first=False):
    first = 0
    if peel_first:
        body(0)
        first = 1
    if count - 1 - first > 1:
        with eng.Fori(first, count - 1) as i:
            body(i)
    else:
        for i in range(first, count - 1):
            body(i)
    body(count - 1)


def peeled(eng, count, body, peel):
    at = 0
    for stop_ in sorted(peel) + [count]:
        if stop_ - at == 1:
            body(at)
        elif stop_ > at:
            with eng.Fori(at, stop_) as i:
                body(i)
        if stop_ < count:
            body(stop_)
        at = stop_ + 1


def wait(eng, sem, value):
    if isinstance(value, int) and value <= 0:
        return
    eng.wait_ge(sem, value)


def build(nc, x_prompt, x_sample, cache_k, cache_v, state_re, state_im, ln_g, ln_b, w_in, w_out,
          a_re, a_im, log_dt, b_re, b_im, c_re, c_im, ssm_d, w_glu, w_q, w_kv, attn_lam, subln_g,
          w_o, rope_cos, rope_sin,
          y_prompt, y_sample, p_re, p_im, p_k, p_v, s_re, s_im, s_k, s_v, stop=99, dump=None):
    ctx = ExitStack()
    with ctx:
        n_tiles = {1: N_GLU, 2: N_FFN01, 3: N_KV, 4: N_Q, 5: N_FFN11}.get(stop, N_TILES)

        def sem(name):
            return ctx.enter_context(nc.semaphore(name))

        start = (nc.sbuf_base + 31) // 32 * 32
        room = nc.sbuf_usable_end - start - 64
        ctx.enter_context(nc.sbuf_tensor("slab", [P, room], mybir.dt.uint8))

        class Map:

            def __init__(self, at):
                self.at = at

            def __call__(self, name, shape, dt=F32):
                size = 4 * int(np.prod(shape[1:]))
                t = nc.alloc_sbuf_tensor_at(name, shape, dt, offset=self.at)
                self.at += (size + 31) // 32 * 32
                assert self.at <= start + room, (name, self.at - start, room)
                return t

        keep = Map(start)
        r = keep("r", [P, DT, T])
        x_at = keep.at
        xh = keep("xh", [P, DT, T], F32R)
        xl = keep("xl", [P, DT, T], F32R)
        raw = [keep(f"raw{s}", [P, FH, P]) for s in range(2)]
        wh = [keep(f"wh{s}", [P, FH, P], F32R) for s in range(2)]
        wl = [keep(f"wl{s}", [P, FH, P], F32R) for s in range(2)]
        ones = keep("ones", [P, P])
        maskrow = keep("maskrow", [1, P + CHUNK])
        ident = keep("ident", [P, P])
        vec = keep("vec", [P, P])
        small = keep("small", [P, 16])
        cosT = keep("cosT", [P, T])
        sinT = keep("sinT", [P, T])
        cb = keep("cb", [P, T])
        zc = keep("zc", [P, T])
        zq = keep("zq", [P, T])
        sq = [keep(f"sq{s}", [P, T]) for s in range(2)]
        rstd = keep("rstd", [P, T])
        sil = keep("sil", [P, T])
        hf = keep("hf", [P, T])
        h_at = keep.at
        fm = Map(h_at)
        hh = fm("hh", [P, FH, T], F32R)
        hl = fm("hl", [P, FH, T], F32R)
        k_at = fm.at
        km = Map(k_at)
        kT = km("kT", [P, NH, T])
        vtok = km("vtok", [P, 5, D])

        im = Map(h_at)
        xtok = im("xtok", [P, 5, D])
        rows = im("rows", [P, 2, P])
        rows2 = im("rows2", [P, P])
        dtrow = im("dtrow", [NPAIR, 2])
        gm = Map(k_at)
        vs = gm("vs", [P, 5, NPAIR])
        lp = gm("lp", [P, 2, NPAIR, BLK + 1])
        s5_at = gm.at
        lpr = gm("lpr", [P, 2, NPAIR, BLK])
        bbar = gm("bbar", [P, 2, NPAIR, GC])
        cmat = gm("cmat", [P, 3, NPAIR, GC])
        pm = Map(gm.at)
        ebuf = gm("ebuf", [P, 2, 4, BLK, 2, GC])
        cp = gm("cp", [P, 2, 4, BLK + 1, 2, GC])
        wt = gm("wt", [P, 2, 4, 2, P])
        tt = gm("tt", [P, 4, BLK, 32])
        tmp = pm("tmp", [P, 20, NPAIR])
        kint = pm("kint", [P, NPAIR], I32)
        braw = pm("braw", [P, 2, NPAIR, GC])
        craw = pm("craw", [P, 2, DT, 2, PS])
        lamv = pm("lamv", [P, 4, HD])
        prod = [cb, zc]
        prodc = [zq, sq[0], sq[1], rstd]

        am = Map(h_at)
        u4 = am("u4", [P, DT, 4, 2, NB])
        hs = am("hs", [P, 2, NPAIR, NB])
        hlast = am("hlast", [P, 2, NPAIR, 2])
        sm = Map(s5_at)
        wt2 = [sm(f"wt2_{s}", [P, 2, 4, 2, P]) for s in range(2)]
        cp2 = [sm(f"cp2_{s}", [P, 2, 4, BLK, 2, GC]) for s in range(2)]
        tt2 = [sm(f"tt2_{s}", [P, 4, BLK, 32]) for s in range(2)]
        am2 = am
        ysb = am2("ysb", [P, T])
        gel = am2("gel", [P, T])
        sa = am2("sa", [P, 2, NPAIR])
        sb2 = am2("sb2", [P, 2, NPAIR])
        lam8 = am2("lam8", [P, 2, 2, NPAIR])
        stin = am2("stin", [P, 2, NPAIR])
        strow = am2("strow", [NPAIR, 4, P])

        vm = Map(h_at)
        vT = vm("vT", [P, NH, T])
        ktok = [vm(f"ktok{s}", [P, D]) for s in range(2)]
        ytok = [vm(f"ytok{s}", [P, D]) for s in range(2)]

        qm = Map(h_at)
        qT = qm("qT", [P, NH, T])
        otok = qm("otok", [P, 5, D])
        ck = [qm(f"ck{s}", [P, PAST // P, P]) for s in range(2)]
        sts = qm("sts", [P, 2, 16])
        ssq = qm("ssq", [P, 5 * NH])
        nrm = qm("nrm", [P, 2, 5 * NH])
        assert qm.at <= k_at
        cm = Map(km.at)
        cv = [cm(f"cv{s}", [P, PAST // P, P]) for s in range(2)]
        xm2 = Map(x_at)
        ex = [xm2(f"ex{s}", [P, 2, PAST + DEC]) for s in range(2)]
        pT = [xm2(f"pT{s}", [P, T]) for s in range(2)]
        qs = [xm2(f"qs{s}", [P, 2, P]) for s in range(2)]
        kTc = [xm2(f"kTc{s}", [P, PAST]) for s in range(2)]
        assert xm2.at <= x_at + 2 * 4 * DT * T

        ps = ctx.enter_context(nc.psum_tensor("tile_ps", [P, 2, 2, 512], F32))
        misc = ctx.enter_context(nc.psum_tensor("misc", [P, 4, 512], F32))
        mflat = misc[:].rearrange("p b n -> p (b n)")

        scr_w = nc.dram_tensor("scr_w", [DT, P, 2 * 4 * 2 * P], F32).ap()
        scr_c = nc.dram_tensor("scr_c", [DT, P, 2 * 4 * BLK * 32], F32).ap()
        scr_t = nc.dram_tensor("scr_t", [DT, P, 4 * BLK * 32], F32).ap()

        w_loaded = [sem(f"w_loaded{s}") for s in range(2)]
        w_hi = sem("w_hi")
        w_lo = sem("w_lo")
        tile_done = sem("tile_done")
        drained = [sem(f"drained{s}") for s in range(2)]
        hh_ready = sem("hh_ready")
        hl_ready = sem("hl_ready")
        xh_ready = sem("xh_ready")
        x_ready = sem("x_ready")
        ln_sum1 = sem("ln_sum1")
        ln_centre_mm = sem("ln_centre_mm")
        ln_centre = sem("ln_centre")
        ln_centred = sem("ln_centred")
        ln_sq = sem("ln_sq")
        ln_sumc = sem("ln_sumc")
        ln_sumq = sem("ln_sumq")
        ln_mm = sem("ln_mm")
        ln_mean = sem("ln_mean")
        ln_var = sem("ln_var")
        ln_sd = sem("ln_sd")
        ln_scaled = sem("ln_scaled")
        ln_out = sem("ln_out")
        step = sem("step")
        s_x = sem("x_loaded")
        s_small = sem("small_loaded")
        s_const = sem("const_ready")
        s_tp = sem("setup_transposed")
        s_tpc = sem("setup_copied")
        s_r = sem("r_loaded")

        w_in_v = w_in.rearrange("l s (k p) c -> l s p k c", p=P)
        w_out_v = w_out.rearrange("l s (k p) c -> l s p k c", p=P)
        glu_v = w_glu.rearrange("a (k p) c -> (a p) k c", p=P)
        kv_v = w_kv.rearrange("(k p) c -> p k c", p=P)
        q_v = w_q.rearrange("a (k p) c -> (a p) k c", p=P)
        o_v = w_o.rearrange("a (k p) c -> (a p) k c", p=P)

        steps = [0]

        def link(eng, ins):
            steps[0] += 1
            ins.then_inc(step, 1)
            eng.wait_ge(step, steps[0])

        def tile(base, i, odd):
            return 2 * i + (base + odd), i + base // 2, odd

        def sp_stage(sp, base, count, view, a, b, k, between=None):
            def body(i):
                n = tile(base, i, 0)[0]
                wait(sp, w_lo, n)
                for s, col in enumerate((a, b)):
                    sp.dma_start(raw[s][:, 0:k, :], view[:, :, bass.ds(col(i), P)]).then_inc(w_loaded[s], 16)
                if between is not None and isinstance(i, int) and i == 0:
                    between(sp)
            pairs(sp, count, body, peel_first=base == 0 or between is not None)

        def sp_ffn(sp, base, l, s, between=None):
            for p in range(2):
                f0 = p * FH
                sp_stage(sp, base, FH,
                         w_in_v[l, s], lambda i: (i + f0) * P, lambda i: (i + (f0 + FT)) * P, DT,
                         between=None if p else between)
                base += 2 * FH
                sp_stage(sp, base, DT // 2,
                         w_out_v[l, s][:, f0:f0 + FH], lambda i: i * 2 * P, lambda i: i * 2 * P + P, FH)
                base += DT

        def sp_plain(sp, base, count, view, between=None):
            sp_stage(sp, base, count, view, lambda i: i * 2 * P, lambda i: i * 2 * P + P, DT, between=between)

        def act_hi(act, n, turn, s, k):
            act.wait_ge(w_loaded[s], 16 * turn + 16)
            wait(act, tile_done, n - 1)
            nc.scalar.copy(wh[s][:, 0:k, :], raw[s][:, 0:k, :]).then_inc(w_hi, 1)

        def dve_lo(dve, n, turn, s, k):
            wait(dve, w_hi, n + 1)
            nc.vector.tensor_tensor(wl[s][:, 0:k, :], raw[s][:, 0:k, :],
                                    wh[s][:, 0:k, :].bitcast(F32), ALU.subtract).then_inc(w_lo, 1)

        def ahead(split, eng, base, i, count, k, which):
            n, turn, s = tile(base, i, which + 1) if which == 0 else tile(base + 2, i, 0)
            if which == 1 and isinstance(i, int) and i == count - 1:
                if base + 2 * count >= n_tiles:
                    return
                k = unit_rows(base + 2 * count)
            split(eng, n, turn, s, k)

        def pe_tile(pe, n, turn, s, k, hi, lo, ready, have):
            wait(pe, w_lo, n + 1)
            if not (isinstance(turn, int) and turn == 0):
                pe.wait_ge(drained[s], turn)
            for kk in range(k):
                if ready is not None:
                    pe.wait_ge(ready, have + kk + 1)
                for hf_ in range(2):
                    cols = slice(hf_ * HALF, (hf_ + 1) * HALF)
                    o = ps[:, s, hf_, 0:HALF]
                    nc.tensor.matmul(o, wh[s][:, kk, :], hi[:, kk, cols], start=kk == 0, stop=False)
                    nc.tensor.matmul(o, wh[s][:, kk, :], lo[:, kk, cols], start=False, stop=False)
                    last = nc.tensor.matmul(o, wl[s][:, kk, :], hi[:, kk, cols], start=False,
                                            stop=kk == k - 1)
            last.then_inc(tile_done, 1)

        def pe_stage(pe, base, count, k, hi, lo, ready, have, hooks={}, tables=False):
            def body(i):
                for odd in range(2):
                    if odd:
                        dt = tables_of(0, tables, i, 1)
                        if dt is not None:
                            pe_tables(pe, dt)
                    pe_tile(pe, *tile(base, i, odd), k, hi, lo, ready, have)
                    if isinstance(i, int) and i == count - 1 and odd in hooks:
                        hooks[odd](pe)
            peeled(pe, count, body, beside(0, 1, "pe") if tables else [0, count - 1] if base == 0 else [count - 1])

        def pe_ffn(pe, base, ffn, have, ln):
            for p in range(2):
                pe_stage(pe, base, FH, DT, xh, xl, x_ready, have, tables=ffn == 0 and p == 1)
                base += 2 * FH
                pe_stage(pe, base, DT // 2, FH, hh, hl, hl_ready, (2 * ffn + p) * FH,
                         hooks={0: lambda e: pe_centre(e, ln), 1: lambda e: pe_stats(e, ln)} if p else {})
                base += DT

        halves = [slice(0, HALF), slice(HALF, T)]

        def pe_centre(pe, ln):
            pe.wait_ge(ln_sum1, NCEN * (ln + 1))
            for q in range(2):
                mm = nc.tensor.matmul(misc[:, q, 0:HALF], ones[:], zc[:, halves[q]], start=True, stop=True)
            mm.then_inc(ln_centre_mm, 1)

        def pe_stats(pe, ln):
            pe.wait_ge(ln_sumc, DT * (ln + 1))
            for q in range(2):
                mm = nc.tensor.matmul(misc[:, q, 0:HALF], ones[:], zc[:, halves[q]], start=True, stop=True)
            pe.wait_ge(ln_sumq, DT * (ln + 1))
            for q in range(2):
                mm = nc.tensor.matmul(misc[:, 2 + q, 0:HALF], ones[:], zq[:, halves[q]], start=True, stop=True)
            mm.then_inc(ln_mm, 1)

        def two(t):
            return t[:, :].rearrange("p (h n) -> p h n", h=2)

        def z_ready(eng, d, z):
            eng.wait_ge(*z(d))

        def pool_ln(pool, ln, z, split):
            for d in range(NCEN):
                z_ready(pool, d, z)
                if d == 0:
                    if ln:
                        pool.wait_ge(ln_scaled, 2 * DT * ln)
                    nc.gpsimd.tensor_copy(zc[:, :], r[:, 0, :]).then_inc(ln_sum1, 1)
                else:
                    pool.wait_ge(ln_sum1, NCEN * ln + d)
                    nc.gpsimd.tensor_tensor(zc[:, :], zc[:, :], r[:, d, :], ALU.add).then_inc(ln_sum1, 1)
            for d in range(DT):
                pool.wait_ge(ln_sq, DT * ln + d + 1)
                if d == 0:
                    nc.gpsimd.tensor_copy(zq[:, :], sq[0][:, :]).then_inc(ln_sumq, 1)
                else:
                    pool.wait_ge(ln_sumq, DT * ln + d)
                    nc.gpsimd.tensor_tensor(zq[:, :], zq[:, :], sq[d % 2][:, :], ALU.add).then_inc(ln_sumq, 1)
            if split is not None:
                pool_lo(pool, split)

        def pool_lo(pool, have, src=None):
            for d in range(DT):
                pool.wait_ge(xh_ready, have + d + 1)
                nc.gpsimd.tensor_tensor(xl[:, d, :], r[:, d, :], xh[:, d, :].bitcast(F32),
                                        ALU.subtract).then_inc(x_ready, 1)

        def dve_centre(dve, ln, d):
            if d == 0:
                dve.wait_ge(ln_centre, ln + 1)
            nc.vector.tensor_tensor(r[:, d, :], r[:, d, :], cb[:, :], ALU.subtract).then_inc(ln_centred, 1)
            dve.wait_ge(ln_centred, DT * ln + d + 1)
            if d == 0:
                nc.vector.tensor_copy(zc[:, :], r[:, 0, :]).then_inc(ln_sumc, 1)
            else:
                dve.wait_ge(ln_sumc, DT * ln + d)
                nc.vector.tensor_tensor(zc[:, :], zc[:, :], r[:, d, :], ALU.add).then_inc(ln_sumc, 1)

        def dve_ln(dve, ln):
            dve.wait_ge(ln_mean, ln + 1)
            link(dve, nc.vector.tensor_tensor(sq[0][:, :], cb[:, :], cb[:, :], ALU.mult))
            nc.vector.scalar_tensor_tensor(out=two(sq[0]), in0=misc[:, 2:4, 0:HALF], scalar=1.0 / D,
                                           in1=two(sq[0]), op0=ALU.mult, op1=ALU.subtract).then_inc(ln_var, 1)
            dve.wait_ge(ln_sd, ln + 1)
            link(dve, nc.vector.reciprocal(rstd[:, :], sq[1][:, :]))
            link(dve, nc.vector.tensor_tensor(cb[:, :], cb[:, :], rstd[:, :], ALU.mult))
            for d in range(DT):
                nc.vector.tensor_tensor(r[:, d, :], r[:, d, :], rstd[:, :], ALU.mult).then_inc(ln_scaled, 1)
                dve.wait_ge(ln_scaled, 2 * DT * ln + 2 * d + 1)
                nc.vector.tensor_tensor(r[:, d, :], r[:, d, :], cb[:, :], ALU.subtract).then_inc(ln_scaled, 1)

        def act_centre(act, ln):
            act.wait_ge(ln_centre_mm, ln + 1)
            nc.scalar.activation(two(cb), misc[:, 0:2, 0:HALF], ACT.Copy, scale=1.0 / (NCEN * P)).then_inc(ln_centre, 1)

        def act_square(act, ln, d):
            act.wait_ge(ln_centred, DT * ln + d + 1)
            if d >= 2:
                act.wait_ge(ln_sumq, DT * ln + d - 1)
            elif ln:
                act.wait_ge(ln_scaled, 2 * DT * ln)
            nc.scalar.activation(sq[d % 2][:, :], r[:, d, :], ACT.Square).then_inc(ln_sq, 1)

        def act_ln(act, ln, split):
            act.wait_ge(ln_mm, ln + 1)
            act.wait_ge(ln_centred, DT * (ln + 1))
            nc.scalar.activation(two(cb), misc[:, 0:2, 0:HALF], ACT.Copy, scale=1.0 / D).then_inc(ln_mean, 1)
            act.wait_ge(ln_var, ln + 1)
            nc.scalar.activation(sq[1][:, :], sq[0][:, :], ACT.Sqrt, bias=small[:, 0:1]).then_inc(ln_sd, 1)
            for d in range(DT):
                act.wait_ge(ln_scaled, 2 * DT * ln + 2 * d + 2)
                col = ln * DT + d
                nc.scalar.activation(r[:, d, :], r[:, d, :], ACT.Identity, scale=vec[:, col:col + 1],
                                     bias=vec[:, 48 + col:49 + col]).then_inc(ln_out, 1)
                if split is not None:
                    act.wait_ge(ln_out, DT * ln + d + 1)
                    nc.scalar.copy(xh[:, d, :], r[:, d, :]).then_inc(xh_ready, 1)

        def act_out(act, base, k, ln):
            def body(i):
                for odd in range(2):
                    ahead(act_hi, act, base, i, DT // 2, k, odd)
                if ln is not None and isinstance(i, int) and i == DT // 2 - 1:
                    act_centre(act, ln)
                    for d in range(DT):
                        act_square(act, ln, d)
            pairs(act, DT // 2, body)

        def dve_out(dve, base, k, alpha, ln):
            def body(i):
                for odd in range(2):
                    n, turn, s = tile(base, i, odd)
                    ahead(dve_lo, dve, base, i, DT // 2, k, odd)
                    dve.wait_ge(tile_done, n + 1)
                    rd = r[:, bass.ds(2 * i + odd, 1), :].rearrange("p a (h n) -> p (a h) n", h=2)
                    nc.vector.scalar_tensor_tensor(out=rd, in0=rd, scalar=alpha, in1=ps[:, s, :, 0:HALF],
                                                   op0=ALU.mult, op1=ALU.add).then_inc(drained[s], 1)
                    if ln is not None and isinstance(i, int) and i == DT // 2 - 1:
                        if odd == 0:
                            for d in range(NCEN):
                                dve_centre(dve, ln, d)
                        dve.wait_ge(drained[s], turn + 1)
                        dve_centre(dve, ln, NCEN + odd)
            pairs(dve, DT // 2, body)

        N_PART = 10
        TRIG_PAIR = 5
        MADE_BY_LOOP = range(2, DT)

        def beside(ffn, p, eng):
            if ffn:
                return [FH - 1]
            if p:
                return [i for i in range(FH) if i not in MADE_BY_LOOP]
            return {"dve": range(FH), "act": [0, TRIG_PAIR, FH - 1]}.get(eng, [0, FH - 1])

        def tables_of(ffn, p, i, lag):
            if ffn or not p or (isinstance(i, int) and not lag <= i < DT + lag):
                return None
            return i - lag

        def act_ffn(act, base, ffn, ln, split):
            for p in range(2):
                def body_in(i, b=base, p=p):
                    n, turn, s = tile(b, i, 0)
                    ahead(act_hi, act, b, i, FH, DT, 0)
                    act.wait_ge(tile_done, n + 1)
                    wait(act, drained[1], turn)
                    nc.scalar.activation(two(sil), ps[:, 0, :, 0:HALF], ACT.Silu).then_inc(drained[0], 1)
                    dt = tables_of(ffn, p, i, 1)
                    if dt is not None:
                        act_input_tables(act, dt)
                    if ffn == 0 and p == 0 and isinstance(i, int) and i == TRIG_PAIR:
                        act_trig(act)
                    ahead(act_hi, act, b, i, FH, DT, 1)
                    if dt is not None:
                        act_toeplitz(act, dt)
                    act.wait_ge(drained[1], turn + 1)
                    nc.scalar.copy(hh[:, bass.ds(i, 1), :], hf[:, :].unsqueeze(1)).then_inc(hh_ready, 1)
                    if dt is not None:
                        act_store_toeplitz(act, dt)
                peeled(act, FH, body_in, beside(ffn, p, "act"))
                base += 2 * FH

                act_out(act, base, FH, ln if p else None)
                base += DT
            act_ln(act, ln, split)

        def dve_ffn(dve, base, ffn, ln):
            for p in range(2):
                def body_in(i, b=base, p=p, done=(2 * ffn + p) * FH):
                    n, turn, s = tile(b, i, 0)
                    ahead(dve_lo, dve, b, i, FH, DT, 0)
                    if ffn == 0 and p == 0 and isinstance(i, int) and i < N_PART:
                        dve_params(dve, i)
                    dt = tables_of(ffn, p, i, 0)
                    if dt is not None:
                        dve_tables(dve, dt)
                    ahead(dve_lo, dve, b, i, FH, DT, 1)
                    dve.wait_ge(tile_done, n + 2)
                    dve.wait_ge(drained[0], turn + 1)
                    wait(dve, hl_ready, i + done)
                    nc.vector.scalar_tensor_tensor(out=two(hf), in0=two(sil), scalar=0.5,
                                                   in1=ps[:, 1, :, 0:HALF], op0=ALU.mult,
                                                   op1=ALU.mult).then_inc(drained[1], 1)
                peeled(dve, FH, body_in, beside(ffn, p, "dve"))
                base += 2 * FH

                dve_out(dve, base, FH, 1.0 if p else ALPHA, ln if p else None)
                base += DT
            dve_ln(dve, ln)

        def pool_ffn(pool, base, ffn, ln, split):
            for p in range(2):
                def body_in(i, p=p, done=(2 * ffn + p) * FH):
                    dt = tables_of(ffn, p, i, 0)
                    if dt is not None:
                        pool_tables(pool, dt)
                    pool.wait_ge(hh_ready, i + (done + 1))
                    nc.gpsimd.tensor_tensor(hl[:, bass.ds(i, 1), :], hf[:, :].unsqueeze(1),
                                            hh[:, bass.ds(i, 1), :].bitcast(F32),
                                            ALU.subtract).then_inc(hl_ready, 1)
                peeled(pool, FH, body_in, beside(ffn, p, "pool"))
            first = base + 2 * (2 * FH) + DT
            pool_ln(pool, ln, lambda d: (drained[d % 2], (first + d) // 2 + 1), split)

        def sp_setup(sp):
            for i in range(4):
                sp.dma_start(xtok[:, i, :], x_prompt[0, i * P:(i + 1) * P, :]).then_inc(s_x, 16)
            sp.dma_start(xtok[0:DEC, 4, :], x_sample[0]).then_inc(s_x, 16)
            loads = [
                (rows[0:48, 0, :], ln_g.rearrange("l s (d p) -> (l s d) p", p=P)),
                (rows[48:96, 0, :], ln_b.rearrange("l s (d p) -> (l s d) p", p=P)),
                (rows[96:104, 0, :], ssm_d.rearrange("a (d p) -> (a d) p", p=P)),
                (rows[104:105, 0, :], subln_g),
                (rows[0:32, 1, :], a_re[0].rearrange("(a b) p -> a (b p)", b=2)),
                (rows[32:64, 1, :], a_im[0].rearrange("(a b) p -> a (b p)", b=2)),
                (rows[96:128, 1, :], state_re[0, 0].rearrange("(a b) p -> a (b p)", b=2)),
                (rows2[0:32, :], state_im[0, 0].rearrange("(a b) p -> a (b p)", b=2)),
                (dtrow[:, :], log_dt[0].rearrange("(a b) -> a b", b=2)),
                (cosT[:, :], rope_cos), (sinT[:, :], rope_sin),
                (braw[:, 0], b_re[0].rearrange("(a b) p c -> (b p) a c", b=2)),
                (braw[:, 1], b_im[0].rearrange("(a b) p c -> (b p) a c", b=2)),
            ]
            for ri, c in enumerate((c_re, c_im)):
                cv = c[0].rearrange("(d g) c p -> (g c) d p", d=DT)
                for dup in range(2):
                    loads.append((craw[:, ri, :, dup, :], cv))
            sp.wait_ge(s_pad, 1)
            loads.append((lamv[:].rearrange("p a b -> p (a b)"),
                          attn_lam.rearrange("a b c -> a (b c)").broadcast_to([P, 4 * HD])))
            for dst, src in loads:
                sp.dma_start(dst, src).then_inc(s_small, 16)
            assert 16 * len(loads) == N_SMALL
        N_SMALL = 16 * 18

        def pool_setup(pool):
            nc.gpsimd.memset(ident[:, :], 0.0).then_inc(s_const, 1)
            pool.wait_ge(s_const, 1)
            nc.gpsimd.affine_select(out=ident[:, :], in_=ident[:, :], compare_op=ALU.not_equal, fill=1.0,
                                    base=0, pattern=[[-1, P]], channel_multiplier=1).then_inc(s_const, 1)
            pool_lo(pool, X_IN)

        def pe_setup(pe):
            pe.wait_ge(s_const, 2)
            pe.wait_ge(s_x, 80)
            for d in range(DT):
                if d >= 2:
                    pe.wait_ge(s_r, d - 1)
                for i, (t0, n) in enumerate(TT):
                    mm = nc.tensor.transpose(mflat[:, (d % 2) * 1024 + t0:(d % 2) * 1024 + t0 + n],
                                             xtok[0:n, i, d * P:(d + 1) * P], ident[0:n, 0:n])
                mm.then_inc(s_tp, 1)
            pe.wait_ge(s_small, N_SMALL)
            pe.wait_ge(s_r, DT)
            pe.wait_ge(s_tpc, 1)
            nc.tensor.transpose(mflat[:, 0:P], rows[:, 0, :], ident[:])
            nc.tensor.transpose(mflat[:, P:2 * P], rows[:, 1, :], ident[:])
            nc.tensor.transpose(mflat[:, 2 * P:2 * P + 32], rows2[0:32, :], ident[0:32, 0:32]).then_inc(s_tp, 1)
            for ri in range(2):
                for d in range(DT):
                    mm = nc.tensor.transpose(mflat[:, 1024 + d * P :1024 + (d + 1) * P],
                                             craw[:, ri, d].rearrange("p a b -> p (a b)"), ident[:])
                mm.then_inc(s_tp, 1)
                if ri == 0:
                    pe.wait_ge(s_cm, 2)

        s_cm = sem("c_copied")

        def act_setup(act):
            for d in range(DT):
                act.wait_ge(s_r, d + 1)
                nc.scalar.copy(xh[:, d, :], r[:, d, :]).then_inc(xh_ready, 1)

        def act_trig(act):
            act.wait_ge(s_ang, 1)
            nc.scalar.activation(tmp[:, 8, :], tmp[:, 6, :], ACT.Sin).then_inc(s_trig, 1)
            nc.scalar.activation(tmp[:, 9, :], tmp[:, 7, :], ACT.Sin).then_inc(s_trig, 1)

        s_ang = sem("angles_ready")
        s_trig = sem("trig_ready")
        s_exps = sem("exponent_int")
        s_params = sem("s5_params_ready")

        def v_exp(dve, out, x_, a, b, c, kint=kint[:, :]):
            V = nc.vector
            link(dve, V.tensor_scalar(c, x_, -87.0, 88.0, ALU.max, ALU.min))
            link(dve, V.tensor_scalar(a, c, 1.0 / math.log(2), ROUND, ALU.mult, ALU.add))
            link(dve, V.tensor_scalar(a, a, ROUND, None, ALU.subtract))
            link(dve, V.scalar_tensor_tensor(out=b, in0=a, scalar=-LN2_1, in1=c, op0=ALU.mult, op1=ALU.add))
            link(dve, V.scalar_tensor_tensor(out=b, in0=a, scalar=-LN2_2, in1=b, op0=ALU.mult, op1=ALU.add))
            link(dve, V.tensor_scalar(kint, a, 127.0, 2.0 ** 23, ALU.add, ALU.mult))
            co = [1.0 / math.factorial(i) for i in range(9)]
            link(dve, V.tensor_scalar(c, b, co[8], None, ALU.mult))
            for i in range(7, 0, -1):
                link(dve, V.scalar_tensor_tensor(out=c, in0=c, scalar=co[i], in1=b, op0=ALU.add, op1=ALU.mult))
            link(dve, V.scalar_tensor_tensor(out=out, in0=c, scalar=1.0, in1=kint.bitcast(F32), op0=ALU.add, op1=ALU.mult))

        def v_cmul(dve, orr, oi, ar, ai, br, bi, t0, t1):
            V = nc.vector
            link(dve, V.tensor_tensor(t0, ar, br, ALU.mult))
            link(dve, V.tensor_tensor(t1, ai, bi, ALU.mult))
            link(dve, V.tensor_tensor(orr, t0, t1, ALU.subtract))
            link(dve, V.tensor_tensor(t0, ar, bi, ALU.mult))
            link(dve, V.tensor_tensor(t1, ai, br, ALU.mult))
            link(dve, V.tensor_tensor(oi, t0, t1, ALU.add))

        def dve_setup(dve):
            V = nc.vector
            V.memset(ones[:, :], 1.0)
            V.memset(small[:, :], LN_EPS)
            V.memset(rows[96:128, 0, :], 0.0).then_inc(s_pad, 1)
            dve.wait_ge(s_pad, 1)
            for d in range(DT):
                dve.wait_ge(s_tp, d + 1)
                nc.vector.tensor_copy(r[:, d, :], mflat[:, (d % 2) * 1024:(d % 2) * 1024 + T]).then_inc(s_r, 1)
            dve.wait_ge(s_small, N_SMALL)
            V.tensor_copy(rows[64:96, 1, :].rearrange("a (b p) -> a b p", b=2),
                          dtrow[:, :].unsqueeze(2).broadcast_to([NPAIR, 2, PS])).then_inc(s_tpc, 1)
            dve.wait_ge(s_tp, DT + 1)
            link(dve, V.tensor_copy(vec[:, :], mflat[:, 0:P]))
            link(dve, V.tensor_copy(vs[:].rearrange("p a b -> p (a b)"), mflat[:, P:P + 160]))
            link(dve, V.tensor_scalar(small[:, 3:4], vec[:, 104:105], 1.0 - LAM_INIT, None, ALU.mult))
            for ri in range(2):
                dve.wait_ge(s_tp, DT + 2 + ri)
                src = mflat[:, 1024:2048].rearrange("p (a g c) -> p a g c", g=2, c=GC)
                for g in range(2):
                    V.tensor_copy(cmat[64 * g:64 * g + 64, ri], src[64 * g:64 * g + 64, :, g, :]).then_inc(s_cm, 1)
            dve.wait_ge(s_cm, 4)
            link(dve, V.tensor_scalar(cmat[:, 2], cmat[:, 1], -1.0, None, ALU.mult))
            link(dve, V.memset(maskrow[:, 0:CHUNK], 1.0))
            link(dve, V.memset(maskrow[:, CHUNK:P], 0.0))
            V.memset(maskrow[:, P:P + CHUNK], -1e30).then_inc(s_pad, 1)

        def dve_params(dve, part):
            V = nc.vector
            X = [tmp[:, i, :] for i in range(20)]
            lr, li = X[0], vs[:, 1, :]
            lbr, lbi = lp[:, 0, :, 1], lp[:, 1, :, 1]
            if part == 0:
                for k in range(2):
                    link(dve, V.tensor_tensor(lamv[:, 2 * k], lamv[:, 2 * k], lamv[:, 2 * k + 1], ALU.mult))
                    link(dve, V.reduce_sum(X[15][:, k:k + 1], lamv[:, 2 * k], axis=AX.X))
                v_exp(dve, X[16][:, 0:2], X[15][:, 0:2], X[17][:, 0:2], X[18][:, 0:2], X[19][:, 0:2], kint[:, 0:2])
                link(dve, V.tensor_tensor(small[:, 1:2], X[16][:, 1:2], X[16][:, 0:1], ALU.subtract))
                link(dve, V.tensor_scalar(small[:, 1:2], small[:, 1:2], -LAM_INIT, None, ALU.add))
            elif part == 1:
                link(dve, V.tensor_scalar(lr, vs[:, 0, :], -1e-4, None, ALU.min))
                v_exp(dve, X[1], vs[:, 2, :], X[10], X[11], X[12])
                link(dve, V.tensor_tensor(X[2], lr, X[1], ALU.mult))
            elif part == 2:
                v_exp(dve, X[3], X[2], X[10], X[11], X[12])
            elif part == 3:
                link(dve, V.tensor_tensor(X[4], li, X[1], ALU.mult))
                for out, shift in ((X[6], 0.0), (X[7], 0.25)):
                    link(dve, V.tensor_scalar(X[10], X[4], 1 / (2 * math.pi), shift, ALU.mult, ALU.add))
                    link(dve, V.tensor_scalar(X[10], X[10], ROUND, ROUND, ALU.add, ALU.subtract))
                    for c in (TWO_PI_1, TWO_PI_2, TWO_PI_3):
                        link(dve, V.scalar_tensor_tensor(out=X[11], in0=X[10], scalar=-c,
                                                         in1=X[4] if c == TWO_PI_1 else X[11],
                                                         op0=ALU.mult, op1=ALU.add))
                    link(dve, V.tensor_scalar(X[11], X[11], shift * 2 * math.pi, math.pi, ALU.add, ALU.min))
                    if shift:
                        V.tensor_scalar(out, X[11], -math.pi, None, ALU.max).then_inc(s_ang, 1)
                    else:
                        link(dve, V.tensor_scalar(out, X[11], -math.pi, None, ALU.max))
            elif part == 4:
                link(dve, V.memset(lp[:, 0, :, 0], 1.0))
                link(dve, V.memset(lp[:, 1, :, 0], 0.0))
            elif part == TRIG_PAIR + 1:
                dve.wait_ge(s_trig, 2)
                link(dve, V.tensor_tensor(lbi, X[3], X[8], ALU.mult))
                link(dve, V.tensor_tensor(lbr, X[3], X[9], ALU.mult))
                link(dve, V.tensor_scalar(X[5], lbr, -1.0, None, ALU.add))
                link(dve, V.tensor_tensor(X[10], lr, lr, ALU.mult))
                link(dve, V.tensor_tensor(X[11], li, li, ALU.mult))
                link(dve, V.tensor_tensor(X[10], X[10], X[11], ALU.add))
                link(dve, V.reciprocal(X[12], X[10]))
                link(dve, V.tensor_tensor(X[10], X[5], lr, ALU.mult))
                link(dve, V.tensor_tensor(X[11], lbi, li, ALU.mult))
                link(dve, V.tensor_tensor(X[10], X[10], X[11], ALU.add))
                link(dve, V.tensor_tensor(X[13], X[10], X[12], ALU.mult))
                link(dve, V.tensor_tensor(X[10], lbi, lr, ALU.mult))
                link(dve, V.tensor_tensor(X[11], X[5], li, ALU.mult))
                link(dve, V.tensor_tensor(X[10], X[10], X[11], ALU.subtract))
                link(dve, V.tensor_tensor(X[14], X[10], X[12], ALU.mult))
            elif part == TRIG_PAIR + 2:
                cr = X[13].unsqueeze(2).broadcast_to([P, NPAIR, GC])
                ci = X[14].unsqueeze(2).broadcast_to([P, NPAIR, GC])
                w0, w1 = (t[:, 0:512].rearrange("p (a c) -> p a c", c=GC) for t in prod)
                v_cmul(dve, bbar[:, 0], bbar[:, 1], cr, ci, braw[:, 0], braw[:, 1], w0, w1)
            elif part == TRIG_PAIR + 3:
                for k in (1, 2, 4):
                    w0, w1 = (t[:, 0:NPAIR * k].rearrange("p (a j) -> p a j", j=k) for t in prod)
                    b0, b1 = (lp[:, ri, :, k:k + 1].broadcast_to([P, NPAIR, k]) for ri in range(2))
                    v_cmul(dve, lp[:, 0, :, k + 1:2 * k + 1], lp[:, 1, :, k + 1:2 * k + 1],
                           lp[:, 0, :, 1:k + 1], lp[:, 1, :, 1:k + 1], b0, b1, w0, w1)
            elif part == TRIG_PAIR + 4:
                for j in range(BLK):
                    V.tensor_copy(lpr[:, :, :, j], lp[:, :, :, BLK - 1 - j])
                V.memset(ebuf[:].rearrange("p a b c d e -> p (a b c d e)"), 0.0)
                V.memset(cp[:].rearrange("p a b c d e -> p (a b c d e)"), 0.0)
                V.memset(tt[:].rearrange("p a b c -> p (a b c)"), 0.0).then_inc(s_params, 1)
                dve.wait_ge(s_params, 1)

        s_pad = sem("padded")

        s_e = sem("input_powers")
        s_c = sem("output_powers")
        s_tb = sem("tables_multiplied")
        s_tw = sem("tables_copied")
        s_tdw, s_tdc, s_tdt = (sem(f"table_{k}_stored") for k in "wct")
        s_pv = sem("products")
        s_pp = sem("pool_products")

        def later(dt):
            return not (isinstance(dt, int) and dt == 0)

        def dve_tables(dve, dt):
            V = nc.vector
            br, bi = (bbar[:, ri, bass.ds(4 * dt, 4), :].unsqueeze(2).broadcast_to([P, 4, BLK, GC]) for ri in range(2))
            lr, li = (lpr[:, ri, bass.ds(4 * dt, 4), :].unsqueeze(3).broadcast_to([P, 4, BLK, GC]) for ri in range(2))
            pr = [t[:, 0:4 * BLK * GC].rearrange("p (q j c) -> p q j c", q=4, c=GC) for t in prod]
            for ri, op in ((0, ALU.subtract), (1, ALU.add)):
                if ri:
                    dve.wait_ge(s_e, 4 * dt + 2)
                elif later(dt):
                    dve.wait_ge(s_e, 4 * dt)
                for k, (a, b) in enumerate(((br, lr), (bi, li)) if ri == 0 else ((br, li), (bi, lr))):
                    V.tensor_tensor(pr[k], a, b, ALU.mult).then_inc(s_pv, 1)
                dve.wait_ge(s_pv, 4 * dt + (2 + 2 * ri))
                if ri == 0 and later(dt):
                    dve.wait_ge(s_tb, 3 * dt)
                for g in range(2):
                    h = slice(64 * g, 64 * g + 64)
                    V.tensor_tensor(ebuf[h, ri, :, :, g, :], pr[0][h], pr[1][h], op).then_inc(s_e, 1)

        def pool_tables(pool, dt):
            G = nc.gpsimd
            cr, ci, nci = (cmat[:, k, bass.ds(4 * dt, 4), :].unsqueeze(2).broadcast_to([P, 4, BLK + 1, GC]) for k in range(3))
            lr, li = (lp[:, ri, bass.ds(4 * dt, 4), :].unsqueeze(3).broadcast_to([P, 4, BLK + 1, GC]) for ri in range(2))
            pr = [t[:, :].rearrange("p (q j c) -> p q j c", q=4, c=GC) for t in prodc]
            if later(dt):
                pool.wait_ge(s_c, 4 * dt)
            else:
                pool.wait_ge(s_params, 1)
            for k, (a, b) in enumerate(((cr, lr), (ci, li), (nci, lr), (cr, li))):
                G.tensor_tensor(pr[k], a, b, ALU.mult).then_inc(s_pp, 1)
            pool.wait_ge(s_pp, 4 * dt + 4)
            if later(dt):
                pool.wait_ge(s_tb, 3 * dt)
                pool.wait_ge(s_tdc, 16 * dt)
            for ri in range(2):
                for g in range(2):
                    h = slice(64 * g, 64 * g + 64)
                    G.tensor_tensor(cp[h, ri, :, :, g, :], pr[2 * ri][h], pr[2 * ri + 1][h],
                                    ALU.subtract).then_inc(s_c, 1)
                    pool.wait_ge(s_c, 4 * dt + (2 * ri + g + 1))

        def pe_tables(pe, dt):
            pe.wait_ge(s_e, 4 * dt + 4)
            if later(dt):
                pe.wait_ge(s_tw, 6 * dt)
            for ri in range(2):
                for q in range(4):
                    for jh in range(2):
                        k = ri * 1024 + (q * 2 + jh) * P
                        mm = nc.tensor.transpose(
                            mflat[:, k:k + P],
                            ebuf[:, ri, q, 4 * jh:4 * jh + 4].rearrange("p j g c -> p (j g c)"), ident[:])
                mm.then_inc(s_tb, 1)
            pe.wait_ge(s_c, 4 * dt + 4)
            pe.wait_ge(s_tw, 6 * dt + 1)
            for q in range(4):
                for ri in range(2):
                    mm = nc.tensor.matmul(mflat[0:32, q * 256:(q + 1) * 256],
                                          ebuf[:, ri, q, BLK - 1].rearrange("p g c -> p (g c)"),
                                          cp[:, ri, q, 0:BLK].rearrange("p j g c -> p (j g c)"),
                                          start=ri == 0, stop=ri == 1, skip_group_check=True)
            mm.then_inc(s_tb, 1)

        def table_row(scr, dt):
            return scr[bass.ds(dt, 1)].rearrange("a p n -> (a p) n")

        def act_input_tables(act, dt):
            act.wait_ge(s_c, 4 * dt + 4)
            act.dma_start(table_row(scr_c, dt).rearrange("p (a b n) -> p a b n", a=2, b=4),
                          cp[:, :, :, 1:BLK + 1].rearrange("p a q j g c -> p a q (j g c)")).then_inc(s_tdc, 16)
            if later(dt):
                act.wait_ge(s_tdw, 16 * dt)
            for ri in range(2):
                act.wait_ge(s_tb, 3 * dt + (ri + 1))
                nc.scalar.copy(wt[:, ri].rearrange("p q j s -> p (q j s)"),
                               mflat[:, ri * 1024:(ri + 1) * 1024]).then_inc(s_tw, 1)

        def act_toeplitz(act, dt):
            act.wait_ge(s_tw, 6 * dt + 2)
            act.dma_start(table_row(scr_w, dt), wt[:].rearrange("p a q j s -> p (a q j s)")).then_inc(s_tdw, 16)
            act.wait_ge(s_tb, 3 * dt + 3)
            if later(dt):
                act.wait_ge(s_tdt, 16 * dt)
            src = mflat[0:32, 0:1024].rearrange("p (q j c) -> p q j c", q=4, c=32)
            for jj in range(4):
                nc.scalar.copy(tt[32 * jj:32 * jj + 32, :, jj:BLK, :], src[:, :, 0:BLK - jj, :]).then_inc(s_tw, 1)

        def act_store_toeplitz(act, dt):
            act.wait_ge(s_tw, 6 * dt + 6)
            act.dma_start(table_row(scr_t, dt), tt[:].rearrange("p q j c -> p (q j c)")).then_inc(s_tdt, 16)

        s_u4 = sem("u4_ready")
        s_wl = [sem(f"wt2_loaded{s}") for s in range(2)]
        s_bl = [sem(f"cp2_tt2_loaded{s}") for s in range(2)]
        s_wm = sem("block_inputs_multiplied")
        s_wc = sem("block_inputs_copied")
        s_init = sem("states_initial")
        s_sa = sem("scan_products")
        s_sh = sem("scan_states")
        s_hp = sem("sample_scan")
        s_ym = sem("y_multiplied")
        s_yd = sem("y_copied_dve")
        s_ya = sem("y_copied_act")
        s_ys = sem("y_with_skip")
        s_ge = sem("gelu_done")
        s_st = sem("states_transposed")
        s_so = sem("states_copied")
        s_out = sem("stored")

        def sp_s5(sp):
            for s_ in (s_tdw, s_tdc, s_tdt):
                sp.wait_ge(s_, 16 * DT)
            for dt in range(DT):
                s = dt % 2
                if dt >= 2:
                    sp.wait_ge(s_wm, dt - 1)
                sp.dma_start(wt2[s][:].rearrange("p a q j s -> p (a q j s)"), scr_w[dt]).then_inc(s_wl[s], 16)
            for dt in range(DT):
                s = dt % 2
                if dt >= 2:
                    sp.wait_ge(s_ym, dt - 1)
                sp.dma_start(cp2[s][:].rearrange("p a q j g c -> p (a q j g c)"), scr_c[dt]).then_inc(s_bl[s], 16)
                sp.dma_start(tt2[s][:].rearrange("p q j c -> p (q j c)"), scr_t[dt]).then_inc(s_bl[s], 16)

        def u4_copy(eng_copy, jj, s):
            for q in range(4):
                src = r[32 * q:32 * q + 32, :, jj::4].rearrange("p d (n j) -> p d j n", j=2)
                eng_copy(u4[32 * jj:32 * jj + 32, :, q, :, :], src).then_inc(s_u4, 1)

        def dve_s5(dve):
            V = nc.vector
            dve.wait_ge(ln_out, DT)
            for jj in (0, 1):
                u4_copy(V.tensor_copy, jj, None)
            for dt in range(DT):
                dve.wait_ge(s_wm, dt + 1)
                b = dt % 2
                src = mflat[:, b * 1024:(b + 1) * 1024].rearrange("p (r n) -> p r n", r=2)[:, :, 0:4 * NB] \
                    .rearrange("p r (q n) -> p r q n", q=4)
                for ri in range(2):
                    V.tensor_copy(hs[:, ri, 4 * dt:4 * dt + 4, 1:NB], src[:, ri, :, 0:NB - 1]).then_inc(s_wc, 1)
                    V.tensor_copy(hlast[:, ri, 4 * dt:4 * dt + 4, :],
                                  src[:, ri, :, NBP - 1::DEC // BLK]).then_inc(s_wc, 1)
            dve.wait_ge(s_wc, 4 * DT)
            V.memset(hs[:, :, :, 0], 0.0).then_inc(s_init, 1)
            V.tensor_copy(hs[:, :, :, NBP], vs[:, 3:5, :]).then_inc(s_init, 1)
            for half in range(2):
                V.tensor_copy(lam8[:, 0, half, :], lp[:, 0, :, BLK]).then_inc(s_init, 1)
            V.tensor_scalar(lam8[:, 1, 0, :], lp[:, 1, :, BLK], -1.0, None, ALU.mult).then_inc(s_init, 1)
            V.tensor_copy(lam8[:, 1, 1, :], lp[:, 1, :, BLK]).then_inc(s_init, 1)
            dve.wait_ge(s_init, 6)
            for n in range(NBP):
                cur = hs[:, :, :, n]
                nxt = hs[:, :, :, n + 1] if n + 1 < NBP else hlast[:, :, :, 0]
                if n:
                    dve.wait_ge(s_sh, n)
                V.tensor_tensor(sa[:], cur, lam8[:, 0], ALU.mult).then_inc(s_sa, 1)
                V.tensor_tensor(sb2[:, 0], hs[:, 1, :, n], lam8[:, 1, 0], ALU.mult).then_inc(s_sa, 1)
                V.tensor_tensor(sb2[:, 1], hs[:, 0, :, n], lam8[:, 1, 1], ALU.mult).then_inc(s_sa, 1)
                dve.wait_ge(s_sa, 4 * n + 1)
                V.tensor_tensor(sa[:], sa[:], nxt, ALU.add).then_inc(s_sa, 1)
                dve.wait_ge(s_sa, 4 * n + 4)
                V.tensor_tensor(nxt, sa[:], sb2[:], ALU.add).then_inc(s_sh, 1)
            for dt in range(DT):
                b = dt % 2
                dve.wait_ge(s_ym, dt + 1)
                if dt:
                    dve.wait_ge(s_ge, dt)
                src = mflat[:, b * 1024:(b + 1) * 1024].rearrange("p (a n) -> p a n", a=2)[:, :, 0:4 * NB] \
                    .rearrange("p a (q j n) -> p a q j n", q=2, j=2)
                for jj in (0, 1):
                    for q in range(4):
                        dst = ysb[32 * q:32 * q + 32, jj::4].rearrange("p (n j) -> p j n", j=2)
                        V.tensor_copy(dst, src[32 * jj:32 * jj + 32, q // 2, q % 2]).then_inc(s_yd, 1)
                dve.wait_ge(s_yd, 8 * dt + 8)
                dve.wait_ge(s_ya, 8 * dt + 8)
                V.scalar_tensor_tensor(out=ysb[:, :], in0=r[:, dt, :], scalar=vec[:, 96 + dt:97 + dt],
                                       in1=ysb[:, :], op0=ALU.mult, op1=ALU.add).then_inc(s_ys, 1)

        def act_s5(act):
            act.wait_ge(ln_out, DT)
            for jj in (2, 3):
                u4_copy(nc.scalar.copy, jj, None)
            for dt in range(DT):
                b = dt % 2
                act.wait_ge(s_ym, dt + 1)
                if dt:
                    act.wait_ge(s_ge, dt)
                src = mflat[:, b * 1024:(b + 1) * 1024].rearrange("p (a n) -> p a n", a=2)[:, :, 0:4 * NB] \
                    .rearrange("p a (q j n) -> p a q j n", q=2, j=2)
                for jj in (2, 3):
                    for q in range(4):
                        dst = ysb[32 * q:32 * q + 32, jj::4].rearrange("p (n j) -> p j n", j=2)
                        nc.scalar.copy(dst, src[32 * jj:32 * jj + 32, q // 2, q % 2]).then_inc(s_ya, 1)
                act.wait_ge(s_ys, dt + 1)
                if dt:
                    act.wait_ge(x_ready, X_GELU + dt)
                nc.scalar.activation(gel[:, :], ysb[:, :], ACT.Gelu_apprx_tanh).then_inc(s_ge, 1)
                act.wait_ge(s_ge, dt + 1)
                nc.scalar.copy(xh[:, dt, :], gel[:, :]).then_inc(xh_ready, 1)
            act.wait_ge(s_st, 4)
            nc.scalar.copy(strow[:].rearrange("p a b -> p (a b)"), mflat[0:NPAIR, 0:512]).then_inc(s_so, 1)

        def pool_s5(pool):
            G = nc.gpsimd
            pool.wait_ge(s_init, 6)
            nb = DEC // BLK
            for n in range(nb):
                c = NBP + n
                cur = hs[:, :, :, c]
                nxt = hs[:, :, :, c + 1] if n + 1 < nb else hlast[:, :, :, 1]
                if n:
                    pool.wait_ge(s_hp, 5 * n)
                G.tensor_tensor(stin[:], cur, lam8[:, 0], ALU.mult).then_inc(s_hp, 1)
                G.tensor_tensor(stmp[:, 0], hs[:, 1, :, c], lam8[:, 1, 0], ALU.mult).then_inc(s_hp, 1)
                G.tensor_tensor(stmp[:, 1], hs[:, 0, :, c], lam8[:, 1, 1], ALU.mult).then_inc(s_hp, 1)
                pool.wait_ge(s_hp, 5 * n + 3)
                G.tensor_tensor(stin[:], stin[:], nxt, ALU.add).then_inc(s_hp, 1)
                pool.wait_ge(s_hp, 5 * n + 4)
                G.tensor_tensor(nxt, stin[:], stmp[:], ALU.add).then_inc(s_hp, 1)
            for d in range(DT):
                pool.wait_ge(xh_ready, X_GELU + d + 1)
                G.tensor_tensor(xl[:, d, :], gel[:, :], xh[:, d, :].bitcast(F32),
                                ALU.subtract).then_inc(x_ready, 1)

        stmp = am2("stmp", [P, 2, NPAIR])
        assert am2.at <= k_at, (am2.at - k_at)

        def pe_s5(pe):
            pe.wait_ge(s_u4, 16)
            for dt in range(DT):
                s = dt % 2
                pe.wait_ge(s_wl[s], 16 * (dt // 2 + 1))
                if dt >= 2:
                    pe.wait_ge(s_wc, 4 * (dt - 1))
                for ri in range(2):
                    for q in range(4):
                        o = misc[:, 2 * s + ri, q * NB:(q + 1) * NB]
                        for jh in range(2):
                            mm = nc.tensor.matmul(o, wt2[s][:, ri, q, jh, :], u4[:, dt, q, jh, :],
                                                  start=jh == 0, stop=jh == 1)
                mm.then_inc(s_wm, 1)
            pe.wait_ge(s_wc, 4 * DT)
            for dt in range(DT):
                s = dt % 2
                if dt == 0:
                    pe.wait_ge(s_sh, NBP)
                    pe.wait_ge(s_hp, 5 * (DEC // BLK))
                pe.wait_ge(s_bl[s], 32 * (dt // 2 + 1))
                if dt >= 2:
                    pe.wait_ge(s_yd, 8 * (dt - 1))
                    pe.wait_ge(s_ya, 8 * (dt - 1))
                for q in range(4):
                    for jh in range(2):
                        c0 = (q % 2) * 2 * NB + jh * NB
                        o = misc[:, 2 * s + q // 2, c0:c0 + NB]
                        t2 = tt2[s][:, q].rearrange("p j c -> p (j c)")
                        nc.tensor.matmul(o, t2[:, 0:P], u4[:, dt, q, jh, :], start=True, stop=False)
                        if jh:
                            nc.tensor.matmul(o, t2[:, P:2 * P], u4[:, dt, q, 0, :], start=False, stop=False)
                        for ri in range(2):
                            v = cp2[s][:, ri, q, 4 * jh:4 * jh + 4].rearrange("p j g c -> p (j g c)")
                            mm = nc.tensor.matmul(o, v, hs[:, ri, 4 * dt + q, :], start=False, stop=ri == 1)
                mm.then_inc(s_ym, 1)
            pe.wait_ge(s_yd, 8 * (DT - 1) + 0)
            pe.wait_ge(s_ya, 8 * (DT - 1))
            for k in range(4):
                nc.tensor.transpose(misc[0:NPAIR, 0, k * P:(k + 1) * P],
                                    hlast[:, k % 2, :, k // 2], ident[:]).then_inc(s_st, 1)
            pe.wait_ge(s_so, 1)

        def sp_states(sp):
            sp.wait_ge(s_so, 1)
            for k, dst in enumerate((p_re, p_im, s_re, s_im)):
                sp.dma_start(dst[0, 0].rearrange("(a b) p -> a (b p)", b=2), strow[:, k, :]).then_inc(s_out, 16)

        def act_glu(act, base, ln):
            def body(i):
                n, turn, s = tile(base, i, 0)
                ahead(act_hi, act, base, i, DT, DT, 0)
                act.wait_ge(tile_done, n + 1)
                wait(act, drained[1], turn)
                nc.scalar.activation(two(sil), ps[:, 0, :, 0:HALF], ACT.Sigmoid).then_inc(drained[0], 1)
                ahead(act_hi, act, base, i, DT, DT, 1)
                if isinstance(i, int) and i == DT - 1:
                    act_centre(act, ln)
                    for d in range(DT):
                        act_square(act, ln, d)
            pairs(act, DT, body)
            act_ln(act, ln, True)

        glu_z = sem("glu_z")

        def dve_glu(dve, base, ln):
            def body(i):
                n, turn, s = tile(base, i, 0)
                ahead(dve_lo, dve, base, i, DT, DT, 0)
                ahead(dve_lo, dve, base, i, DT, DT, 1)
                dve.wait_ge(tile_done, n + 2)
                dve.wait_ge(drained[0], turn + 1)
                wait(dve, glu_z, i)
                nc.vector.tensor_tensor(two(hf), two(sil), ps[:, 1, :, 0:HALF], ALU.mult).then_inc(drained[1], 1)
                dve.wait_ge(drained[1], turn + 1)
                rd = r[:, bass.ds(i, 1), :].rearrange("p a n -> p (a n)")
                nc.vector.scalar_tensor_tensor(out=rd, in0=rd, scalar=ALPHA, in1=hf[:, :], op0=ALU.mult,
                                               op1=ALU.add).then_inc(glu_z, 1)
                if isinstance(i, int) and i == DT - 1:
                    dve.wait_ge(glu_z, DT)
                    for d in range(DT):
                        dve_centre(dve, ln, d)
            pairs(dve, DT, body, peel_first=True)
            dve_ln(dve, ln)

        s_swap = sem("halves_swapped")
        s_rot = sem("sine_part")
        s_rope = sem("heads_rotated")
        s_vT = sem("v_copied")
        s_kvt = sem("kv_transposed")
        s_kc = sem("k_rows_copied")
        s_vc = sem("v_rows_copied")
        s_kout = sem("k_stored")

        def act_rope(act, base, done):
            def body(i):
                for odd in range(2):
                    n, turn, s = tile(base, i, odd)
                    ahead(act_hi, act, base, i, NH // 2, DT, odd)
                    act.wait_ge(tile_done, n + 1)
                    wait(act, s_rope, 2 * i + (done + odd))
                    for a, b in ((0, 32), (32, 0), (64, 96), (96, 64)):
                        nc.scalar.copy(two(sil)[a:a + 32], ps[b:b + 32, s, :, 0:HALF]).then_inc(s_swap, 1)
            pairs(act, NH // 2, body, peel_first=done == 0)

        def dve_rope(dve, base, done, dst):
            def body(i):
                for odd in range(2):
                    n, turn, s = tile(base, i, odd)
                    h = 2 * i + (done + odd)
                    ahead(dve_lo, dve, base, i, NH // 2, DT, odd)
                    dve.wait_ge(s_swap, 8 * i + (4 * (done + odd) + 4))
                    nc.vector.tensor_tensor(two(hf), ps[:, s, :, 0:HALF], two(cosT), ALU.mult).then_inc(drained[s], 1)
                    nc.vector.tensor_tensor(sil[:, :], sil[:, :], sinT[:, :], ALU.mult).then_inc(s_rot, 1)
                    dve.wait_ge(s_rot, h + 1)
                    nc.vector.tensor_tensor(dst[:, bass.ds(2 * i + odd, 1), :].rearrange("p a n -> p (a n)"),
                                            hf[:, :], sil[:, :], ALU.add).then_inc(s_rope, 1)
                    dve.wait_ge(s_rope, h + 1)
            pairs(dve, NH // 2, body)

        def act_v(act, base):
            def body(i):
                for odd in range(2):
                    n, turn, s = tile(base, i, odd)
                    ahead(act_hi, act, base, i, NH // 2, DT, odd)
                    act.wait_ge(tile_done, n + 1)
                    nc.scalar.copy(vT[:, bass.ds(2 * i + odd, 1), :].rearrange("p a (h n) -> p (a h) n", h=2),
                                   ps[:, s, :, 0:HALF]).then_inc(drained[s], 1)
            pairs(act, NH // 2, body)

        def dve_v(dve, base):
            def body(i):
                for odd in range(2):
                    ahead(dve_lo, dve, base, i, NH // 2, DT, odd)
            pairs(dve, NH // 2, body)

        def pe_kv_rows(pe):
            pe.wait_ge(s_rope, NH)
            for s in range(2):
                pe.wait_ge(drained[s], N_FFN10 // 2)
            for i, (t0, n) in enumerate(TT):
                if i:
                    pe.wait_ge(s_kc, i)
                for h in range(NH):
                    mm = nc.tensor.transpose(mflat[0:n, h * P:(h + 1) * P], kT[:, h, t0:t0 + n], ident[:])
                mm.then_inc(s_kvt, 1)
                if i:
                    pe.wait_ge(s_vc, i)
                for h in range(NH):
                    mm = nc.tensor.transpose(mflat[0:n, 1024 + h * P:1024 + (h + 1) * P], vT[:, h, t0:t0 + n], ident[:])
                mm.then_inc(s_kvt, 1)

        def act_kv_rows(act):
            for i, (t0, n) in enumerate(TT):
                act.wait_ge(s_kvt, 2 * i + 1)
                if i >= 2:
                    act.wait_ge(s_kout, 16 * (i - 1))
                nc.scalar.copy(ktok[i % 2][0:n, :], mflat[0:n, 0:1024]).then_inc(s_kc, 1)

        def dve_kv_rows(dve):
            nc.vector.memset(vtok[DEC:P, 4, :], 0.0)
            for i, (t0, n) in enumerate(TT):
                dve.wait_ge(s_kvt, 2 * i + 2)
                nc.vector.tensor_copy(vtok[0:n, i, :], mflat[0:n, 1024:2048]).then_inc(s_vc, 1)

        def sp_kv_rows(sp):
            for i, (t0, n) in enumerate(TT):
                kd = (p_k[0, t0:t0 + n] if i < 4 else s_k[0]).rearrange("t h m d -> t (h m d)")
                vd = (p_v[0, t0:t0 + n] if i < 4 else s_v[0]).rearrange("t h e -> t (h e)")
                sp.wait_ge(s_kc, i + 1)
                if i:
                    sp.wait_ge(s_kout, 16 * i)
                sp.dma_start(kd, ktok[i % 2][0:n, :]).then_inc(s_kout, 16)
                sp.wait_ge(s_vc, i + 1)
                sp.dma_start(vd, vtok[0:n, i, :]).then_inc(s_out, 16)

        s_qs = sem("queries_staged")
        s_sc = sem("scores")
        s_max = sem("maxima")
        s_exp = sem("exponentials")
        s_rat = sem("ratios")
        s_pr = sem("probabilities")
        s_pt = sem("p_transposed")
        s_ptc = sem("p_copied")
        s_o = sem("pv_done")
        s_oe = sem("o_copied")
        s_zq = sem("qs_cleared")
        v_mx = sem("v_stats")

        def prompt_items(eng, fn, pre=None, post=None):
            for i in range(4):
                def body(j, i=i):
                    for b in range(2):
                        fn(i, 2 * j + b, b, 2 * j + (8 * i + b))
                pairs(eng, NH // 2, body)

        def pool_attn(pool):
            G = nc.gpsimd
            pool.wait_ge(tile_done, N_O)
            for b in range(2):
                G.memset(qs[b][:].rearrange("p a b -> p (a b)"), 0.0).then_inc(s_zq, 1)
                pool.wait_ge(s_zq, 2 * b + 1)
                G.memset(pT[b][DEC:P, 512:512 + DEC], 0.0).then_inc(s_zq, 1)
                pool.wait_ge(s_zq, 2 * b + 2)
            pool.wait_ge(s_rope, 2 * NH)

            def stage(i, h, b, it):
                wait(pool, s_sc, it - 1)
                n = P if i < 4 else DEC
                for m in range(2):
                    G.tensor_copy(qs[b][64 * m:64 * m + 64, m, 0:n],
                                  qT[64 * m:64 * m + 64, bass.ds(h, 1), i * P:i * P + n].rearrange("p a n -> p (a n)")
                                  ).then_inc(s_qs, 1)
            first_items(pool, stage)
            sample_items(pool, lambda h, b, it: stage(4, h, b, it))

        def first_items(eng, fn):
            for i in range(4):
                def body(j, i=i):
                    for b in range(2):
                        fn(i, 2 * j + b, b, 2 * j + (8 * i + b))
                pairs(eng, NH // 2, body, peel_first=i == 0)

        def sample_items(eng, fn, peel=False):
            def body(j):
                for b in range(2):
                    fn(2 * j + b, b, 2 * j + (32 + b))
            pairs(eng, NH // 2, body, peel_first=peel)

        def head(t, h, cols):
            return t[:, bass.ds(h, 1), cols].rearrange("p a n -> p (a n)")

        def vhead(i, h, rows_=P):
            return vtok[0:rows_, i, bass.ds(h * P, P)]

        def pe_scores(i, h, b, it):
            pe = nc.tensor
            pe.wait_ge(s_qs, 2 * it + 2)
            wait(pe, s_exp, 2 * it - 2)
            kn = (i + 1) * P
            for m in range(2):
                nc.tensor.matmul(ps[:, b, m, 0:kn], qs[b][:, m, :], head(kT, h, slice(0, kn)), start=True, stop=False)
                mm = nc.tensor.matmul(ps[:, b, m, kn - CHUNK:kn], maskrow[0:1, 0:P], maskrow[0:1, P:P + CHUNK],
                                      start=False, stop=True)
            mm.then_inc(s_sc, 1)

        def pe_pv(i, h, b, it):
            pe = nc.tensor
            pe.wait_ge(s_pr, it + 1)
            wait(pe, s_ptc, it - 1)
            for kt in range(i + 1):
                mm = nc.tensor.transpose(misc[:, b, kt * P:(kt + 1) * P], ex[b][:, 0, kt * P:(kt + 1) * P], ident[:])
            mm.then_inc(s_pt, 1)
            pe.wait_ge(s_ptc, it + 1)
            wait(pe, s_oe, 2 * it - 2)
            for kt in range(i + 1):
                mm = nc.tensor.matmul(misc[:, 2 + b, 0:P], pT[b][:, kt * P:(kt + 1) * P], vhead(kt, h),
                                      start=kt == 0, stop=kt == i)
            mm.then_inc(s_o, 1)

        def pe_attn(pe):
            pe.wait_ge(drained[0], N_O // 2)
            pe.wait_ge(drained[1], N_O // 2)
            pe_scores(0, 0, 0, 0)
            for i in range(4):
                def body(j, i=i):
                    it = 2 * j + 8 * i
                    pe_scores(i, 2 * j + 1, 1, it + 1)
                    pe_pv(i, 2 * j, 0, it)
                    if not (isinstance(j, int) and j == NH // 2 - 1):
                        pe_scores(i, 2 * j + 2, 0, it + 2)
                    elif i < 3:
                        pe_scores(i + 1, 0, 0, it + 2)
                    pe_pv(i, 2 * j + 1, 1, it + 1)
                pairs(pe, NH // 2, body, peel_first=i == 0)
            pe.wait_ge(s_exp, 64)
            pe.wait_ge(s_oe, 64)

            def cached(h, b, it):
                pe.wait_ge(s_ck[b], (8 * (it - b) - 8 * 32) + 16)
                wait(pe, s_ktc, it - 32)
                for kt in range(PAST // P):
                    mm = nc.tensor.transpose(mflat[:, kt * P:(kt + 1) * P], ck[b][:, kt, :], ident[:])
                mm.then_inc(s_kt, 1)
            cached(0, 0, 32)

            def one(h, b, it):
                pe.wait_ge(s_qs, 2 * it + 2)
                pe.wait_ge(s_ktc, it - 31)
                wait(pe, s_exp, 4 * (it - 32) + 64)
                wait(pe, s_oe, 2 * it)
                for m in range(2):
                    for c in range(2):
                        nc.tensor.matmul(ps[0:DEC, m, c, :], qs[b][:, m, 0:DEC], kTc[b][:, c * 512:(c + 1) * 512],
                                         start=True, stop=True)
                    mm = nc.tensor.matmul(misc[0:DEC, 3, m * DEC:(m + 1) * DEC], qs[b][:, m, 0:DEC],
                                          head(kT, h, slice(SEQ, T)), start=True, stop=True, skip_group_check=True)
                mm.then_inc(s_sc, 1)
                if not (isinstance(h, int) and h == NH - 1):
                    cached(h + 1, 1 - b, it + 1)
                pe.wait_ge(s_pr, it + 1)
                wait(pe, s_ptc, 32 + 2 * (it - 32))
                for kt in range(PAST // P):
                    if kt == 0:
                        nc.tensor.matmul(misc[:, 2, 0:DEC], ex[b][0:DEC, 0, 0:P], ident[0:DEC, 0:DEC],
                                         start=True, stop=True)
                        continue
                    nc.tensor.transpose(misc[:, 2, kt * DEC:(kt + 1) * DEC], ex[b][0:DEC, 0, kt * P:(kt + 1) * P],
                                        ident[0:DEC, 0:DEC])
                nc.tensor.transpose(misc[0:DEC, 3, 2 * DEC:3 * DEC], ex[b][0:DEC, 0, PAST:PAST + DEC],
                                    ident[0:DEC, 0:DEC]).then_inc(s_pt, 1)
                pe.wait_ge(s_ptc, 32 + 2 * (it - 31))
                pe.wait_ge(s_cv[b], (8 * (it - b) - 8 * 32) + 16)
                for kt in range(PAST // P):
                    nc.tensor.matmul(misc[0:DEC, 3, 256:256 + P], pT[b][:, kt * DEC:(kt + 1) * DEC],
                                     cv[b][:, kt, :], start=kt == 0, stop=False, skip_group_check=True)
                nc.tensor.matmul(misc[0:DEC, 3, 256:256 + P], pT[b][:, 512:512 + DEC], vhead(4, h),
                                 start=False, stop=True, skip_group_check=True).then_inc(s_o, 1)
            sample_items(pe, one, peel=True)

            for h in range(NH):
                if h == 0:
                    pe.wait_ge(s_on, 5)
                if h >= 2:
                    pe.wait_ge(s_ox, h - 1)
                for i, (t0, n) in enumerate(TT):
                    mm = nc.tensor.transpose(mflat[:, (h % 2) * 1024 + t0:(h % 2) * 1024 + t0 + n],
                                             otok[0:n, i, h * P:(h + 1) * P], ident[0:n, 0:n])
                mm.then_inc(s_ot, 1)

        s_ck = [sem(f"cached_k_loaded{s}") for s in range(2)]
        s_cv = [sem(f"cached_v_loaded{s}") for s in range(2)]
        s_kt = sem("cached_k_transposed")
        s_ktc = sem("cached_k_copied")
        s_on = sem("heads_normalised")
        s_ns = sem("norm_roots")
        s_ox = sem("o_scaled")
        s_ot = sem("o_transposed")

        def dve_attn(dve):
            V = nc.vector

            def softmax(i, h, b, it):
                st = sts[:, b]
                kn = (i + 1) * P
                dve.wait_ge(s_sc, it + 1)
                V.reduce_max(st[:, 0:2], ps[:, b, :, 0:kn], axis=AX.X).then_inc(v_mx, 1)
                dve.wait_ge(v_mx, 3 * it + 1)
                V.tensor_scalar(st[:, 2:4], st[:, 0:2], -SCALE, None, ALU.mult).then_inc(s_max, 1)
                dve.wait_ge(s_exp, 2 * it + 2)
                V.reciprocal(st[:, 6:8], st[:, 4:6]).then_inc(v_mx, 1)
                dve.wait_ge(v_mx, 3 * it + 2)
                V.scalar_tensor_tensor(out=st[:, 8:9], in0=st[:, 4:5], scalar=small[:, 1:2], in1=st[:, 7:8],
                                       op0=ALU.mult, op1=ALU.mult).then_inc(v_mx, 1)
                dve.wait_ge(v_mx, 3 * it + 3)
                V.scalar_tensor_tensor(out=ex[b][:, 0, 0:kn], in0=ex[b][:, 1, 0:kn], scalar=st[:, 8:9],
                                       in1=ex[b][:, 0, 0:kn], op0=ALU.mult, op1=ALU.add).then_inc(s_pr, 1)
            prompt_items(dve, softmax)

            def one(h, b, it):
                st = sts[0:DEC, b]
                k = it - 32
                dve.wait_ge(s_ktf, k + 1)
                dve.wait_ge(s_sc, it + 1)
                V.reduce_max(st[:, 0:2], ps[0:DEC].rearrange("p m c n -> p m (c n)"), axis=AX.X).then_inc(v_mx, 1)
                V.reduce_max(st[:, 10:12], misc[0:DEC, 3, 0:2 * DEC].rearrange("p (m n) -> p m n", m=2),
                             axis=AX.X).then_inc(v_mx, 1)
                dve.wait_ge(v_mx, 6 * k + (96 + 2))
                V.tensor_tensor(st[:, 0:2], st[:, 0:2], st[:, 10:12], ALU.max).then_inc(v_mx, 1)
                dve.wait_ge(v_mx, 6 * k + (96 + 3))
                V.tensor_scalar(st[:, 2:4], st[:, 0:2], -SCALE, None, ALU.mult).then_inc(s_max, 1)
                dve.wait_ge(s_exp, 4 * k + (64 + 4))
                V.tensor_tensor(st[:, 4:6], st[:, 4:6], st[:, 12:14], ALU.add).then_inc(v_mx, 1)
                dve.wait_ge(v_mx, 6 * k + (96 + 4))
                V.reciprocal(st[:, 6:8], st[:, 4:6]).then_inc(v_mx, 1)
                dve.wait_ge(v_mx, 6 * k + (96 + 5))
                V.scalar_tensor_tensor(out=st[:, 8:9], in0=st[:, 4:5], scalar=small[0:DEC, 1:2], in1=st[:, 7:8],
                                       op0=ALU.mult, op1=ALU.mult).then_inc(v_mx, 1)
                dve.wait_ge(v_mx, 6 * k + (96 + 6))
                V.scalar_tensor_tensor(out=ex[b][0:DEC, 0, :], in0=ex[b][0:DEC, 1, :], scalar=st[:, 8:9],
                                       in1=ex[b][0:DEC, 0, :], op0=ALU.mult, op1=ALU.add).then_inc(s_pr, 1)
            sample_items(dve, one)

            dve.wait_ge(s_oe, 80)
            dve.wait_ge(s_ns, 2)
            link(dve, V.reciprocal(nrm[:, 1, 0:32], nrm[:, 0, 0:32]))
            link(dve, V.reciprocal(nrm[0:DEC, 1, 32:40], nrm[0:DEC, 0, 32:40]))
            for i, (t0, n) in enumerate(TT):
                o3 = otok[0:n, i].rearrange("p (h e) -> p h e", h=NH)
                V.tensor_tensor(o3, o3, nrm[0:n, 1, i * NH:(i + 1) * NH].unsqueeze(2).broadcast_to([n, NH, P]),
                                ALU.mult).then_inc(s_on, 1)

        s_ktf = sem("cached_k_ready")

        def act_attn(act):
            A = nc.scalar

            def evac(i, h, b, it, n):
                act.wait_ge(s_o, it + 1)
                A.activation(otok[0:n, i, bass.ds(h * P, P)], misc[0:n, 2 + b, 0:P] if n == P else misc[0:n, 3, 256:256 + P],
                             ACT.Copy, scale=sts[0:n, b, 6:7]).then_inc(s_oe, 1)
                A.activation(sq[b][0:n, 0:P], misc[0:n, 2 + b, 0:P] if n == P else misc[0:n, 3, 256:256 + P],
                             ACT.Square, scale=sts[0:n, b, 6:7],
                             accum_out=ssq[0:n, bass.ds(it, 1)]).then_inc(s_oe, 1)

            def exps(i, h, b, it):
                kn = (i + 1) * P
                act.wait_ge(s_max, it + 1)
                wait(act, s_pt, it - 1)
                for m in range(2):
                    A.activation(ex[b][:, m, 0:kn], ps[:, b, m, 0:kn], ACT.Exp, scale=SCALE,
                                 bias=sts[:, b, 2 + m:3 + m], accum_out=sts[:, b, 4 + m:5 + m]).then_inc(s_exp, 1)

            def pcopy(i, h, b, it):
                act.wait_ge(s_pt, it + 1)
                wait(act, s_o, it - 1)
                A.copy(pT[b][:, 0:(i + 1) * P], misc[:, b, 0:(i + 1) * P]).then_inc(s_ptc, 1)

            exps(0, 0, 0, 0)
            for i in range(4):
                def body(j, i=i):
                    it = 2 * j + 8 * i
                    exps(i, 2 * j + 1, 1, it + 1)
                    pcopy(i, 2 * j, 0, it)
                    evac(i, 2 * j, 0, it, P)
                    if not (isinstance(j, int) and j == NH // 2 - 1):
                        exps(i, 2 * j + 2, 0, it + 2)
                    elif i < 3:
                        exps(i + 1, 0, 0, it + 2)
                    pcopy(i, 2 * j + 1, 1, it + 1)
                    evac(i, 2 * j + 1, 1, it + 1, P)
                pairs(act, NH // 2, body, peel_first=i == 0)

            def kcopy(h, b, it):
                act.wait_ge(s_kt, it - 31)
                wait(act, s_sc, it - 1)
                A.copy(kTc[b][:, :], mflat[:, 0:PAST]).then_inc(s_ktc, 1)
                act.wait_ge(s_ktc, it - 31)
                A.copy(sq[0][:, 512:513], small[:, 0:1]).then_inc(s_ktf, 1)
            kcopy(0, 0, 32)

            def one(h, b, it):
                k = it - 32
                act.wait_ge(s_max, it + 1)
                wait(act, s_pt, it - 1)
                for m in range(2):
                    A.activation(ex[b][0:DEC, m, 0:PAST], ps[0:DEC, m].rearrange("p c n -> p (c n)"), ACT.Exp,
                                 scale=SCALE, bias=sts[0:DEC, b, 2 + m:3 + m],
                                 accum_out=sts[0:DEC, b, 4 + m:5 + m]).then_inc(s_exp, 1)
                    A.activation(ex[b][0:DEC, m, PAST:PAST + DEC], misc[0:DEC, 3, m * DEC:(m + 1) * DEC], ACT.Exp,
                                 scale=SCALE, bias=sts[0:DEC, b, 2 + m:3 + m],
                                 accum_out=sts[0:DEC, b, 12 + m:13 + m]).then_inc(s_exp, 1)
                if not (isinstance(h, int) and h == NH - 1):
                    kcopy(h + 1, 1 - b, it + 1)
                act.wait_ge(s_pt, it + 1)
                A.copy(pT[b][:, 0:512], misc[:, 2, :]).then_inc(s_ptc, 1)
                A.copy(pT[b][0:DEC, 512:512 + DEC], misc[0:DEC, 3, 2 * DEC:3 * DEC]).then_inc(s_ptc, 1)
                evac(4, h, b, it, DEC)
            sample_items(act, one)

            act.wait_ge(s_oe, 80)
            A.activation(nrm[:, 0, 0:32], ssq[:, 0:32], ACT.Sqrt, scale=1.0 / P, bias=small[:, 0:1]).then_inc(s_ns, 1)
            A.activation(nrm[0:DEC, 0, 32:40], ssq[0:DEC, 32:40], ACT.Sqrt, scale=1.0 / P,
                         bias=small[0:DEC, 0:1]).then_inc(s_ns, 1)
            for h in range(NH):
                buf = (sil, hf)[h % 2]
                act.wait_ge(s_ot, h + 1)
                if h >= 2:
                    act.wait_ge(x_ready, X_ATT + h - 1)
                A.activation(buf[:, :], mflat[:, (h % 2) * 1024:(h % 2) * 1024 + T], ACT.Copy,
                             scale=small[:, 3:4]).then_inc(s_ox, 1)
                act.wait_ge(s_ox, h + 1)
                A.copy(xh[:, h, :], buf[:, :]).then_inc(xh_ready, 1)

        def pool_attn_out(pool):
            for h in range(NH):
                pool.wait_ge(xh_ready, X_ATT + h + 1)
                nc.gpsimd.tensor_tensor(xl[:, h, :], (sil, hf)[h % 2][:, :], xh[:, h, :].bitcast(F32),
                                        ALU.subtract).then_inc(x_ready, 1)

        def sp_attn(sp):
            sp.wait_ge(tile_done, N_O - 1)
            for h in range(NH):
                b = h % 2
                if h == 0:
                    sp.wait_ge(tile_done, N_Q)
                if h >= 2:
                    sp.wait_ge(s_kt, h - 1)
                    sp.wait_ge(s_o, 32 + h - 1)
                sp.dma_start(ck[b][:], cache_k[0].rearrange("(a p) h m d -> p a h (m d)", p=P)[:, :, h]).then_inc(s_ck[b], 16)
                sp.dma_start(cv[b][:], cache_v[0].rearrange("(a p) h e -> p a h e", p=P)[:, :, h]).then_inc(s_cv[b], 16)

        s_yt = sem("y_transposed")
        s_yc = sem("y_rows_copied")
        s_yo = [sem(f"y_stored{s}") for s in range(2)]

        def pe_y(pe):
            pe.wait_ge(ln_out, 6 * DT)
            for i, (t0, n) in enumerate(TT):
                if i >= 2:
                    pe.wait_ge(s_yc, i - 1)
                for d in range(DT):
                    mm = nc.tensor.transpose(mflat[0:n, (i % 2) * 1024 + d * P:(i % 2) * 1024 + (d + 1) * P],
                                             r[:, d, t0:t0 + n], ident[:])
                mm.then_inc(s_yt, 1)

        def act_y(act):
            for i, (t0, n) in enumerate(TT):
                act.wait_ge(s_yt, i + 1)
                if i >= 2:
                    act.wait_ge(s_yo[i % 2], 16 * (i // 2))
                nc.scalar.copy(ytok[i % 2][0:n, :], mflat[0:n, (i % 2) * 1024:(i % 2) * 1024 + 1024]).then_inc(s_yc, 1)

        def sp_y(sp):
            for i, (t0, n) in enumerate(TT):
                sp.wait_ge(s_yc, i + 1)
                sp.dma_start(y_prompt[0, t0:t0 + n] if i < 4 else y_sample[0], ytok[i % 2][0:n, :]).then_inc(s_yo[i % 2], 16)
            sp.wait_ge(s_yo[0], 48)
            sp.wait_ge(s_yo[1], 32)

        def dump_r(sp, sems):
            for s_, v in sems:
                sp.wait_ge(s_, v)
            sp.dma_start(dump.rearrange("p (a b) -> p a b", a=DT), r[:]).then_inc(s_out, 16)

        block = ctx.enter_context(nc.Block())

        @block.sync
        def _(sp):
            sp_setup(sp)
            sp_ffn(sp, N_FFN00, 0, 0)
            n_out = 0
            if stop > 1:
                sp_stage(sp, N_GLU, DT, glu_v, lambda i: i * P + D, lambda i: i * P, DT, between=sp_s5)
                n_out += 4
            if stop > 2:
                sp_ffn(sp, N_FFN01, 0, 1, between=sp_states)
            elif stop > 1:
                sp_states(sp)
            if stop > 3:
                sp_plain(sp, N_KV, DT, kv_v)
                sp_ffn(sp, N_FFN10, 1, 0, between=sp_kv_rows)
                n_out += 5
            if stop > 4:
                sp_plain(sp, N_Q, DT // 2, q_v)
                sp_plain(sp, N_O, DT // 2, o_v, between=sp_attn)
            if stop > 5:
                sp_ffn(sp, N_FFN11, 1, 1)
                sp_y(sp)
            if dump is not None:
                dump_r(sp, [(ln_out, DT * stop)])
                n_out += 1
            if stop > 3:
                sp.wait_ge(s_kout, 80)
            for s_ in (s_tdw, s_tdc, s_tdt):
                sp.wait_ge(s_, 16 * DT)
            sp.wait_ge(s_out, 16 * n_out)

        @block.scalar
        def _(act):
            act_setup(act)
            act_hi(act, 0, 0, 0, DT)
            act_ffn(act, N_FFN00, 0, 0, None)
            if stop > 1:
                act_s5(act)
                act_glu(act, N_GLU, 1)
            if stop > 2:
                act_ffn(act, N_FFN01, 1, 2, True)
            if stop > 3:
                act_rope(act, N_KV, 0)
                act_v(act, N_KV + NH)
                act_kv_rows(act)
                act.wait_ge(s_kout, 80)
                act_ffn(act, N_FFN10, 2, 3, True)
            if stop > 4:
                act_rope(act, N_Q, NH)
                act_attn(act)
                act_out(act, N_O, DT, 4)
                act_ln(act, 4, True)
            if stop > 5:
                act_ffn(act, N_FFN11, 3, 5, None)
                act_y(act)

        @block.vector
        def _(dve):
            dve_setup(dve)
            dve_lo(dve, 0, 0, 0, DT)
            dve_ffn(dve, N_FFN00, 0, 0)
            if stop > 1:
                dve_s5(dve)
                dve_glu(dve, N_GLU, 1)
            if stop > 2:
                dve_ffn(dve, N_FFN01, 1, 2)
            if stop > 3:
                dve_rope(dve, N_KV, 0, kT)
                dve_v(dve, N_KV + NH)
                dve_kv_rows(dve)
                dve_ffn(dve, N_FFN10, 2, 3)
            if stop > 4:
                dve_rope(dve, N_Q, NH, qT)
                dve_attn(dve)
                dve_out(dve, N_O, DT, ALPHA, 4)
                dve_ln(dve, 4)
            if stop > 5:
                dve_ffn(dve, N_FFN11, 3, 5)

        @block.gpsimd
        def _(pool):
            pool_setup(pool)
            pool_ffn(pool, N_FFN00, 0, 0, None)
            if stop > 1:
                pool_s5(pool)
                pool_ln(pool, 1, lambda d: (glu_z, d + 1), X_LN1)
            if stop > 2:
                pool_ffn(pool, N_FFN01, 1, 2, X_LN2)
            if stop > 3:
                pool_ffn(pool, N_FFN10, 2, 3, X_LN3)
            if stop > 4:
                pool_attn(pool)
                pool_attn_out(pool)
                pool_ln(pool, 4, lambda d: (drained[d % 2], (N_O + d) // 2 + 1), X_LN4)
            if stop > 5:
                pool_ffn(pool, N_FFN11, 3, 5, None)

        @block.tensor
        def _(pe):
            pe_setup(pe)
            pe_ffn(pe, N_FFN00, 0, X_IN, 0)
            if stop > 1:
                pe_s5(pe)
                pe_stage(pe, N_GLU, DT, DT, xh, xl, x_ready, X_GELU, hooks={1: lambda e: (pe_centre(e, 1), pe_stats(e, 1))})
            if stop > 2:
                pe_ffn(pe, N_FFN01, 1, X_LN1, 2)
            if stop > 3:
                pe_stage(pe, N_KV, DT, DT, xh, xl, x_ready, X_LN2)
                pe_kv_rows(pe)
                pe_ffn(pe, N_FFN10, 2, X_LN2, 3)
            if stop > 4:
                pe_stage(pe, N_Q, DT // 2, DT, xh, xl, x_ready, X_LN3)
                pe_attn(pe)
                pe_stage(pe, N_O, DT // 2, DT, xh, xl, x_ready, X_ATT,
                         hooks={0: lambda e: pe_centre(e, 4), 1: lambda e: pe_stats(e, 4)})
            if stop > 5:
                pe_ffn(pe, N_FFN11, 3, X_LN4, 5)
                pe_y(pe)


def rope_tables():
    half = HD // 2
    inv = (10000.0 ** (-np.arange(half) / half)).astype(np.float32)
    pos = np.concatenate([np.arange(SEQ), PAST + np.arange(DEC)]).astype(np.float32)
    ang = (inv[:, None] * pos[None, :]).astype(np.float32)
    c, s = np.cos(ang).astype(np.float32), np.sin(ang).astype(np.float32)
    return {"rope_cos": np.concatenate([c, c, c, c]), "rope_sin": np.concatenate([-s, s, -s, s])}


_INS = ["x_prompt", "x_sample", "cache_k", "cache_v", "state_ssm_re", "state_ssm_im", "ln_g", "ln_b",
        "ffn_w_in", "ffn_w_out", "ssm_a_re", "ssm_a_im", "ssm_log_dt", "ssm_b_re", "ssm_b_im",
        "ssm_c_re", "ssm_c_im", "ssm_d", "ssm_w_glu", "attn_w_q", "attn_w_kv", "attn_lam",
        "attn_subln_g", "attn_w_o"]
_OUTS = [(1, SEQ, D), (1, DEC, D), (1, 1, GROUPS, PS), (1, 1, GROUPS, PS), (1, SEQ, NH, 2, HD),
         (1, SEQ, NH, 2 * HD), (1, 1, GROUPS, PS), (1, 1, GROUPS, PS), (1, DEC, NH, 2, HD),
         (1, DEC, NH, 2 * HD)]


def kernel(**inputs):
    import numpy as _np
    import concourse.bacc as _bacc
    from concourse import mybir as _mybir
    from concourse.bass_utils import run_bass_kernel_spmd as _run

    nc = _bacc.Bacc("TRN2", target_bir_lowering=False, num_devices=1)
    arrays, args = {}, []
    consts = rope_tables()
    for name in _INS + list(consts):
        a = _np.ascontiguousarray(inputs[name] if name in inputs else consts[name])
        arrays[f"in_{name}_dram"] = a
        args.append(nc.dram_tensor(f"in_{name}_dram", a.shape, _mybir.dt.from_np(a.dtype), kind="ExternalInput").ap())
    for i, shape in enumerate(_OUTS):
        args.append(nc.dram_tensor(f"out_{i}_dram", shape, F32, kind="ExternalOutput").ap())
    build(nc, *args)
    r = _run(nc, [arrays], core_ids=[0])
    return tuple(r.results[0][f"out_{i}_dram"] for i in range(len(_OUTS)))
```

```python
import math
from contextlib import ExitStack

import numpy as np

import concourse.bass as bass
from concourse import mybir

F32 = mybir.dt.float32
F32R = mybir.dt.float32r
I32 = mybir.dt.int32
ALU = mybir.AluOpType
ACT = mybir.ActivationFunctionType
AX = mybir.AxisListType

P = 128
D = 1024
DT = D // P
SEQ, DEC, PAST = 512, 64, 1024
T = SEQ + DEC
HALF = T // 2
DEPTH = 2
FF = ((8 * D // 3 + 127) // 128) * 128
FT = FF // P
FH = FT // 2
CHUNK = 64
HD, NH = 64, 8
GROUPS, GC, PS = 64, 16, 64
NPAIR = GROUPS // 2
BLK = 8
NB = T // BLK
NBP = SEQ // BLK
ALPHA = (2 * DEPTH) ** 0.25
LN_EPS = RMS_EPS = 1e-5
SCALE = HD ** -0.5
TT = [(i * P, min(P, T - i * P)) for i in range(5)]
NCEN = 6

FFN_TILES = 2 * (2 * FH + DT)
N_FFN00 = 0
N_GLU = N_FFN00 + FFN_TILES
N_FFN01 = N_GLU + 2 * DT
N_KV = N_FFN01 + FFN_TILES
N_FFN10 = N_KV + 2 * DT
N_Q = N_FFN10 + FFN_TILES
N_O = N_Q + DT
N_FFN11 = N_O + DT
N_TILES = N_FFN11 + FFN_TILES

X_IN, X_GELU, X_LN1, X_LN2, X_LN3, X_ATT, X_LN4 = (8 * i for i in range(7))
TWO_PI_1 = 6.28125
TWO_PI_2 = float(np.float32(2 * math.pi - TWO_PI_1))
TWO_PI_3 = float(2 * math.pi - TWO_PI_1 - TWO_PI_2)
LN2_1 = 0.693359375
LN2_2 = math.log(2) - LN2_1
ROUND = 1.5 * 2.0 ** 23
LAM_INIT = 0.8 - 0.6 * math.exp(-0.3 * 1)


def unit_rows(n):
    for base in (N_FFN00, N_FFN01, N_FFN10, N_FFN11):
        if base <= n < base + FFN_TILES:
            return DT if (n - base) % (2 * FH + DT) < 2 * FH else FH
    return DT


def pairs(eng, count, body, peel_first=False):
    first = 0
    if peel_first:
        body(0)
        first = 1
    if count - 1 - first > 1:
        with eng.Fori(first, count - 1) as i:
            body(i)
    else:
        for i in range(first, count - 1):
            body(i)
    body(count - 1)


def peeled(eng, count, body, peel):
    at = 0
    for stop_ in sorted(peel) + [count]:
        if stop_ - at == 1:
            body(at)
        elif stop_ > at:
            with eng.Fori(at, stop_) as i:
                body(i)
        if stop_ < count:
            body(stop_)
        at = stop_ + 1


def wait(eng, sem, value):
    if isinstance(value, int) and value <= 0:
        return
    eng.wait_ge(sem, value)


def build(nc, x_prompt, x_sample, cache_k, cache_v, state_re, state_im, ln_g, ln_b, w_in, w_out,
          a_re, a_im, log_dt, b_re, b_im, c_re, c_im, ssm_d, w_glu, w_q, w_kv, attn_lam, subln_g,
          w_o, rope_cos, rope_sin,
          y_prompt, y_sample, p_re, p_im, p_k, p_v, s_re, s_im, s_k, s_v, stop=99, dump=None):
    ctx = ExitStack()
    with ctx:
        n_tiles = {1: N_GLU, 2: N_FFN01, 3: N_KV, 4: N_Q, 5: N_FFN11}.get(stop, N_TILES)

        def sem(name):
            return ctx.enter_context(nc.semaphore(name))

        start = (nc.sbuf_base + 31) // 32 * 32
        room = nc.sbuf_usable_end - start - 64
        ctx.enter_context(nc.sbuf_tensor("slab", [P, room], mybir.dt.uint8))

        class Map:

            def __init__(self, at):
                self.at = at

            def __call__(self, name, shape, dt=F32):
                size = 4 * int(np.prod(shape[1:]))
                t = nc.alloc_sbuf_tensor_at(name, shape, dt, offset=self.at)
                self.at += (size + 31) // 32 * 32
                assert self.at <= start + room, (name, self.at - start, room)
                return t

        keep = Map(start)
        r = keep("r", [P, DT, T])
        x_at = keep.at
        xh = keep("xh", [P, DT, T], F32R)
        xl = keep("xl", [P, DT, T], F32R)
        raw = [keep(f"raw{s}", [P, FH, P]) for s in range(2)]
        wh = [keep(f"wh{s}", [P, FH, P], F32R) for s in range(2)]
        wl = [keep(f"wl{s}", [P, FH, P], F32R) for s in range(2)]
        ones = keep("ones", [P, P])
        maskrow = keep("maskrow", [1, P + CHUNK])
        ident = keep("ident", [P, P])
        vec = keep("vec", [P, P])
        small = keep("small", [P, 16])
        cosT = keep("cosT", [P, T])
        sinT = keep("sinT", [P, T])
        cb = keep("cb", [P, T])
        zc = keep("zc", [P, T])
        zq = keep("zq", [P, T])
        sq = [keep(f"sq{s}", [P, T]) for s in range(2)]
        rstd = keep("rstd", [P, T])
        sil = keep("sil", [P, T])
        hf = keep("hf", [P, T])
        h_at = keep.at
        fm = Map(h_at)
        hh = fm("hh", [P, FH, T], F32R)
        hl = fm("hl", [P, FH, T], F32R)
        k_at = fm.at
        km = Map(k_at)
        kT = km("kT", [P, NH, T])
        vtok = km("vtok", [P, 5, D])

        im = Map(h_at)
        xtok = im("xtok", [P, 5, D])
        rows = im("rows", [P, 2, P])
        rows2 = im("rows2", [P, P])
        dtrow = im("dtrow", [NPAIR, 2])
        gm = Map(k_at)
        vs = gm("vs", [P, 5, NPAIR])
        lp = gm("lp", [P, 2, NPAIR, BLK + 1])
        s5_at = gm.at
        lpr = gm("lpr", [P, 2, NPAIR, BLK])
        bbar = gm("bbar", [P, 2, NPAIR, GC])
        cmat = gm("cmat", [P, 3, NPAIR, GC])
        pm = Map(gm.at)
        ebuf = gm("ebuf", [P, 2, 4, BLK, 2, GC])
        cp = gm("cp", [P, 2, 4, BLK + 1, 2, GC])
        wt = gm("wt", [P, 2, 4, 2, P])
        tt = gm("tt", [P, 4, BLK, 32])
        tmp = pm("tmp", [P, 20, NPAIR])
        kint = pm("kint", [P, NPAIR], I32)
        braw = pm("braw", [P, 2, NPAIR, GC])
        craw = pm("craw", [P, 2, DT, 2, PS])
        lamv = pm("lamv", [P, 4, HD])
        prod = [cb, zc]
        prodc = [zq, sq[0], sq[1], rstd]

        am = Map(h_at)
        u4 = am("u4", [P, DT, 4, 2, NB])
        hs = am("hs", [P, 2, NPAIR, NB])
        hlast = am("hlast", [P, 2, NPAIR, 2])
        sm = Map(s5_at)
        wt2 = [sm(f"wt2_{s}", [P, 2, 4, 2, P]) for s in range(2)]
        cp2 = [sm(f"cp2_{s}", [P, 2, 4, BLK, 2, GC]) for s in range(2)]
        tt2 = [sm(f"tt2_{s}", [P, 4, BLK, 32]) for s in range(2)]
        am2 = am
        ysb = am2("ysb", [P, T])
        gel = am2("gel", [P, T])
        sa = am2("sa", [P, 2, NPAIR])
        sb2 = am2("sb2", [P, 2, NPAIR])
        lam8 = am2("lam8", [P, 2, 2, NPAIR])
        stin = am2("stin", [P, 2, NPAIR])
        strow = am2("strow", [NPAIR, 4, P])

        vm = Map(h_at)
        vT = vm("vT", [P, NH, T])
        ktok = [vm(f"ktok{s}", [P, D]) for s in range(2)]
        ytok = [vm(f"ytok{s}", [P, D]) for s in range(2)]

        qm = Map(h_at)
        qT = qm("qT", [P, NH, T])
        otok = qm("otok", [P, 5, D])
        ck = [qm(f"ck{s}", [P, PAST // P, P]) for s in range(2)]
        sts = qm("sts", [P, 2, 16])
        ssq = qm("ssq", [P, 5 * NH])
        nrm = qm("nrm", [P, 2, 5 * NH])
        stz = qm("stz", [P, 2, 8])
        ov = [qm(f"ov{s}", [DEC, P]) for s in range(2)]
        assert qm.at <= k_at
        cm = Map(km.at)
        cv = [cm(f"cv{s}", [P, PAST // P, P]) for s in range(2)]
        xm2 = Map(x_at)
        ex = [xm2(f"ex{s}", [P, 2, SEQ]) for s in range(2)]
        pT = [xm2(f"pT{s}", [P, SEQ]) for s in range(2)]
        qs = [xm2(f"qs{s}", [P, 2, P]) for s in range(2)]
        exS = [xm2(f"exS{s}", [P, PAST + DEC]) for s in range(2)]
        kTc = [xm2(f"kTc{s}", [P, PAST]) for s in range(2)]
        qd = [xm2(f"qd{s}", [P, P]) for s in range(2)]
        sqb = xm2("sqb", [P, D])
        assert xm2.at <= x_at + 2 * 4 * DT * T
        xm3 = Map(x_at)
        pTS = [xm3(f"pTS{s}", [P, (PAST // P + 1) * P]) for s in range(2)]

        ps = ctx.enter_context(nc.psum_tensor("tile_ps", [P, 2, 2, 512], F32))
        misc = ctx.enter_context(nc.psum_tensor("misc", [P, 4, 512], F32))
        mflat = misc[:].rearrange("p b n -> p (b n)")

        scr_w = nc.dram_tensor("scr_w", [DT, P, 2 * 4 * 2 * P], F32).ap()
        scr_c = nc.dram_tensor("scr_c", [DT, P, 2 * 4 * BLK * 32], F32).ap()
        scr_t = nc.dram_tensor("scr_t", [DT, P, 4 * BLK * 32], F32).ap()

        w_loaded = [sem(f"w_loaded{s}") for s in range(2)]
        w_hi = sem("w_hi")
        w_lo = sem("w_lo")
        tile_done = sem("tile_done")
        drained = [sem(f"drained{s}") for s in range(2)]
        hh_ready = sem("hh_ready")
        hl_ready = sem("hl_ready")
        xh_ready = sem("xh_ready")
        x_ready = sem("x_ready")
        ln_sum1 = sem("ln_sum1")
        ln_centre_mm = sem("ln_centre_mm")
        ln_centre = sem("ln_centre")
        ln_centred = sem("ln_centred")
        ln_sq = sem("ln_sq")
        ln_sumc = sem("ln_sumc")
        ln_sumq = sem("ln_sumq")
        ln_mm = sem("ln_mm")
        ln_mean = sem("ln_mean")
        ln_var = sem("ln_var")
        ln_sd = sem("ln_sd")
        ln_scaled = sem("ln_scaled")
        ln_out = sem("ln_out")
        step = sem("step")
        s_x = sem("x_loaded")
        s_small = sem("small_loaded")
        s_const = sem("const_ready")
        s_tp = sem("setup_transposed")
        s_tpc = sem("setup_copied")
        s_r = sem("r_loaded")

        w_in_v = w_in.rearrange("l s (k p) c -> l s p k c", p=P)
        w_out_v = w_out.rearrange("l s (k p) c -> l s p k c", p=P)
        glu_v = w_glu.rearrange("a (k p) c -> (a p) k c", p=P)
        kv_v = w_kv.rearrange("(k p) c -> p k c", p=P)
        q_v = w_q.rearrange("a (k p) c -> (a p) k c", p=P)
        o_v = w_o.rearrange("a (k p) c -> (a p) k c", p=P)

        steps = [0]

        def link(eng, ins):
            steps[0] += 1
            ins.then_inc(step, 1)
            eng.wait_ge(step, steps[0])

        def tile(base, i, odd):
            return 2 * i + (base + odd), i + base // 2, odd

        def sp_stage(sp, base, count, view, a, b, k, between=None):
            def body(i):
                n = tile(base, i, 0)[0]
                wait(sp, w_lo, n)
                for s, col in enumerate((a, b)):
                    sp.dma_start(raw[s][:, 0:k, :], view[:, :, bass.ds(col(i), P)]).then_inc(w_loaded[s], 16)
                if between is not None and isinstance(i, int) and i == 0:
                    between(sp)
            pairs(sp, count, body, peel_first=base == 0 or between is not None)

        def sp_ffn(sp, base, l, s, between=None):
            for p in range(2):
                f0 = p * FH
                sp_stage(sp, base, FH,
                         w_in_v[l, s], lambda i: (i + f0) * P, lambda i: (i + (f0 + FT)) * P, DT,
                         between=None if p else between)
                base += 2 * FH
                sp_stage(sp, base, DT // 2,
                         w_out_v[l, s][:, f0:f0 + FH], lambda i: i * 2 * P, lambda i: i * 2 * P + P, FH)
                base += DT

        def sp_plain(sp, base, count, view, between=None):
            sp_stage(sp, base, count, view, lambda i: i * 2 * P, lambda i: i * 2 * P + P, DT, between=between)

        def act_hi(act, n, turn, s, k):
            act.wait_ge(w_loaded[s], 16 * turn + 16)
            wait(act, tile_done, n - 1)
            nc.scalar.copy(wh[s][:, 0:k, :], raw[s][:, 0:k, :]).then_inc(w_hi, 1)

        def dve_lo(dve, n, turn, s, k):
            wait(dve, w_hi, n + 1)
            nc.vector.tensor_tensor(wl[s][:, 0:k, :], raw[s][:, 0:k, :],
                                    wh[s][:, 0:k, :].bitcast(F32), ALU.subtract).then_inc(w_lo, 1)

        def ahead(split, eng, base, i, count, k, which):
            n, turn, s = tile(base, i, which + 1) if which == 0 else tile(base + 2, i, 0)
            if which == 1 and isinstance(i, int) and i == count - 1:
                if base + 2 * count >= n_tiles:
                    return
                k = unit_rows(base + 2 * count)
            split(eng, n, turn, s, k)

        def pe_tile(pe, n, turn, s, k, hi, lo, ready, have):
            wait(pe, w_lo, n + 1)
            if not (isinstance(turn, int) and turn == 0):
                pe.wait_ge(drained[s], turn)
            for kk in range(k):
                if ready is not None:
                    pe.wait_ge(ready, have + kk + 1)
                for hf_ in range(2):
                    cols = slice(hf_ * HALF, (hf_ + 1) * HALF)
                    o = ps[:, s, hf_, 0:HALF]
                    nc.tensor.matmul(o, wh[s][:, kk, :], hi[:, kk, cols], start=kk == 0, stop=False)
                    nc.tensor.matmul(o, wh[s][:, kk, :], lo[:, kk, cols], start=False, stop=False)
                    last = nc.tensor.matmul(o, wl[s][:, kk, :], hi[:, kk, cols], start=False,
                                            stop=kk == k - 1)
            last.then_inc(tile_done, 1)

        def pe_stage(pe, base, count, k, hi, lo, ready, have, hooks={}, tables=False):
            def body(i):
                for odd in range(2):
                    if odd:
                        dt = tables_of(0, tables, i, 1)
                        if dt is not None:
                            pe_tables(pe, dt)
                    pe_tile(pe, *tile(base, i, odd), k, hi, lo, ready, have)
                    if isinstance(i, int) and i == count - 1 and odd in hooks:
                        hooks[odd](pe)
            peeled(pe, count, body, beside(0, 1, "pe") if tables else [0, count - 1] if base == 0 else [count - 1])

        def pe_ffn(pe, base, ffn, have, ln):
            for p in range(2):
                pe_stage(pe, base, FH, DT, xh, xl, x_ready, have, tables=ffn == 0 and p == 1)
                base += 2 * FH
                pe_stage(pe, base, DT // 2, FH, hh, hl, hl_ready, (2 * ffn + p) * FH,
                         hooks={0: lambda e: pe_centre(e, ln), 1: lambda e: pe_stats(e, ln)} if p else {})
                base += DT

        halves = [slice(0, HALF), slice(HALF, T)]

        def pe_centre(pe, ln):
            pe.wait_ge(ln_sum1, NCEN * (ln + 1))
            for q in range(2):
                mm = nc.tensor.matmul(misc[:, q, 0:HALF], ones[:], zc[:, halves[q]], start=True, stop=True)
            mm.then_inc(ln_centre_mm, 1)

        def pe_stats(pe, ln):
            pe.wait_ge(ln_sumc, DT * (ln + 1))
            for q in range(2):
                mm = nc.tensor.matmul(misc[:, q, 0:HALF], ones[:], zc[:, halves[q]], start=True, stop=True)
            pe.wait_ge(ln_sumq, DT * (ln + 1))
            for q in range(2):
                mm = nc.tensor.matmul(misc[:, 2 + q, 0:HALF], ones[:], zq[:, halves[q]], start=True, stop=True)
            mm.then_inc(ln_mm, 1)

        def two(t):
            return t[:, :].rearrange("p (h n) -> p h n", h=2)

        def z_ready(eng, d, z):
            eng.wait_ge(*z(d))

        def pool_ln(pool, ln, z, split):
            for d in range(NCEN):
                z_ready(pool, d, z)
                if d == 0:
                    if ln:
                        pool.wait_ge(ln_scaled, 2 * DT * ln)
                    nc.gpsimd.tensor_copy(zc[:, :], r[:, 0, :]).then_inc(ln_sum1, 1)
                else:
                    pool.wait_ge(ln_sum1, NCEN * ln + d)
                    nc.gpsimd.tensor_tensor(zc[:, :], zc[:, :], r[:, d, :], ALU.add).then_inc(ln_sum1, 1)
            for d in range(DT):
                pool.wait_ge(ln_sq, DT * ln + d + 1)
                if d == 0:
                    nc.gpsimd.tensor_copy(zq[:, :], sq[0][:, :]).then_inc(ln_sumq, 1)
                else:
                    pool.wait_ge(ln_sumq, DT * ln + d)
                    nc.gpsimd.tensor_tensor(zq[:, :], zq[:, :], sq[d % 2][:, :], ALU.add).then_inc(ln_sumq, 1)
            if split is not None:
                pool_lo(pool, split)

        def pool_lo(pool, have, src=None):
            for d in range(DT):
                pool.wait_ge(xh_ready, have + d + 1)
                nc.gpsimd.tensor_tensor(xl[:, d, :], r[:, d, :], xh[:, d, :].bitcast(F32),
                                        ALU.subtract).then_inc(x_ready, 1)

        def dve_centre(dve, ln, d):
            if d == 0:
                dve.wait_ge(ln_centre, ln + 1)
            nc.vector.tensor_tensor(r[:, d, :], r[:, d, :], cb[:, :], ALU.subtract).then_inc(ln_centred, 1)
            dve.wait_ge(ln_centred, DT * ln + d + 1)
            if d == 0:
                nc.vector.tensor_copy(zc[:, :], r[:, 0, :]).then_inc(ln_sumc, 1)
            else:
                dve.wait_ge(ln_sumc, DT * ln + d)
                nc.vector.tensor_tensor(zc[:, :], zc[:, :], r[:, d, :], ALU.add).then_inc(ln_sumc, 1)

        def dve_ln(dve, ln):
            dve.wait_ge(ln_mean, ln + 1)
            link(dve, nc.vector.tensor_tensor(sq[0][:, :], cb[:, :], cb[:, :], ALU.mult))
            nc.vector.scalar_tensor_tensor(out=two(sq[0]), in0=misc[:, 2:4, 0:HALF], scalar=1.0 / D,
                                           in1=two(sq[0]), op0=ALU.mult, op1=ALU.subtract).then_inc(ln_var, 1)
            dve.wait_ge(ln_sd, ln + 1)
            link(dve, nc.vector.reciprocal(rstd[:, :], sq[1][:, :]))
            link(dve, nc.vector.tensor_tensor(cb[:, :], cb[:, :], rstd[:, :], ALU.mult))
            for d in range(DT):
                nc.vector.tensor_tensor(r[:, d, :], r[:, d, :], rstd[:, :], ALU.mult).then_inc(ln_scaled, 1)
                dve.wait_ge(ln_scaled, 2 * DT * ln + 2 * d + 1)
                nc.vector.tensor_tensor(r[:, d, :], r[:, d, :], cb[:, :], ALU.subtract).then_inc(ln_scaled, 1)

        def act_centre(act, ln):
            act.wait_ge(ln_centre_mm, ln + 1)
            nc.scalar.activation(two(cb), misc[:, 0:2, 0:HALF], ACT.Copy, scale=1.0 / (NCEN * P)).then_inc(ln_centre, 1)

        def act_square(act, ln, d):
            act.wait_ge(ln_centred, DT * ln + d + 1)
            if d >= 2:
                act.wait_ge(ln_sumq, DT * ln + d - 1)
            elif ln:
                act.wait_ge(ln_scaled, 2 * DT * ln)
            nc.scalar.activation(sq[d % 2][:, :], r[:, d, :], ACT.Square).then_inc(ln_sq, 1)

        def act_ln(act, ln, split):
            act.wait_ge(ln_mm, ln + 1)
            act.wait_ge(ln_centred, DT * (ln + 1))
            nc.scalar.activation(two(cb), misc[:, 0:2, 0:HALF], ACT.Copy, scale=1.0 / D).then_inc(ln_mean, 1)
            act.wait_ge(ln_var, ln + 1)
            nc.scalar.activation(sq[1][:, :], sq[0][:, :], ACT.Sqrt, bias=small[:, 0:1]).then_inc(ln_sd, 1)
            for d in range(DT):
                act.wait_ge(ln_scaled, 2 * DT * ln + 2 * d + 2)
                col = ln * DT + d
                nc.scalar.activation(r[:, d, :], r[:, d, :], ACT.Identity, scale=vec[:, col:col + 1],
                                     bias=vec[:, 48 + col:49 + col]).then_inc(ln_out, 1)
                if split is not None:
                    act.wait_ge(ln_out, DT * ln + d + 1)
                    nc.scalar.copy(xh[:, d, :], r[:, d, :]).then_inc(xh_ready, 1)

        def act_out(act, base, k, ln):
            def body(i):
                for odd in range(2):
                    ahead(act_hi, act, base, i, DT // 2, k, odd)
                if ln is not None and isinstance(i, int) and i == DT // 2 - 1:
                    act_centre(act, ln)
                    for d in range(DT):
                        act_square(act, ln, d)
            pairs(act, DT // 2, body)

        def dve_out(dve, base, k, alpha, ln):
            def body(i):
                for odd in range(2):
                    n, turn, s = tile(base, i, odd)
                    ahead(dve_lo, dve, base, i, DT // 2, k, odd)
                    dve.wait_ge(tile_done, n + 1)
                    rd = r[:, bass.ds(2 * i + odd, 1), :].rearrange("p a (h n) -> p (a h) n", h=2)
                    nc.vector.scalar_tensor_tensor(out=rd, in0=rd, scalar=alpha, in1=ps[:, s, :, 0:HALF],
                                                   op0=ALU.mult, op1=ALU.add).then_inc(drained[s], 1)
                    if ln is not None and isinstance(i, int) and i == DT // 2 - 1:
                        if odd == 0:
                            for d in range(NCEN):
                                dve_centre(dve, ln, d)
                        dve.wait_ge(drained[s], turn + 1)
                        dve_centre(dve, ln, NCEN + odd)
            pairs(dve, DT // 2, body)

        N_PART = 10
        TRIG_PAIR = 5
        MADE_BY_LOOP = range(2, DT)

        def beside(ffn, p, eng):
            if ffn:
                return [FH - 1]
            if p:
                return [i for i in range(FH) if i not in MADE_BY_LOOP]
            return {"dve": range(FH), "act": [0, TRIG_PAIR, FH - 1]}.get(eng, [0, FH - 1])

        def tables_of(ffn, p, i, lag):
            if ffn or not p or (isinstance(i, int) and not lag <= i < DT + lag):
                return None
            return i - lag

        def act_ffn(act, base, ffn, ln, split):
            for p in range(2):
                def body_in(i, b=base, p=p):
                    n, turn, s = tile(b, i, 0)
                    ahead(act_hi, act, b, i, FH, DT, 0)
                    act.wait_ge(tile_done, n + 1)
                    wait(act, drained[1], turn)
                    nc.scalar.activation(two(sil), ps[:, 0, :, 0:HALF], ACT.Silu).then_inc(drained[0], 1)
                    dt = tables_of(ffn, p, i, 1)
                    if dt is not None:
                        act_input_tables(act, dt)
                    if ffn == 0 and p == 0 and isinstance(i, int) and i == TRIG_PAIR:
                        act_trig(act)
                    ahead(act_hi, act, b, i, FH, DT, 1)
                    if dt is not None:
                        act_toeplitz(act, dt)
                    act.wait_ge(drained[1], turn + 1)
                    nc.scalar.copy(hh[:, bass.ds(i, 1), :], hf[:, :].unsqueeze(1)).then_inc(hh_ready, 1)
                    if dt is not None:
                        act_store_toeplitz(act, dt)
                peeled(act, FH, body_in, beside(ffn, p, "act"))
                base += 2 * FH

                act_out(act, base, FH, ln if p else None)
                base += DT
            act_ln(act, ln, split)

        def dve_ffn(dve, base, ffn, ln):
            for p in range(2):
                def body_in(i, b=base, p=p, done=(2 * ffn + p) * FH):
                    n, turn, s = tile(b, i, 0)
                    ahead(dve_lo, dve, b, i, FH, DT, 0)
                    if ffn == 0 and p == 0 and isinstance(i, int) and i < N_PART:
                        dve_params(dve, i)
                    dt = tables_of(ffn, p, i, 0)
                    if dt is not None:
                        dve_tables(dve, dt)
                    ahead(dve_lo, dve, b, i, FH, DT, 1)
                    dve.wait_ge(tile_done, n + 2)
                    dve.wait_ge(drained[0], turn + 1)
                    wait(dve, hl_ready, i + done)
                    nc.vector.scalar_tensor_tensor(out=two(hf), in0=two(sil), scalar=0.5,
                                                   in1=ps[:, 1, :, 0:HALF], op0=ALU.mult,
                                                   op1=ALU.mult).then_inc(drained[1], 1)
                peeled(dve, FH, body_in, beside(ffn, p, "dve"))
                base += 2 * FH

                dve_out(dve, base, FH, 1.0 if p else ALPHA, ln if p else None)
                base += DT
            dve_ln(dve, ln)

        def pool_ffn(pool, base, ffn, ln, split):
            for p in range(2):
                def body_in(i, p=p, done=(2 * ffn + p) * FH):
                    dt = tables_of(ffn, p, i, 0)
                    if dt is not None:
                        pool_tables(pool, dt)
                    pool.wait_ge(hh_ready, i + (done + 1))
                    nc.gpsimd.tensor_tensor(hl[:, bass.ds(i, 1), :], hf[:, :].unsqueeze(1),
                                            hh[:, bass.ds(i, 1), :].bitcast(F32),
                                            ALU.subtract).then_inc(hl_ready, 1)
                peeled(pool, FH, body_in, beside(ffn, p, "pool"))
            first = base + 2 * (2 * FH) + DT
            pool_ln(pool, ln, lambda d: (drained[d % 2], (first + d) // 2 + 1), split)

        def sp_setup(sp):
            for i in range(4):
                sp.dma_start(xtok[:, i, :], x_prompt[0, i * P:(i + 1) * P, :]).then_inc(s_x, 16)
            sp.dma_start(xtok[0:DEC, 4, :], x_sample[0]).then_inc(s_x, 16)
            loads = [
                (rows[0:48, 0, :], ln_g.rearrange("l s (d p) -> (l s d) p", p=P)),
                (rows[48:96, 0, :], ln_b.rearrange("l s (d p) -> (l s d) p", p=P)),
                (rows[96:104, 0, :], ssm_d.rearrange("a (d p) -> (a d) p", p=P)),
                (rows[104:105, 0, :], subln_g),
                (rows[0:32, 1, :], a_re[0].rearrange("(a b) p -> a (b p)", b=2)),
                (rows[32:64, 1, :], a_im[0].rearrange("(a b) p -> a (b p)", b=2)),
                (rows[96:128, 1, :], state_re[0, 0].rearrange("(a b) p -> a (b p)", b=2)),
                (rows2[0:32, :], state_im[0, 0].rearrange("(a b) p -> a (b p)", b=2)),
                (dtrow[:, :], log_dt[0].rearrange("(a b) -> a b", b=2)),
                (cosT[:, :], rope_cos), (sinT[:, :], rope_sin),
                (braw[:, 0], b_re[0].rearrange("(a b) p c -> (b p) a c", b=2)),
                (braw[:, 1], b_im[0].rearrange("(a b) p c -> (b p) a c", b=2)),
            ]
            for ri, c in enumerate((c_re, c_im)):
                cv = c[0].rearrange("(d g) c p -> (g c) d p", d=DT)
                for dup in range(2):
                    loads.append((craw[:, ri, :, dup, :], cv))
            sp.wait_ge(s_pad, 1)
            loads.append((lamv[:].rearrange("p a b -> p (a b)"),
                          attn_lam.rearrange("a b c -> a (b c)").broadcast_to([P, 4 * HD])))
            for dst, src in loads:
                sp.dma_start(dst, src).then_inc(s_small, 16)
            assert 16 * len(loads) == N_SMALL
        N_SMALL = 16 * 18

        def pool_setup(pool):
            nc.gpsimd.memset(ident[:, :], 0.0).then_inc(s_const, 1)
            pool.wait_ge(s_const, 1)
            nc.gpsimd.affine_select(out=ident[:, :], in_=ident[:, :], compare_op=ALU.not_equal, fill=1.0,
                                    base=0, pattern=[[-1, P]], channel_multiplier=1).then_inc(s_const, 1)
            pool_lo(pool, X_IN)

        def pe_setup(pe):
            pe.wait_ge(s_const, 2)
            pe.wait_ge(s_x, 80)
            for d in range(DT):
                if d >= 2:
                    pe.wait_ge(s_r, d - 1)
                for i, (t0, n) in enumerate(TT):
                    mm = nc.tensor.transpose(mflat[:, (d % 2) * 1024 + t0:(d % 2) * 1024 + t0 + n],
                                             xtok[0:n, i, d * P:(d + 1) * P], ident[0:n, 0:n])
                mm.then_inc(s_tp, 1)
            pe.wait_ge(s_small, N_SMALL)
            pe.wait_ge(s_r, DT)
            pe.wait_ge(s_tpc, 1)
            nc.tensor.transpose(mflat[:, 0:P], rows[:, 0, :], ident[:])
            nc.tensor.transpose(mflat[:, P:2 * P], rows[:, 1, :], ident[:])
            nc.tensor.transpose(mflat[:, 2 * P:2 * P + 32], rows2[0:32, :], ident[0:32, 0:32]).then_inc(s_tp, 1)
            for ri in range(2):
                for d in range(DT):
                    mm = nc.tensor.transpose(mflat[:, 1024 + d * P :1024 + (d + 1) * P],
                                             craw[:, ri, d].rearrange("p a b -> p (a b)"), ident[:])
                mm.then_inc(s_tp, 1)
                if ri == 0:
                    pe.wait_ge(s_cm, 2)

        s_cm = sem("c_copied")

        def act_setup(act):
            for d in range(DT):
                act.wait_ge(s_r, d + 1)
                nc.scalar.copy(xh[:, d, :], r[:, d, :]).then_inc(xh_ready, 1)

        def act_trig(act):
            act.wait_ge(s_ang, 1)
            nc.scalar.activation(tmp[:, 8, :], tmp[:, 6, :], ACT.Sin).then_inc(s_trig, 1)
            nc.scalar.activation(tmp[:, 9, :], tmp[:, 7, :], ACT.Sin).then_inc(s_trig, 1)

        s_ang = sem("angles_ready")
        s_trig = sem("trig_ready")
        s_exps = sem("exponent_int")
        s_params = sem("s5_params_ready")

        def v_exp(dve, out, x_, a, b, c, kint=kint[:, :]):
            V = nc.vector
            link(dve, V.tensor_scalar(c, x_, -87.0, 88.0, ALU.max, ALU.min))
            link(dve, V.tensor_scalar(a, c, 1.0 / math.log(2), ROUND, ALU.mult, ALU.add))
            link(dve, V.tensor_scalar(a, a, ROUND, None, ALU.subtract))
            link(dve, V.scalar_tensor_tensor(out=b, in0=a, scalar=-LN2_1, in1=c, op0=ALU.mult, op1=ALU.add))
            link(dve, V.scalar_tensor_tensor(out=b, in0=a, scalar=-LN2_2, in1=b, op0=ALU.mult, op1=ALU.add))
            link(dve, V.tensor_scalar(kint, a, 127.0, 2.0 ** 23, ALU.add, ALU.mult))
            co = [1.0 / math.factorial(i) for i in range(9)]
            link(dve, V.tensor_scalar(c, b, co[8], None, ALU.mult))
            for i in range(7, 0, -1):
                link(dve, V.scalar_tensor_tensor(out=c, in0=c, scalar=co[i], in1=b, op0=ALU.add, op1=ALU.mult))
            link(dve, V.scalar_tensor_tensor(out=out, in0=c, scalar=1.0, in1=kint.bitcast(F32), op0=ALU.add, op1=ALU.mult))

        def v_cmul(dve, orr, oi, ar, ai, br, bi, t0, t1):
            V = nc.vector
            link(dve, V.tensor_tensor(t0, ar, br, ALU.mult))
            link(dve, V.tensor_tensor(t1, ai, bi, ALU.mult))
            link(dve, V.tensor_tensor(orr, t0, t1, ALU.subtract))
            link(dve, V.tensor_tensor(t0, ar, bi, ALU.mult))
            link(dve, V.tensor_tensor(t1, ai, br, ALU.mult))
            link(dve, V.tensor_tensor(oi, t0, t1, ALU.add))

        def dve_setup(dve):
            V = nc.vector
            V.memset(ones[:, :], 1.0)
            V.memset(small[:, :], LN_EPS)
            V.memset(rows[96:128, 0, :], 0.0).then_inc(s_pad, 1)
            dve.wait_ge(s_pad, 1)
            for d in range(DT):
                dve.wait_ge(s_tp, d + 1)
                nc.vector.tensor_copy(r[:, d, :], mflat[:, (d % 2) * 1024:(d % 2) * 1024 + T]).then_inc(s_r, 1)
            dve.wait_ge(s_small, N_SMALL)
            V.tensor_copy(rows[64:96, 1, :].rearrange("a (b p) -> a b p", b=2),
                          dtrow[:, :].unsqueeze(2).broadcast_to([NPAIR, 2, PS])).then_inc(s_tpc, 1)
            dve.wait_ge(s_tp, DT + 1)
            link(dve, V.tensor_copy(vec[:, :], mflat[:, 0:P]))
            link(dve, V.tensor_copy(vs[:].rearrange("p a b -> p (a b)"), mflat[:, P:P + 160]))
            link(dve, V.tensor_scalar(small[:, 3:4], vec[:, 104:105], 1.0 - LAM_INIT, None, ALU.mult))
            for ri in range(2):
                dve.wait_ge(s_tp, DT + 2 + ri)
                src = mflat[:, 1024:2048].rearrange("p (a g c) -> p a g c", g=2, c=GC)
                for g in range(2):
                    V.tensor_copy(cmat[64 * g:64 * g + 64, ri], src[64 * g:64 * g + 64, :, g, :]).then_inc(s_cm, 1)
            dve.wait_ge(s_cm, 4)
            link(dve, V.tensor_scalar(cmat[:, 2], cmat[:, 1], -1.0, None, ALU.mult))
            link(dve, V.memset(maskrow[:, 0:CHUNK], 1.0))
            link(dve, V.memset(maskrow[:, CHUNK:P], 0.0))
            V.memset(maskrow[:, P:P + CHUNK], -1e30).then_inc(s_pad, 1)

        def dve_params(dve, part):
            V = nc.vector
            X = [tmp[:, i, :] for i in range(20)]
            lr, li = X[0], vs[:, 1, :]
            lbr, lbi = lp[:, 0, :, 1], lp[:, 1, :, 1]
            if part == 0:
                for k in range(2):
                    link(dve, V.tensor_tensor(lamv[:, 2 * k], lamv[:, 2 * k], lamv[:, 2 * k + 1], ALU.mult))
                    link(dve, V.reduce_sum(X[15][:, k:k + 1], lamv[:, 2 * k], axis=AX.X))
                v_exp(dve, X[16][:, 0:2], X[15][:, 0:2], X[17][:, 0:2], X[18][:, 0:2], X[19][:, 0:2], kint[:, 0:2])
                link(dve, V.tensor_tensor(small[:, 1:2], X[16][:, 1:2], X[16][:, 0:1], ALU.subtract))
                link(dve, V.tensor_scalar(small[:, 1:2], small[:, 1:2], -LAM_INIT, None, ALU.add))
                link(dve, V.memset(small[0:DEC, 4:5], 1.0))
                link(dve, V.tensor_copy(small[DEC:P, 4:5], small[DEC:P, 1:2]))
            elif part == 1:
                link(dve, V.tensor_scalar(lr, vs[:, 0, :], -1e-4, None, ALU.min))
                v_exp(dve, X[1], vs[:, 2, :], X[10], X[11], X[12])
                link(dve, V.tensor_tensor(X[2], lr, X[1], ALU.mult))
            elif part == 2:
                v_exp(dve, X[3], X[2], X[10], X[11], X[12])
            elif part == 3:
                link(dve, V.tensor_tensor(X[4], li, X[1], ALU.mult))
                for out, shift in ((X[6], 0.0), (X[7], 0.25)):
                    link(dve, V.tensor_scalar(X[10], X[4], 1 / (2 * math.pi), shift, ALU.mult, ALU.add))
                    link(dve, V.tensor_scalar(X[10], X[10], ROUND, ROUND, ALU.add, ALU.subtract))
                    for c in (TWO_PI_1, TWO_PI_2, TWO_PI_3):
                        link(dve, V.scalar_tensor_tensor(out=X[11], in0=X[10], scalar=-c,
                                                         in1=X[4] if c == TWO_PI_1 else X[11],
                                                         op0=ALU.mult, op1=ALU.add))
                    link(dve, V.tensor_scalar(X[11], X[11], shift * 2 * math.pi, math.pi, ALU.add, ALU.min))
                    if shift:
                        V.tensor_scalar(out, X[11], -math.pi, None, ALU.max).then_inc(s_ang, 1)
                    else:
                        link(dve, V.tensor_scalar(out, X[11], -math.pi, None, ALU.max))
            elif part == 4:
                link(dve, V.memset(lp[:, 0, :, 0], 1.0))
                link(dve, V.memset(lp[:, 1, :, 0], 0.0))
            elif part == TRIG_PAIR + 1:
                dve.wait_ge(s_trig, 2)
                link(dve, V.tensor_tensor(lbi, X[3], X[8], ALU.mult))
                link(dve, V.tensor_tensor(lbr, X[3], X[9], ALU.mult))
                link(dve, V.tensor_scalar(X[5], lbr, -1.0, None, ALU.add))
                link(dve, V.tensor_tensor(X[10], lr, lr, ALU.mult))
                link(dve, V.tensor_tensor(X[11], li, li, ALU.mult))
                link(dve, V.tensor_tensor(X[10], X[10], X[11], ALU.add))
                link(dve, V.reciprocal(X[12], X[10]))
                link(dve, V.tensor_tensor(X[10], X[5], lr, ALU.mult))
                link(dve, V.tensor_tensor(X[11], lbi, li, ALU.mult))
                link(dve, V.tensor_tensor(X[10], X[10], X[11], ALU.add))
                link(dve, V.tensor_tensor(X[13], X[10], X[12], ALU.mult))
                link(dve, V.tensor_tensor(X[10], lbi, lr, ALU.mult))
                link(dve, V.tensor_tensor(X[11], X[5], li, ALU.mult))
                link(dve, V.tensor_tensor(X[10], X[10], X[11], ALU.subtract))
                link(dve, V.tensor_tensor(X[14], X[10], X[12], ALU.mult))
            elif part == TRIG_PAIR + 2:
                cr = X[13].unsqueeze(2).broadcast_to([P, NPAIR, GC])
                ci = X[14].unsqueeze(2).broadcast_to([P, NPAIR, GC])
                w0, w1 = (t[:, 0:512].rearrange("p (a c) -> p a c", c=GC) for t in prod)
                v_cmul(dve, bbar[:, 0], bbar[:, 1], cr, ci, braw[:, 0], braw[:, 1], w0, w1)
            elif part == TRIG_PAIR + 3:
                for k in (1, 2, 4):
                    w0, w1 = (t[:, 0:NPAIR * k].rearrange("p (a j) -> p a j", j=k) for t in prod)
                    b0, b1 = (lp[:, ri, :, k:k + 1].broadcast_to([P, NPAIR, k]) for ri in range(2))
                    v_cmul(dve, lp[:, 0, :, k + 1:2 * k + 1], lp[:, 1, :, k + 1:2 * k + 1],
                           lp[:, 0, :, 1:k + 1], lp[:, 1, :, 1:k + 1], b0, b1, w0, w1)
            elif part == TRIG_PAIR + 4:
                for j in range(BLK):
                    V.tensor_copy(lpr[:, :, :, j], lp[:, :, :, BLK - 1 - j])
                V.memset(ebuf[:].rearrange("p a b c d e -> p (a b c d e)"), 0.0)
                V.memset(cp[:].rearrange("p a b c d e -> p (a b c d e)"), 0.0)
                V.memset(tt[:].rearrange("p a b c -> p (a b c)"), 0.0).then_inc(s_params, 1)
                dve.wait_ge(s_params, 1)

        s_pad = sem("padded")

        s_e = sem("input_powers")
        s_c = sem("output_powers")
        s_tb = sem("tables_multiplied")
        s_tw = sem("tables_copied")
        s_tdw, s_tdc, s_tdt = (sem(f"table_{k}_stored") for k in "wct")
        s_pv = sem("products")
        s_pp = sem("pool_products")

        def later(dt):
            return not (isinstance(dt, int) and dt == 0)

        def dve_tables(dve, dt):
            V = nc.vector
            br, bi = (bbar[:, ri, bass.ds(4 * dt, 4), :].unsqueeze(2).broadcast_to([P, 4, BLK, GC]) for ri in range(2))
            lr, li = (lpr[:, ri, bass.ds(4 * dt, 4), :].unsqueeze(3).broadcast_to([P, 4, BLK, GC]) for ri in range(2))
            pr = [t[:, 0:4 * BLK * GC].rearrange("p (q j c) -> p q j c", q=4, c=GC) for t in prod]
            for ri, op in ((0, ALU.subtract), (1, ALU.add)):
                if ri:
                    dve.wait_ge(s_e, 4 * dt + 2)
                elif later(dt):
                    dve.wait_ge(s_e, 4 * dt)
                for k, (a, b) in enumerate(((br, lr), (bi, li)) if ri == 0 else ((br, li), (bi, lr))):
                    V.tensor_tensor(pr[k], a, b, ALU.mult).then_inc(s_pv, 1)
                dve.wait_ge(s_pv, 4 * dt + (2 + 2 * ri))
                if ri == 0 and later(dt):
                    dve.wait_ge(s_tb, 3 * dt)
                for g in range(2):
                    h = slice(64 * g, 64 * g + 64)
                    V.tensor_tensor(ebuf[h, ri, :, :, g, :], pr[0][h], pr[1][h], op).then_inc(s_e, 1)

        def pool_tables(pool, dt):
            G = nc.gpsimd
            cr, ci, nci = (cmat[:, k, bass.ds(4 * dt, 4), :].unsqueeze(2).broadcast_to([P, 4, BLK + 1, GC]) for k in range(3))
            lr, li = (lp[:, ri, bass.ds(4 * dt, 4), :].unsqueeze(3).broadcast_to([P, 4, BLK + 1, GC]) for ri in range(2))
            pr = [t[:, :].rearrange("p (q j c) -> p q j c", q=4, c=GC) for t in prodc]
            if later(dt):
                pool.wait_ge(s_c, 4 * dt)
            else:
                pool.wait_ge(s_params, 1)
            for k, (a, b) in enumerate(((cr, lr), (ci, li), (nci, lr), (cr, li))):
                G.tensor_tensor(pr[k], a, b, ALU.mult).then_inc(s_pp, 1)
            pool.wait_ge(s_pp, 4 * dt + 4)
            if later(dt):
                pool.wait_ge(s_tb, 3 * dt)
                pool.wait_ge(s_tdc, 16 * dt)
            for ri in range(2):
                for g in range(2):
                    h = slice(64 * g, 64 * g + 64)
                    G.tensor_tensor(cp[h, ri, :, :, g, :], pr[2 * ri][h], pr[2 * ri + 1][h],
                                    ALU.subtract).then_inc(s_c, 1)
                    pool.wait_ge(s_c, 4 * dt + (2 * ri + g + 1))

        def pe_tables(pe, dt):
            pe.wait_ge(s_e, 4 * dt + 4)
            if later(dt):
                pe.wait_ge(s_tw, 6 * dt)
            for ri in range(2):
                for q in range(4):
                    for jh in range(2):
                        k = ri * 1024 + (q * 2 + jh) * P
                        mm = nc.tensor.transpose(
                            mflat[:, k:k + P],
                            ebuf[:, ri, q, 4 * jh:4 * jh + 4].rearrange("p j g c -> p (j g c)"), ident[:])
                mm.then_inc(s_tb, 1)
            pe.wait_ge(s_c, 4 * dt + 4)
            pe.wait_ge(s_tw, 6 * dt + 1)
            for q in range(4):
                for ri in range(2):
                    mm = nc.tensor.matmul(mflat[0:32, q * 256:(q + 1) * 256],
                                          ebuf[:, ri, q, BLK - 1].rearrange("p g c -> p (g c)"),
                                          cp[:, ri, q, 0:BLK].rearrange("p j g c -> p (j g c)"),
                                          start=ri == 0, stop=ri == 1, skip_group_check=True)
            mm.then_inc(s_tb, 1)

        def table_row(scr, dt):
            return scr[bass.ds(dt, 1)].rearrange("a p n -> (a p) n")

        def act_input_tables(act, dt):
            act.wait_ge(s_c, 4 * dt + 4)
            act.dma_start(table_row(scr_c, dt).rearrange("p (a b n) -> p a b n", a=2, b=4),
                          cp[:, :, :, 1:BLK + 1].rearrange("p a q j g c -> p a q (j g c)")).then_inc(s_tdc, 16)
            if later(dt):
                act.wait_ge(s_tdw, 16 * dt)
            for ri in range(2):
                act.wait_ge(s_tb, 3 * dt + (ri + 1))
                nc.scalar.copy(wt[:, ri].rearrange("p q j s -> p (q j s)"),
                               mflat[:, ri * 1024:(ri + 1) * 1024]).then_inc(s_tw, 1)

        def act_toeplitz(act, dt):
            act.wait_ge(s_tw, 6 * dt + 2)
            act.dma_start(table_row(scr_w, dt), wt[:].rearrange("p a q j s -> p (a q j s)")).then_inc(s_tdw, 16)
            act.wait_ge(s_tb, 3 * dt + 3)
            if later(dt):
                act.wait_ge(s_tdt, 16 * dt)
            src = mflat[0:32, 0:1024].rearrange("p (q j c) -> p q j c", q=4, c=32)
            for jj in range(4):
                nc.scalar.copy(tt[32 * jj:32 * jj + 32, :, jj:BLK, :], src[:, :, 0:BLK - jj, :]).then_inc(s_tw, 1)

        def act_store_toeplitz(act, dt):
            act.wait_ge(s_tw, 6 * dt + 6)
            act.dma_start(table_row(scr_t, dt), tt[:].rearrange("p q j c -> p (q j c)")).then_inc(s_tdt, 16)

        s_u4 = sem("u4_ready")
        s_wl = [sem(f"wt2_loaded{s}") for s in range(2)]
        s_bl = [sem(f"cp2_tt2_loaded{s}") for s in range(2)]
        s_wm = sem("block_inputs_multiplied")
        s_wc = sem("block_inputs_copied")
        s_init = sem("states_initial")
        s_sa = sem("scan_products")
        s_sh = sem("scan_states")
        s_hp = sem("sample_scan")
        s_ym = sem("y_multiplied")
        s_yd = sem("y_copied_dve")
        s_ya = sem("y_copied_act")
        s_ys = sem("y_with_skip")
        s_ge = sem("gelu_done")
        s_st = sem("states_transposed")
        s_so = sem("states_copied")
        s_out = sem("stored")

        def sp_s5(sp):
            for s_ in (s_tdw, s_tdc, s_tdt):
                sp.wait_ge(s_, 16 * DT)
            for dt in range(DT):
                s = dt % 2
                if dt >= 2:
                    sp.wait_ge(s_wm, dt - 1)
                sp.dma_start(wt2[s][:].rearrange("p a q j s -> p (a q j s)"), scr_w[dt]).then_inc(s_wl[s], 16)
            for dt in range(DT):
                s = dt % 2
                if dt >= 2:
                    sp.wait_ge(s_ym, dt - 1)
                sp.dma_start(cp2[s][:].rearrange("p a q j g c -> p (a q j g c)"), scr_c[dt]).then_inc(s_bl[s], 16)
                sp.dma_start(tt2[s][:].rearrange("p q j c -> p (q j c)"), scr_t[dt]).then_inc(s_bl[s], 16)

        def u4_copy(eng_copy, jj, s):
            for q in range(4):
                src = r[32 * q:32 * q + 32, :, jj::4].rearrange("p d (n j) -> p d j n", j=2)
                eng_copy(u4[32 * jj:32 * jj + 32, :, q, :, :], src).then_inc(s_u4, 1)

        def dve_s5(dve):
            V = nc.vector
            dve.wait_ge(ln_out, DT)
            for jj in (0, 1):
                u4_copy(V.tensor_copy, jj, None)
            for dt in range(DT):
                dve.wait_ge(s_wm, dt + 1)
                b = dt % 2
                src = mflat[:, b * 1024:(b + 1) * 1024].rearrange("p (r n) -> p r n", r=2)[:, :, 0:4 * NB] \
                    .rearrange("p r (q n) -> p r q n", q=4)
                for ri in range(2):
                    V.tensor_copy(hs[:, ri, 4 * dt:4 * dt + 4, 1:NB], src[:, ri, :, 0:NB - 1]).then_inc(s_wc, 1)
                    V.tensor_copy(hlast[:, ri, 4 * dt:4 * dt + 4, :],
                                  src[:, ri, :, NBP - 1::DEC // BLK]).then_inc(s_wc, 1)
            dve.wait_ge(s_wc, 4 * DT)
            V.memset(hs[:, :, :, 0], 0.0).then_inc(s_init, 1)
            V.tensor_copy(hs[:, :, :, NBP], vs[:, 3:5, :]).then_inc(s_init, 1)
            for half in range(2):
                V.tensor_copy(lam8[:, 0, half, :], lp[:, 0, :, BLK]).then_inc(s_init, 1)
            V.tensor_scalar(lam8[:, 1, 0, :], lp[:, 1, :, BLK], -1.0, None, ALU.mult).then_inc(s_init, 1)
            V.tensor_copy(lam8[:, 1, 1, :], lp[:, 1, :, BLK]).then_inc(s_init, 1)
            dve.wait_ge(s_init, 6)
            for n in range(NBP):
                cur = hs[:, :, :, n]
                nxt = hs[:, :, :, n + 1] if n + 1 < NBP else hlast[:, :, :, 0]
                if n:
                    dve.wait_ge(s_sh, n)
                V.tensor_tensor(sa[:], cur, lam8[:, 0], ALU.mult).then_inc(s_sa, 1)
                V.tensor_tensor(sb2[:, 0], hs[:, 1, :, n], lam8[:, 1, 0], ALU.mult).then_inc(s_sa, 1)
                V.tensor_tensor(sb2[:, 1], hs[:, 0, :, n], lam8[:, 1, 1], ALU.mult).then_inc(s_sa, 1)
                dve.wait_ge(s_sa, 4 * n + 1)
                V.tensor_tensor(sa[:], sa[:], nxt, ALU.add).then_inc(s_sa, 1)
                dve.wait_ge(s_sa, 4 * n + 4)
                V.tensor_tensor(nxt, sa[:], sb2[:], ALU.add).then_inc(s_sh, 1)
            for dt in range(DT):
                b = dt % 2
                dve.wait_ge(s_ym, dt + 1)
                if dt:
                    dve.wait_ge(s_ge, dt)
                src = mflat[:, b * 1024:(b + 1) * 1024].rearrange("p (a n) -> p a n", a=2)[:, :, 0:4 * NB] \
                    .rearrange("p a (q j n) -> p a q j n", q=2, j=2)
                for jj in (0, 1):
                    for q in range(4):
                        dst = ysb[32 * q:32 * q + 32, jj::4].rearrange("p (n j) -> p j n", j=2)
                        V.tensor_copy(dst, src[32 * jj:32 * jj + 32, q // 2, q % 2]).then_inc(s_yd, 1)
                dve.wait_ge(s_yd, 8 * dt + 8)
                dve.wait_ge(s_ya, 8 * dt + 8)
                V.scalar_tensor_tensor(out=ysb[:, :], in0=r[:, dt, :], scalar=vec[:, 96 + dt:97 + dt],
                                       in1=ysb[:, :], op0=ALU.mult, op1=ALU.add).then_inc(s_ys, 1)

        def act_s5(act):
            act.wait_ge(ln_out, DT)
            for jj in (2, 3):
                u4_copy(nc.scalar.copy, jj, None)
            for dt in range(DT):
                b = dt % 2
                act.wait_ge(s_ym, dt + 1)
                if dt:
                    act.wait_ge(s_ge, dt)
                src = mflat[:, b * 1024:(b + 1) * 1024].rearrange("p (a n) -> p a n", a=2)[:, :, 0:4 * NB] \
                    .rearrange("p a (q j n) -> p a q j n", q=2, j=2)
                for jj in (2, 3):
                    for q in range(4):
                        dst = ysb[32 * q:32 * q + 32, jj::4].rearrange("p (n j) -> p j n", j=2)
                        nc.scalar.copy(dst, src[32 * jj:32 * jj + 32, q // 2, q % 2]).then_inc(s_ya, 1)
                act.wait_ge(s_ys, dt + 1)
                if dt:
                    act.wait_ge(x_ready, X_GELU + dt)
                nc.scalar.activation(gel[:, :], ysb[:, :], ACT.Gelu_apprx_tanh).then_inc(s_ge, 1)
                act.wait_ge(s_ge, dt + 1)
                nc.scalar.copy(xh[:, dt, :], gel[:, :]).then_inc(xh_ready, 1)
            act.wait_ge(s_st, 4)
            nc.scalar.copy(strow[:].rearrange("p a b -> p (a b)"), mflat[0:NPAIR, 0:512]).then_inc(s_so, 1)

        def pool_s5(pool):
            G = nc.gpsimd
            pool.wait_ge(s_init, 6)
            nb = DEC // BLK
            for n in range(nb):
                c = NBP + n
                cur = hs[:, :, :, c]
                nxt = hs[:, :, :, c + 1] if n + 1 < nb else hlast[:, :, :, 1]
                if n:
                    pool.wait_ge(s_hp, 5 * n)
                G.tensor_tensor(stin[:], cur, lam8[:, 0], ALU.mult).then_inc(s_hp, 1)
                G.tensor_tensor(stmp[:, 0], hs[:, 1, :, c], lam8[:, 1, 0], ALU.mult).then_inc(s_hp, 1)
                G.tensor_tensor(stmp[:, 1], hs[:, 0, :, c], lam8[:, 1, 1], ALU.mult).then_inc(s_hp, 1)
                pool.wait_ge(s_hp, 5 * n + 3)
                G.tensor_tensor(stin[:], stin[:], nxt, ALU.add).then_inc(s_hp, 1)
                pool.wait_ge(s_hp, 5 * n + 4)
                G.tensor_tensor(nxt, stin[:], stmp[:], ALU.add).then_inc(s_hp, 1)
            for d in range(DT):
                pool.wait_ge(xh_ready, X_GELU + d + 1)
                G.tensor_tensor(xl[:, d, :], gel[:, :], xh[:, d, :].bitcast(F32),
                                ALU.subtract).then_inc(x_ready, 1)

        stmp = am2("stmp", [P, 2, NPAIR])
        assert am2.at <= k_at, (am2.at - k_at)

        def pe_s5(pe):
            pe.wait_ge(s_u4, 16)
            for dt in range(DT):
                s = dt % 2
                pe.wait_ge(s_wl[s], 16 * (dt // 2 + 1))
                if dt >= 2:
                    pe.wait_ge(s_wc, 4 * (dt - 1))
                for ri in range(2):
                    for q in range(4):
                        o = misc[:, 2 * s + ri, q * NB:(q + 1) * NB]
                        for jh in range(2):
                            mm = nc.tensor.matmul(o, wt2[s][:, ri, q, jh, :], u4[:, dt, q, jh, :],
                                                  start=jh == 0, stop=jh == 1)
                mm.then_inc(s_wm, 1)
            pe.wait_ge(s_wc, 4 * DT)
            for dt in range(DT):
                s = dt % 2
                if dt == 0:
                    pe.wait_ge(s_sh, NBP)
                    pe.wait_ge(s_hp, 5 * (DEC // BLK))
                pe.wait_ge(s_bl[s], 32 * (dt // 2 + 1))
                if dt >= 2:
                    pe.wait_ge(s_yd, 8 * (dt - 1))
                    pe.wait_ge(s_ya, 8 * (dt - 1))
                for q in range(4):
                    for jh in range(2):
                        c0 = (q % 2) * 2 * NB + jh * NB
                        o = misc[:, 2 * s + q // 2, c0:c0 + NB]
                        t2 = tt2[s][:, q].rearrange("p j c -> p (j c)")
                        nc.tensor.matmul(o, t2[:, 0:P], u4[:, dt, q, jh, :], start=True, stop=False)
                        if jh:
                            nc.tensor.matmul(o, t2[:, P:2 * P], u4[:, dt, q, 0, :], start=False, stop=False)
                        for ri in range(2):
                            v = cp2[s][:, ri, q, 4 * jh:4 * jh + 4].rearrange("p j g c -> p (j g c)")
                            mm = nc.tensor.matmul(o, v, hs[:, ri, 4 * dt + q, :], start=False, stop=ri == 1)
                mm.then_inc(s_ym, 1)
            pe.wait_ge(s_yd, 8 * (DT - 1) + 0)
            pe.wait_ge(s_ya, 8 * (DT - 1))
            for k in range(4):
                nc.tensor.transpose(misc[0:NPAIR, 0, k * P:(k + 1) * P],
                                    hlast[:, k % 2, :, k // 2], ident[:]).then_inc(s_st, 1)
            pe.wait_ge(s_so, 1)

        def sp_states(sp):
            sp.wait_ge(s_so, 1)
            for k, dst in enumerate((p_re, p_im, s_re, s_im)):
                sp.dma_start(dst[0, 0].rearrange("(a b) p -> a (b p)", b=2), strow[:, k, :]).then_inc(s_out, 16)

        def act_glu(act, base, ln):
            def body(i):
                n, turn, s = tile(base, i, 0)
                ahead(act_hi, act, base, i, DT, DT, 0)
                act.wait_ge(tile_done, n + 1)
                wait(act, drained[1], turn)
                nc.scalar.activation(two(sil), ps[:, 0, :, 0:HALF], ACT.Sigmoid).then_inc(drained[0], 1)
                ahead(act_hi, act, base, i, DT, DT, 1)
                if isinstance(i, int) and i == DT - 1:
                    act_centre(act, ln)
                    for d in range(DT):
                        act_square(act, ln, d)
            pairs(act, DT, body)
            act_ln(act, ln, True)

        glu_z = sem("glu_z")

        def dve_glu(dve, base, ln):
            def body(i):
                n, turn, s = tile(base, i, 0)
                ahead(dve_lo, dve, base, i, DT, DT, 0)
                ahead(dve_lo, dve, base, i, DT, DT, 1)
                dve.wait_ge(tile_done, n + 2)
                dve.wait_ge(drained[0], turn + 1)
                wait(dve, glu_z, i)
                nc.vector.tensor_tensor(two(hf), two(sil), ps[:, 1, :, 0:HALF], ALU.mult).then_inc(drained[1], 1)
                dve.wait_ge(drained[1], turn + 1)
                rd = r[:, bass.ds(i, 1), :].rearrange("p a n -> p (a n)")
                nc.vector.scalar_tensor_tensor(out=rd, in0=rd, scalar=ALPHA, in1=hf[:, :], op0=ALU.mult,
                                               op1=ALU.add).then_inc(glu_z, 1)
                if isinstance(i, int) and i == DT - 1:
                    dve.wait_ge(glu_z, DT)
                    for d in range(DT):
                        dve_centre(dve, ln, d)
            pairs(dve, DT, body, peel_first=True)
            dve_ln(dve, ln)

        s_swap = sem("halves_swapped")
        s_rot = sem("sine_part")
        s_rope = sem("heads_rotated")
        s_vT = sem("v_copied")
        s_kvt = sem("kv_transposed")
        s_kc = sem("k_rows_copied")
        s_vc = sem("v_rows_copied")
        s_kout = sem("k_stored")

        def act_rope(act, base, done):
            def body(i):
                for odd in range(2):
                    n, turn, s = tile(base, i, odd)
                    ahead(act_hi, act, base, i, NH // 2, DT, odd)
                    act.wait_ge(tile_done, n + 1)
                    wait(act, s_rope, 2 * i + (done + odd))
                    for a, b in ((0, 32), (32, 0), (64, 96), (96, 64)):
                        nc.scalar.copy(two(sil)[a:a + 32], ps[b:b + 32, s, :, 0:HALF]).then_inc(s_swap, 1)
            pairs(act, NH // 2, body, peel_first=done == 0)

        def dve_rope(dve, base, done, dst):
            def body(i):
                for odd in range(2):
                    n, turn, s = tile(base, i, odd)
                    h = 2 * i + (done + odd)
                    ahead(dve_lo, dve, base, i, NH // 2, DT, odd)
                    dve.wait_ge(s_swap, 8 * i + (4 * (done + odd) + 4))
                    nc.vector.tensor_tensor(two(hf), ps[:, s, :, 0:HALF], two(cosT), ALU.mult).then_inc(drained[s], 1)
                    nc.vector.tensor_tensor(sil[:, :], sil[:, :], sinT[:, :], ALU.mult).then_inc(s_rot, 1)
                    dve.wait_ge(s_rot, h + 1)
                    nc.vector.tensor_tensor(dst[:, bass.ds(2 * i + odd, 1), :].rearrange("p a n -> p (a n)"),
                                            hf[:, :], sil[:, :], ALU.add).then_inc(s_rope, 1)
                    dve.wait_ge(s_rope, h + 1)
            pairs(dve, NH // 2, body)

        def act_v(act, base):
            def body(i):
                for odd in range(2):
                    n, turn, s = tile(base, i, odd)
                    ahead(act_hi, act, base, i, NH // 2, DT, odd)
                    act.wait_ge(tile_done, n + 1)
                    nc.scalar.copy(vT[:, bass.ds(2 * i + odd, 1), :].rearrange("p a (h n) -> p (a h) n", h=2),
                                   ps[:, s, :, 0:HALF]).then_inc(drained[s], 1)
            pairs(act, NH // 2, body)

        def dve_v(dve, base):
            def body(i):
                for odd in range(2):
                    ahead(dve_lo, dve, base, i, NH // 2, DT, odd)
            pairs(dve, NH // 2, body)

        def pe_kv_rows(pe):
            pe.wait_ge(s_rope, NH)
            for s in range(2):
                pe.wait_ge(drained[s], N_FFN10 // 2)
            for i, (t0, n) in enumerate(TT):
                if i:
                    pe.wait_ge(s_kc, i)
                for h in range(NH):
                    mm = nc.tensor.transpose(mflat[0:n, h * P:(h + 1) * P], kT[:, h, t0:t0 + n], ident[:])
                mm.then_inc(s_kvt, 1)
                if i:
                    pe.wait_ge(s_vc, i)
                for h in range(NH):
                    mm = nc.tensor.transpose(mflat[0:n, 1024 + h * P:1024 + (h + 1) * P], vT[:, h, t0:t0 + n], ident[:])
                mm.then_inc(s_kvt, 1)

        def act_kv_rows(act):
            for i, (t0, n) in enumerate(TT):
                act.wait_ge(s_kvt, 2 * i + 1)
                if i >= 2:
                    act.wait_ge(s_kout, 16 * (i - 1))
                nc.scalar.copy(ktok[i % 2][0:n, :], mflat[0:n, 0:1024]).then_inc(s_kc, 1)

        def dve_kv_rows(dve):
            nc.vector.memset(vtok[DEC:P, 4, :], 0.0)
            for i, (t0, n) in enumerate(TT):
                dve.wait_ge(s_kvt, 2 * i + 2)
                nc.vector.tensor_copy(vtok[0:n, i, :], mflat[0:n, 1024:2048]).then_inc(s_vc, 1)

        def sp_kv_rows(sp):
            for i, (t0, n) in enumerate(TT):
                kd = (p_k[0, t0:t0 + n] if i < 4 else s_k[0]).rearrange("t h m d -> t (h m d)")
                vd = (p_v[0, t0:t0 + n] if i < 4 else s_v[0]).rearrange("t h e -> t (h e)")
                sp.wait_ge(s_kc, i + 1)
                if i:
                    sp.wait_ge(s_kout, 16 * i)
                sp.dma_start(kd, ktok[i % 2][0:n, :]).then_inc(s_kout, 16)
                sp.wait_ge(s_vc, i + 1)
                sp.dma_start(vd, vtok[0:n, i, :]).then_inc(s_out, 16)

        ITEMS = 4 * NH
        s_qs = sem("queries_staged")
        s_sc = sem("scores")
        s_max = sem("maxima")
        s_exp = sem("exponentials")
        s_pr = sem("probabilities")
        s_pt = sem("p_transposed")
        s_ptc = sem("p_copied")
        s_o = sem("pv_done")
        s_oe = sem("o_copied")
        s_zq = sem("qs_cleared")
        v_mx = sem("v_stats")
        z_qs = sem("sample_queries_staged")
        z_kt = sem("cached_k_transposed")
        z_ktc = sem("cached_k_copied")
        z_sc = sem("sample_scores")
        z_own = sem("sample_own_scores")
        z_big = sem("sample_cached_maxima")
        z_st = sem("sample_stats")
        z_max = sem("sample_maxima")
        z_exp = sem("sample_exponentials")
        z_sum = sem("sample_sums")
        z_w = sem("sample_weights")
        z_pt = sem("sample_p_transposed")
        z_ptc = sem("sample_p_copied")
        z_o = sem("sample_pv_done")
        z_ov = sem("sample_second_map")
        z_fin = sem("sample_heads")
        s_sq = sem("squared_outputs")
        s_nq = sem("squared_norms")
        s_ck = [sem(f"cached_k_loaded{s}") for s in range(2)]
        s_cv = [sem(f"cached_v_loaded{s}") for s in range(2)]
        s_on = sem("heads_normalised")
        s_ns = sem("norm_roots")
        s_ox = sem("o_scaled")
        s_ot = sem("o_transposed")

        def item(i, j, k):
            if isinstance(j, int):
                it = 2 * j + 8 * i + k
                return it // NH, it % NH, k % 2, it
            return i, 2 * j + k, k % 2, 2 * j + (8 * i + k)

        def at_end(i, j, k):
            return isinstance(j, int) and 8 * i + 2 * j + k >= ITEMS

        def prompt_pairs(eng, body):
            for i in range(4):
                peeled(eng, NH // 2, lambda j, i=i: body(i, j), [0, NH // 2 - 1] if i == 0 else [NH // 2 - 1])

        def head(t, h, cols):
            return t[:, bass.ds(h, 1), cols].rearrange("p a n -> p (a n)")

        def vhead(i, h, rows_=P):
            return vtok[0:rows_, i, bass.ds(h * P, P)]

        def pool_attn(pool):
            G = nc.gpsimd
            pool.wait_ge(tile_done, N_O)
            for b in range(2):
                G.memset(qs[b][:].rearrange("p a b -> p (a b)"), 0.0).then_inc(s_zq, 1)
                G.memset(qd[b][:, :], 0.0).then_inc(s_zq, 1)
            pool.wait_ge(s_zq, 4)
            pool.wait_ge(s_rope, 2 * NH)

            def body(i, j):
                for k in range(2):
                    _, h, b, it = item(i, j, k)
                    wait(pool, s_sc, it - 1)
                    for m in range(2):
                        G.tensor_copy(qs[b][64 * m:64 * m + 64, m, :],
                                      head(qT, h, slice(i * P, i * P + P))[64 * m:64 * m + 64]).then_inc(s_qs, 1)
            prompt_pairs(pool, body)
            for h in range(NH):
                b = h % 2
                wait(pool, z_own, h - 1)
                for m in range(2):
                    G.tensor_copy(qd[b][64 * m:64 * m + 64, 64 * m:64 * m + 64],
                                  qT[64 * m:64 * m + 64, h, SEQ:T]).then_inc(z_qs, 1)

        def pe_attn(pe):
            pe.wait_ge(drained[0], N_O // 2)
            pe.wait_ge(drained[1], N_O // 2)
            mask_q, mask_k = maskrow[0:1, 0:P], maskrow[0:1, P:P + CHUNK]

            def scores(i, h, b, it):
                pe.wait_ge(s_qs, 2 * it + 2)
                wait(pe, s_exp, 2 * it - 2)
                kn = (i + 1) * P
                for m in range(2):
                    nc.tensor.matmul(ps[:, b, m, 0:kn], qs[b][:, m, :], head(kT, h, slice(0, kn)),
                                     start=True, stop=False)
                    mm = nc.tensor.matmul(ps[:, b, m, kn - CHUNK:kn], mask_q, mask_k, start=False, stop=True)
                mm.then_inc(s_sc, 1)

            def transposes(i, h, b, it):
                pe.wait_ge(s_pr, it + 1)
                wait(pe, s_ptc, it - 1)
                for kt in range(i + 1):
                    mm = nc.tensor.transpose(misc[:, b, kt * P:(kt + 1) * P], ex[b][:, 0, kt * P:(kt + 1) * P],
                                             ident[:])
                mm.then_inc(s_pt, 1)

            def output(i, h, b, it):
                pe.wait_ge(s_ptc, it + 1)
                wait(pe, s_oe, it - 1)
                for kt in range(i + 1):
                    mm = nc.tensor.matmul(misc[:, 2 + b, 0:P], pT[b][:, kt * P:(kt + 1) * P], vhead(kt, h),
                                          start=kt == 0, stop=kt == i)
                mm.then_inc(s_o, 1)

            def body(i, j):
                for k in range(2):
                    transposes(*item(i, j, k))
                    if not at_end(i, j, k + 2):
                        scores(*item(i, j, k + 2))
                    output(*item(i, j, k))
            for k in range(2):
                scores(*item(0, 0, k))
            prompt_pairs(pe, body)


            def cached(h, b):
                pe.wait_ge(s_ck[b], 16 * (h // 2 + 1))
                if h == 0:
                    pe.wait_ge(s_ptc, ITEMS)
                    pe.wait_ge(s_oe, ITEMS)
                wait(pe, z_ktc, h)
                for kt in range(PAST // P):
                    mm = nc.tensor.transpose(mflat[:, kt * P:(kt + 1) * P], ck[b][:, kt, :], ident[:])
                mm.then_inc(z_kt, 1)

            def scores_s(h, b):
                pe.wait_ge(z_qs, 2 * h + 2)
                pe.wait_ge(z_ktc, h + 1)
                wait(pe, z_ptc, 2 * (h - 1))
                for c in range(2):
                    mm = nc.tensor.matmul(ps[:, b, c, :], qd[b][:, :], kTc[b][:, c * 512:(c + 1) * 512],
                                          start=True, stop=True)
                mm.then_inc(z_sc, 1)

            def scores_own(h, b):
                wait(pe, z_fin, h - 1)
                nc.tensor.matmul(misc[:, 2 + b, 0:DEC], qd[b][:, :], kT[:, h, SEQ:T], start=True, stop=True,
                                 skip_group_check=True).then_inc(z_own, 1)

            for h in range(2):
                cached(h, h)
                scores_s(h, h)
            scores_own(0, 0)
            for h in range(NH):
                b = h % 2
                pe.wait_ge(z_exp, 2 * h + 2)
                for kt in range(PAST // P):
                    nc.tensor.transpose(ps[:, b].rearrange("p c n -> p (c n)")[:, kt * P:(kt + 1) * P],
                                        exS[b][:, kt * P:(kt + 1) * P], ident[:])
                nc.tensor.transpose(misc[0:DEC, 2 + b, P:2 * P], exS[b][:, PAST:PAST + DEC], ident[:]).then_inc(z_pt, 1)
                if h + 1 < NH:
                    scores_own(h + 1, 1 - b)
                if h + 2 < NH:
                    cached(h + 2, b)
                pe.wait_ge(z_ptc, 2 * h + 2)
                pe.wait_ge(s_cv[b], 16 * (h // 2 + 1))
                for kt in range(PAST // P):
                    nc.tensor.matmul(misc[:, 2 + b, 2 * P:3 * P], pTS[b][:, kt * P:(kt + 1) * P],
                                     cv[b][:, kt, :], start=kt == 0, stop=False, skip_group_check=True)
                nc.tensor.matmul(misc[:, 2 + b, 2 * P:3 * P], pTS[b][0:DEC, PAST:PAST + P], vhead(4, h, DEC),
                                 start=False, stop=True, skip_group_check=True).then_inc(z_o, 1)
                if h + 2 < NH:
                    scores_s(h + 2, b)

            for h in range(NH):
                if h == 0:
                    pe.wait_ge(s_on, 5)
                if h >= 2:
                    pe.wait_ge(s_ox, h - 1)
                for i, (t0, n) in enumerate(TT):
                    mm = nc.tensor.transpose(mflat[:, (h % 2) * 1024 + t0:(h % 2) * 1024 + t0 + n],
                                             otok[0:n, i, h * P:(h + 1) * P], ident[0:n, 0:n])
                mm.then_inc(s_ot, 1)

        def dve_attn(dve):
            V = nc.vector

            def maxima(i, h, b, it):
                st = sts[:, b]
                dve.wait_ge(s_sc, it + 1)
                V.reduce_max(st[:, 0:2], ps[:, b, :, 0:(i + 1) * P], axis=AX.X).then_inc(v_mx, 1)
                dve.wait_ge(v_mx, it + 1)
                V.tensor_scalar(st[:, 2:4], st[:, 0:2], -SCALE, None, ALU.mult).then_inc(s_max, 1)

            def combine(i, h, b, it):
                st = sts[:, b]
                kn = (i + 1) * P
                dve.wait_ge(s_exp, 2 * it + 2)
                V.reciprocal(st[:, 6:8], st[:, 4:6]).then_inc(v_rc, 1)
                dve.wait_ge(v_rc, 2 * it + 1)
                V.scalar_tensor_tensor(out=st[:, 8:9], in0=st[:, 4:5], scalar=small[:, 1:2], in1=st[:, 7:8],
                                       op0=ALU.mult, op1=ALU.mult).then_inc(v_rc, 1)
                dve.wait_ge(v_rc, 2 * it + 2)
                V.scalar_tensor_tensor(out=ex[b][:, 0, 0:kn], in0=ex[b][:, 1, 0:kn], scalar=st[:, 8:9],
                                       in1=ex[b][:, 0, 0:kn], op0=ALU.mult, op1=ALU.add).then_inc(s_pr, 1)

            def body(i, j):
                for k in range(2):
                    if not at_end(i, j, k + 1):
                        combine(*item(i, j, k + 1))
                    if not at_end(i, j, k + 2):
                        maxima(*item(i, j, k + 2))
            for k in range(2):
                maxima(*item(0, 0, k))
            combine(*item(0, 0, 0))
            prompt_pairs(dve, body)

            def keys(h, b):
                dve.wait_ge(z_kt, h + 1)
                wait(dve, z_sc, h - 1)
                V.tensor_copy(kTc[b][:, :], mflat[:, 0:PAST]).then_inc(z_ktc, 1)

            def maxima_s(h, b):
                st = stz[:, b]
                dve.wait_ge(z_sc, h + 1)
                V.reduce_max(st[:, 0:1], ps[:, b].rearrange("p c n -> p (c n)"), axis=AX.X).then_inc(z_big, 1)

            def shift_s(h, b):
                st = stz[:, b]
                dve.wait_ge(z_own, h + 1)
                V.reduce_max(st[:, 1:2], misc[:, 2 + b, 0:DEC], axis=AX.X).then_inc(z_st, 1)
                dve.wait_ge(z_big, h + 1)
                dve.wait_ge(z_st, 2 * h + 1)
                V.tensor_tensor(st[:, 2:3], st[:, 0:1], st[:, 1:2], ALU.max).then_inc(z_st, 1)
                dve.wait_ge(z_st, 2 * h + 2)
                V.tensor_scalar(st[:, 3:4], st[:, 2:3], -SCALE, None, ALU.mult).then_inc(z_max, 1)

            def weights(h, b):
                st = stz[:, b]
                dve.wait_ge(z_exp, 2 * h + 2)
                V.tensor_tensor(st[:, 4:5], st[:, 4:5], st[:, 5:6], ALU.add).then_inc(z_sum, 1)
                dve.wait_ge(z_sum, 2 * h + 1)
                V.reciprocal(st[:, 7:8], st[:, 4:5]).then_inc(z_sum, 1)
                dve.wait_ge(z_sum, 2 * h + 2)
                V.tensor_tensor(st[:, 6:7], st[:, 7:8], small[:, 4:5], ALU.mult).then_inc(z_w, 1)

            def finish(h, b):
                dve.wait_ge(z_ov, h + 1)
                V.scalar_tensor_tensor(out=otok[0:DEC, 4, h * P:(h + 1) * P], in0=misc[0:DEC, 2 + b, 2 * P:3 * P],
                                       scalar=stz[0:DEC, b, 6:7], in1=ov[b][:, :],
                                       op0=ALU.mult, op1=ALU.add).then_inc(z_fin, 1)

            def squares(i, n):
                if i == 0:
                    dve.wait_ge(s_oe, ITEMS)
                else:
                    dve.wait_ge(s_nq, i)
                V.tensor_tensor(sqb[0:n, :], otok[0:n, i, :], otok[0:n, i, :], ALU.mult).then_inc(s_sq, 1)
                dve.wait_ge(s_sq, i + 1)
                V.reduce_sum(ssq[0:n, i * NH:(i + 1) * NH], sqb[0:n, :].rearrange("p (h e) -> p h e", h=NH),
                             axis=AX.X).then_inc(s_nq, 1)

            for h in range(2):
                keys(h, h)
                maxima_s(h, h)
            shift_s(0, 0)
            for h in range(NH):
                b = h % 2
                if h:
                    finish(h - 1, 1 - b)
                weights(h, b)
                if h + 1 < NH:
                    shift_s(h + 1, 1 - b)
                if h + 2 < NH:
                    keys(h + 2, b)
                    maxima_s(h + 2, b)
                if h < 4:
                    squares(h, P)
            finish(NH - 1, 1)
            dve.wait_ge(z_fin, NH)
            squares(4, DEC)

            dve.wait_ge(s_ns, 2)
            link(dve, V.reciprocal(nrm[:, 1, 0:32], nrm[:, 0, 0:32]))
            link(dve, V.reciprocal(nrm[0:DEC, 1, 32:40], nrm[0:DEC, 0, 32:40]))
            for i, (t0, n) in enumerate(TT):
                o3 = otok[0:n, i].rearrange("p (h e) -> p h e", h=NH)
                V.tensor_tensor(o3, o3, nrm[0:n, 1, i * NH:(i + 1) * NH].unsqueeze(2).broadcast_to([n, NH, P]),
                                ALU.mult).then_inc(s_on, 1)

        v_rc = sem("v_reciprocals")

        def act_attn(act):
            A = nc.scalar

            def exps(i, h, b, it):
                kn = (i + 1) * P
                act.wait_ge(s_max, it + 1)
                wait(act, s_pt, it - 1)
                for m in range(2):
                    A.activation(ex[b][:, m, 0:kn], ps[:, b, m, 0:kn], ACT.Exp, scale=SCALE,
                                 bias=sts[:, b, 2 + m:3 + m], accum_out=sts[:, b, 4 + m:5 + m]).then_inc(s_exp, 1)

            def body(i, j):
                for k in range(2):
                    i_, h, b, it = item(i, j, k)
                    act.wait_ge(s_pt, it + 1)
                    wait(act, s_o, it - 1)
                    A.copy(pT[b][:, 0:(i + 1) * P], misc[:, b, 0:(i + 1) * P]).then_inc(s_ptc, 1)
                    act.wait_ge(s_o, it + 1)
                    A.activation(otok[:, i, bass.ds(h * P, P)], misc[:, 2 + b, 0:P], ACT.Copy,
                                 scale=sts[:, b, 6:7]).then_inc(s_oe, 1)
                    if not at_end(i, j, k + 2):
                        exps(*item(i, j, k + 2))
            for k in range(2):
                exps(*item(0, 0, k))
            prompt_pairs(act, body)

            def exps_s(h, b):
                st = stz[:, b]
                act.wait_ge(z_max, h + 1)
                wait(act, z_pt, h - 1)
                A.activation(exS[b][:, 0:PAST], ps[:, b].rearrange("p c n -> p (c n)"), ACT.Exp, scale=SCALE,
                             bias=st[:, 3:4], accum_out=st[:, 4:5]).then_inc(z_exp, 1)
                A.activation(exS[b][:, PAST:PAST + DEC], misc[:, 2 + b, 0:DEC], ACT.Exp, scale=SCALE,
                             bias=st[:, 3:4], accum_out=st[:, 5:6]).then_inc(z_exp, 1)
            exps_s(0, 0)
            for h in range(NH):
                b = h % 2
                act.wait_ge(z_pt, h + 1)
                wait(act, z_o, h - 1)
                A.copy(pTS[b][:, 0:PAST], ps[:, b].rearrange("p c n -> p (c n)")).then_inc(z_ptc, 1)
                A.copy(pTS[b][0:DEC, PAST:PAST + P], misc[0:DEC, 2 + b, P:2 * P]).then_inc(z_ptc, 1)
                if h + 1 < NH:
                    exps_s(h + 1, 1 - b)
                act.wait_ge(z_o, h + 1)
                act.wait_ge(z_w, h + 1)
                wait(act, z_fin, h - 1)
                A.activation(ov[b][:, :], misc[DEC:P, 2 + b, 2 * P:3 * P], ACT.Copy,
                             scale=stz[DEC:P, b, 6:7]).then_inc(z_ov, 1)

            act.wait_ge(s_nq, 5)
            A.activation(nrm[:, 0, 0:32], ssq[:, 0:32], ACT.Sqrt, scale=1.0 / P, bias=small[:, 0:1]).then_inc(s_ns, 1)
            A.activation(nrm[0:DEC, 0, 32:40], ssq[0:DEC, 32:40], ACT.Sqrt, scale=1.0 / P,
                         bias=small[0:DEC, 0:1]).then_inc(s_ns, 1)
            for h in range(NH):
                buf = (sil, hf)[h % 2]
                act.wait_ge(s_ot, h + 1)
                if h >= 2:
                    act.wait_ge(x_ready, X_ATT + h - 1)
                A.activation(buf[:, :], mflat[:, (h % 2) * 1024:(h % 2) * 1024 + T], ACT.Copy,
                             scale=small[:, 3:4]).then_inc(s_ox, 1)
                act.wait_ge(s_ox, h + 1)
                A.copy(xh[:, h, :], buf[:, :]).then_inc(xh_ready, 1)

        def pool_attn_out(pool):
            for h in range(NH):
                pool.wait_ge(xh_ready, X_ATT + h + 1)
                nc.gpsimd.tensor_tensor(xl[:, h, :], (sil, hf)[h % 2][:, :], xh[:, h, :].bitcast(F32),
                                        ALU.subtract).then_inc(x_ready, 1)

        def sp_attn(sp):
            sp.wait_ge(tile_done, N_Q)
            for h in range(NH + 1):
                if h < NH:
                    wait(sp, z_kt, h - 1)
                    sp.dma_start(ck[h % 2][:], cache_k[0].rearrange("(a p) h m d -> p a h (m d)", p=P)[:, :, h]
                                 ).then_inc(s_ck[h % 2], 16)
                v = h - 1
                if v >= 0:
                    wait(sp, z_o, v - 1)
                    sp.dma_start(cv[v % 2][:], cache_v[0].rearrange("(a p) h e -> p a h e", p=P)[:, :, v]
                                 ).then_inc(s_cv[v % 2], 16)

        s_yt = sem("y_transposed")
        s_yc = sem("y_rows_copied")
        s_yo = [sem(f"y_stored{s}") for s in range(2)]

        def pe_y(pe):
            pe.wait_ge(ln_out, 6 * DT)
            for i, (t0, n) in enumerate(TT):
                if i >= 2:
                    pe.wait_ge(s_yc, i - 1)
                for d in range(DT):
                    mm = nc.tensor.transpose(mflat[0:n, (i % 2) * 1024 + d * P:(i % 2) * 1024 + (d + 1) * P],
                                             r[:, d, t0:t0 + n], ident[:])
                mm.then_inc(s_yt, 1)

        def act_y(act):
            for i, (t0, n) in enumerate(TT):
                act.wait_ge(s_yt, i + 1)
                if i >= 2:
                    act.wait_ge(s_yo[i % 2], 16 * (i // 2))
                nc.scalar.copy(ytok[i % 2][0:n, :], mflat[0:n, (i % 2) * 1024:(i % 2) * 1024 + 1024]).then_inc(s_yc, 1)

        def sp_y(sp):
            for i, (t0, n) in enumerate(TT):
                sp.wait_ge(s_yc, i + 1)
                sp.dma_start(y_prompt[0, t0:t0 + n] if i < 4 else y_sample[0], ytok[i % 2][0:n, :]).then_inc(s_yo[i % 2], 16)
            sp.wait_ge(s_yo[0], 48)
            sp.wait_ge(s_yo[1], 32)

        def dump_r(sp, sems):
            for s_, v in sems:
                sp.wait_ge(s_, v)
            sp.dma_start(dump.rearrange("p (a b) -> p a b", a=DT), r[:]).then_inc(s_out, 16)

        block = ctx.enter_context(nc.Block())

        @block.sync
        def _(sp):
            sp_setup(sp)
            sp_ffn(sp, N_FFN00, 0, 0)
            n_out = 0
            if stop > 1:
                sp_stage(sp, N_GLU, DT, glu_v, lambda i: i * P + D, lambda i: i * P, DT, between=sp_s5)
                n_out += 4
            if stop > 2:
                sp_ffn(sp, N_FFN01, 0, 1, between=sp_states)
            elif stop > 1:
                sp_states(sp)
            if stop > 3:
                sp_plain(sp, N_KV, DT, kv_v)
                sp_ffn(sp, N_FFN10, 1, 0, between=sp_kv_rows)
                n_out += 5
            if stop > 4:
                sp_plain(sp, N_Q, DT // 2, q_v)
                sp_plain(sp, N_O, DT // 2, o_v, between=sp_attn)
            if stop > 5:
                sp_ffn(sp, N_FFN11, 1, 1)
                sp_y(sp)
            if dump is not None:
                dump_r(sp, [(ln_out, DT * stop)])
                n_out += 1
            if stop > 3:
                sp.wait_ge(s_kout, 80)
            for s_ in (s_tdw, s_tdc, s_tdt):
                sp.wait_ge(s_, 16 * DT)
            sp.wait_ge(s_out, 16 * n_out)

        @block.scalar
        def _(act):
            act_setup(act)
            act_hi(act, 0, 0, 0, DT)
            act_ffn(act, N_FFN00, 0, 0, None)
            if stop > 1:
                act_s5(act)
                act_glu(act, N_GLU, 1)
            if stop > 2:
                act_ffn(act, N_FFN01, 1, 2, True)
            if stop > 3:
                act_rope(act, N_KV, 0)
                act_v(act, N_KV + NH)
                act_kv_rows(act)
                act.wait_ge(s_kout, 80)
                act_ffn(act, N_FFN10, 2, 3, True)
            if stop > 4:
                act_rope(act, N_Q, NH)
                act_attn(act)
                act_out(act, N_O, DT, 4)
                act_ln(act, 4, True)
            if stop > 5:
                act_ffn(act, N_FFN11, 3, 5, None)
                act_y(act)

        @block.vector
        def _(dve):
            dve_setup(dve)
            dve_lo(dve, 0, 0, 0, DT)
            dve_ffn(dve, N_FFN00, 0, 0)
            if stop > 1:
                dve_s5(dve)
                dve_glu(dve, N_GLU, 1)
            if stop > 2:
                dve_ffn(dve, N_FFN01, 1, 2)
            if stop > 3:
                dve_rope(dve, N_KV, 0, kT)
                dve_v(dve, N_KV + NH)
                dve_kv_rows(dve)
                dve_ffn(dve, N_FFN10, 2, 3)
            if stop > 4:
                dve_rope(dve, N_Q, NH, qT)
                dve_attn(dve)
                dve_out(dve, N_O, DT, ALPHA, 4)
                dve_ln(dve, 4)
            if stop > 5:
                dve_ffn(dve, N_FFN11, 3, 5)

        @block.gpsimd
        def _(pool):
            pool_setup(pool)
            pool_ffn(pool, N_FFN00, 0, 0, None)
            if stop > 1:
                pool_s5(pool)
                pool_ln(pool, 1, lambda d: (glu_z, d + 1), X_LN1)
            if stop > 2:
                pool_ffn(pool, N_FFN01, 1, 2, X_LN2)
            if stop > 3:
                pool_ffn(pool, N_FFN10, 2, 3, X_LN3)
            if stop > 4:
                pool_attn(pool)
                pool_attn_out(pool)
                pool_ln(pool, 4, lambda d: (drained[d % 2], (N_O + d) // 2 + 1), X_LN4)
            if stop > 5:
                pool_ffn(pool, N_FFN11, 3, 5, None)

        @block.tensor
        def _(pe):
            pe_setup(pe)
            pe_ffn(pe, N_FFN00, 0, X_IN, 0)
            if stop > 1:
                pe_s5(pe)
                pe_stage(pe, N_GLU, DT, DT, xh, xl, x_ready, X_GELU, hooks={1: lambda e: (pe_centre(e, 1), pe_stats(e, 1))})
            if stop > 2:
                pe_ffn(pe, N_FFN01, 1, X_LN1, 2)
            if stop > 3:
                pe_stage(pe, N_KV, DT, DT, xh, xl, x_ready, X_LN2)
                pe_kv_rows(pe)
                pe_ffn(pe, N_FFN10, 2, X_LN2, 3)
            if stop > 4:
                pe_stage(pe, N_Q, DT // 2, DT, xh, xl, x_ready, X_LN3)
                pe_attn(pe)
                pe_stage(pe, N_O, DT // 2, DT, xh, xl, x_ready, X_ATT,
                         hooks={0: lambda e: pe_centre(e, 4), 1: lambda e: pe_stats(e, 4)})
            if stop > 5:
                pe_ffn(pe, N_FFN11, 3, X_LN4, 5)
                pe_y(pe)


def rope_tables():
    half = HD // 2
    inv = (10000.0 ** (-np.arange(half) / half)).astype(np.float32)
    pos = np.concatenate([np.arange(SEQ), PAST + np.arange(DEC)]).astype(np.float32)
    ang = (inv[:, None] * pos[None, :]).astype(np.float32)
    c, s = np.cos(ang).astype(np.float32), np.sin(ang).astype(np.float32)
    return {"rope_cos": np.concatenate([c, c, c, c]), "rope_sin": np.concatenate([-s, s, -s, s])}


_INS = ["x_prompt", "x_sample", "cache_k", "cache_v", "state_ssm_re", "state_ssm_im", "ln_g", "ln_b",
        "ffn_w_in", "ffn_w_out", "ssm_a_re", "ssm_a_im", "ssm_log_dt", "ssm_b_re", "ssm_b_im",
        "ssm_c_re", "ssm_c_im", "ssm_d", "ssm_w_glu", "attn_w_q", "attn_w_kv", "attn_lam",
        "attn_subln_g", "attn_w_o"]
_OUTS = [(1, SEQ, D), (1, DEC, D), (1, 1, GROUPS, PS), (1, 1, GROUPS, PS), (1, SEQ, NH, 2, HD),
         (1, SEQ, NH, 2 * HD), (1, 1, GROUPS, PS), (1, 1, GROUPS, PS), (1, DEC, NH, 2, HD),
         (1, DEC, NH, 2 * HD)]


def kernel(**inputs):
    import numpy as _np
    import concourse.bacc as _bacc
    from concourse import mybir as _mybir
    from concourse.bass_utils import run_bass_kernel_spmd as _run

    nc = _bacc.Bacc("TRN2", target_bir_lowering=False, num_devices=1)
    arrays, args = {}, []
    consts = rope_tables()
    for name in _INS + list(consts):
        a = _np.ascontiguousarray(inputs[name] if name in inputs else consts[name])
        arrays[f"in_{name}_dram"] = a
        args.append(nc.dram_tensor(f"in_{name}_dram", a.shape, _mybir.dt.from_np(a.dtype), kind="ExternalInput").ap())
    for i, shape in enumerate(_OUTS):
        args.append(nc.dram_tensor(f"out_{i}_dram", shape, F32, kind="ExternalOutput").ap())
    build(nc, *args)
    r = _run(nc, [arrays], core_ids=[0])
    return tuple(r.results[0][f"out_{i}_dram"] for i in range(len(_OUTS)))
```

```python
import math
from contextlib import ExitStack

import numpy as np

import concourse.bass as bass
from concourse import mybir

F32 = mybir.dt.float32
F32R = mybir.dt.float32r
I32 = mybir.dt.int32
ALU = mybir.AluOpType
ACT = mybir.ActivationFunctionType
AX = mybir.AxisListType

P = 128
D = 1024
DT = D // P
SEQ, DEC, PAST = 512, 64, 1024
T = SEQ + DEC
HALF = T // 2
DEPTH = 2
FF = ((8 * D // 3 + 127) // 128) * 128
FT = FF // P
FH = FT // 2
CHUNK = 64
HD, NH = 64, 8
GROUPS, GC, PS = 64, 16, 64
NPAIR = GROUPS // 2
BLK = 8
NB = T // BLK
NBP = SEQ // BLK
ALPHA = (2 * DEPTH) ** 0.25
LN_EPS = RMS_EPS = 1e-5
SCALE = HD ** -0.5
TT = [(i * P, min(P, T - i * P)) for i in range(5)]
NCEN = 2
NSUB = 4
CENTRED_AT = {3: (0, 1), 4: (2, 3), 5: (4, 5), 6: (6,), 7: (7,)}

FFN_TILES = 2 * (2 * FH + DT)
N_FFN00 = 0
N_GLU = N_FFN00 + FFN_TILES
N_FFN01 = N_GLU + 2 * DT
N_KV = N_FFN01 + FFN_TILES
N_FFN10 = N_KV + 2 * DT
N_Q = N_FFN10 + FFN_TILES
N_O = N_Q + DT
N_FFN11 = N_O + DT
N_TILES = N_FFN11 + FFN_TILES

X_IN, X_GELU, X_LN1, X_LN2, X_LN3, X_ATT, X_LN4 = (8 * i for i in range(7))
TWO_PI_1 = 6.28125
TWO_PI_2 = float(np.float32(2 * math.pi - TWO_PI_1))
TWO_PI_3 = float(2 * math.pi - TWO_PI_1 - TWO_PI_2)
LN2_1 = 0.693359375
LN2_2 = math.log(2) - LN2_1
ROUND = 1.5 * 2.0 ** 23
LAM_INIT = 0.8 - 0.6 * math.exp(-0.3 * 1)


def unit_rows(n):
    for base in (N_FFN00, N_FFN01, N_FFN10, N_FFN11):
        if base <= n < base + FFN_TILES:
            return DT if (n - base) % (2 * FH + DT) < 2 * FH else FH
    return DT


def pairs(eng, count, body, peel_first=False):
    first = 0
    if peel_first:
        body(0)
        first = 1
    if count - 1 - first > 1:
        with eng.Fori(first, count - 1) as i:
            body(i)
    else:
        for i in range(first, count - 1):
            body(i)
    body(count - 1)


def peeled(eng, count, body, peel):
    at = 0
    for stop_ in sorted(peel) + [count]:
        if stop_ - at == 1:
            body(at)
        elif stop_ > at:
            with eng.Fori(at, stop_) as i:
                body(i)
        if stop_ < count:
            body(stop_)
        at = stop_ + 1


def wait(eng, sem, value):
    if isinstance(value, int) and value <= 0:
        return
    eng.wait_ge(sem, value)


def build(nc, x_prompt, x_sample, cache_k, cache_v, state_re, state_im, ln_g, ln_b, w_in, w_out,
          a_re, a_im, log_dt, b_re, b_im, c_re, c_im, ssm_d, w_glu, w_q, w_kv, attn_lam, subln_g,
          w_o, rope_cos, rope_sin,
          y_prompt, y_sample, p_re, p_im, p_k, p_v, s_re, s_im, s_k, s_v, stop=99, dump=None):
    ctx = ExitStack()
    with ctx:
        n_tiles = {1: N_GLU, 2: N_FFN01, 3: N_KV, 4: N_Q, 5: N_FFN11}.get(stop, N_TILES)

        def sem(name):
            return ctx.enter_context(nc.semaphore(name))

        start = (nc.sbuf_base + 31) // 32 * 32
        room = nc.sbuf_usable_end - start - 64
        ctx.enter_context(nc.sbuf_tensor("slab", [P, room], mybir.dt.uint8))

        class Map:

            def __init__(self, at):
                self.at = at

            def __call__(self, name, shape, dt=F32):
                size = 4 * int(np.prod(shape[1:]))
                t = nc.alloc_sbuf_tensor_at(name, shape, dt, offset=self.at)
                self.at += (size + 31) // 32 * 32
                assert self.at <= start + room, (name, self.at - start, room)
                return t

        keep = Map(start)
        r = keep("r", [P, DT, T])
        x_at = keep.at
        xh = keep("xh", [P, DT, T], F32R)
        xl = keep("xl", [P, DT, T], F32R)
        raw = [keep(f"raw{s}", [P, FH, P]) for s in range(2)]
        wh = [keep(f"wh{s}", [P, FH, P], F32R) for s in range(2)]
        wl = [keep(f"wl{s}", [P, FH, P], F32R) for s in range(2)]
        ones = keep("ones", [P, P])
        maskrow = keep("maskrow", [1, P + CHUNK])
        ident = keep("ident", [P, P])
        vec = keep("vec", [P, P])
        small = keep("small", [P, 16])
        cosT = keep("cosT", [P, T])
        sinT = keep("sinT", [P, T])
        cb = keep("cb", [P, T])
        zc = keep("zc", [P, T])
        zq = keep("zq", [P, T])
        sq = [keep(f"sq{s}", [P, T]) for s in range(2)]
        rstd = keep("rstd", [P, T])
        sil = keep("sil", [P, T])
        hf = keep("hf", [P, T])
        h_at = keep.at
        fm = Map(h_at)
        hh = fm("hh", [P, FH, T], F32R)
        hl = fm("hl", [P, FH, T], F32R)
        k_at = fm.at
        km = Map(k_at)
        kT = km("kT", [P, NH, T])
        vtok = km("vtok", [P, 5, D])

        im = Map(h_at)
        xtok = im("xtok", [P, 5, D])
        rows = im("rows", [P, 2, P])
        rows2 = im("rows2", [P, P])
        dtrow = im("dtrow", [NPAIR, 2])
        gm = Map(k_at)
        vs = gm("vs", [P, 5, NPAIR])
        lp = gm("lp", [P, 2, NPAIR, BLK + 1])
        s5_at = gm.at
        lpr = gm("lpr", [P, 2, NPAIR, BLK])
        bbar = gm("bbar", [P, 2, NPAIR, GC])
        cmat = gm("cmat", [P, 3, NPAIR, GC])
        pm = Map(gm.at)
        ebuf = gm("ebuf", [P, 2, 4, BLK, 2, GC])
        cp = gm("cp", [P, 2, 4, BLK + 1, 2, GC])
        wt = gm("wt", [P, 2, 4, 2, P])
        tt = gm("tt", [P, 4, BLK, 32])
        tmp = pm("tmp", [P, 20, NPAIR])
        kint = pm("kint", [P, NPAIR], I32)
        braw = pm("braw", [P, 2, NPAIR, GC])
        craw = pm("craw", [P, 2, DT, 2, PS])
        lamv = pm("lamv", [P, 4, HD])
        prod = [cb, zc]
        prodc = [zq, sq[0], sq[1], rstd]

        am = Map(h_at)
        u4 = am("u4", [P, DT, 4, 2, NB])
        hs = am("hs", [P, 2, NPAIR, NB])
        hlast = am("hlast", [P, 2, NPAIR, 2])
        sm = Map(s5_at)
        wt2 = [sm(f"wt2_{s}", [P, 2, 4, 2, P]) for s in range(2)]
        cp2 = [sm(f"cp2_{s}", [P, 2, 4, BLK, 2, GC]) for s in range(2)]
        tt2 = [sm(f"tt2_{s}", [P, 4, BLK, 32]) for s in range(2)]
        ysb = am("ysb", [P, T])
        gel = am("gel", [P, T])
        sa = am("sa", [P, 2 * 4 * NB // 2])
        sb2 = am("sb2", [P, 2 * 4 * NB // 2])
        lamp = [am(f"lam{BLK << k}", [P, 2, 2, NPAIR]) for k in range(4)]
        strow = am("strow", [NPAIR, 4, P])

        vm = Map(h_at)
        vT = vm("vT", [P, NH, T])
        ktok = [vm(f"ktok{s}", [P, D]) for s in range(2)]

        qm = Map(h_at)
        qT = qm("qT", [P, NH, T])
        otok = qm("otok", [P, 5, D])
        ck = [qm(f"ck{s}", [P, PAST // P, P]) for s in range(2)]
        sts = qm("sts", [P, 2, 16])
        ssq = qm("ssq", [P, 5 * NH])
        nrm = qm("nrm", [P, 2, 5 * NH])
        stz = qm("stz", [P, 2, 8])
        ov = [qm(f"ov{s}", [DEC, P]) for s in range(2)]
        assert qm.at <= k_at
        cm = Map(km.at)
        cv = [cm(f"cv{s}", [P, PAST // P, P]) for s in range(2)]
        xm2 = Map(x_at)
        ex = [xm2(f"ex{s}", [P, 2, SEQ]) for s in range(2)]
        pT = [xm2(f"pT{s}", [P, SEQ]) for s in range(2)]
        qs = [xm2(f"qs{s}", [P, 2, P]) for s in range(2)]
        exS = [xm2(f"exS{s}", [P, PAST + DEC]) for s in range(2)]
        kTc = [xm2(f"kTc{s}", [P, PAST]) for s in range(2)]
        qd = [xm2(f"qd{s}", [P, P]) for s in range(2)]
        sqb = xm2("sqb", [P, D])
        assert xm2.at <= x_at + 2 * 4 * DT * T
        xm3 = Map(x_at)
        pTS = [xm3(f"pTS{s}", [P, (PAST // P + 1) * P]) for s in range(2)]

        ps = ctx.enter_context(nc.psum_tensor("tile_ps", [P, 2, 2, 512], F32))
        misc = ctx.enter_context(nc.psum_tensor("misc", [P, 4, 512], F32))
        mflat = misc[:].rearrange("p b n -> p (b n)")

        scr_w = nc.dram_tensor("scr_w", [DT, P, 2 * 4 * 2 * P], F32).ap()
        scr_c = nc.dram_tensor("scr_c", [DT, P, 2 * 4 * BLK * 32], F32).ap()
        scr_t = nc.dram_tensor("scr_t", [DT, P, 4 * BLK * 32], F32).ap()

        w_loaded = [sem(f"w_loaded{s}") for s in range(2)]
        w_hi = sem("w_hi")
        w_lo = sem("w_lo")
        tile_done = sem("tile_done")
        drained = [sem(f"drained{s}") for s in range(2)]
        hh_ready = sem("hh_ready")
        hl_ready = sem("hl_ready")
        xh_ready = sem("xh_ready")
        x_ready = sem("x_ready")
        ln_sum1 = sem("ln_sum1")
        ln_centre_mm = sem("ln_centre_mm")
        ln_centre = sem("ln_centre")
        ln_centred = sem("ln_centred")
        ln_sq = sem("ln_sq")
        ln_sumc = sem("ln_sumc")
        ln_sumq = sem("ln_sumq")
        ln_mm1 = sem("ln_mm1")
        ln_mm = sem("ln_mm")
        ln_scaled_a, ln_out_a, xh_ready_a, x_ready_a = (sem(k) for k in (
            "ln_scaled_a", "ln_out_a", "xh_ready_a", "x_ready_a"))
        ln_sub = sem("ln_sub")
        ln_dsub = sem("ln_dsub")
        ln_mean = sem("ln_mean")
        ln_var = sem("ln_var")
        ln_sd = sem("ln_sd")
        ln_scaled = sem("ln_scaled")
        ln_out = sem("ln_out")
        step = sem("step")
        s_x = sem("x_loaded")
        s_small = sem("small_loaded")
        s_const = sem("const_ready")
        s_tp = sem("setup_transposed")
        s_tpc = sem("setup_copied")
        s_r = sem("r_loaded")

        w_in_v = w_in.rearrange("l s (k p) c -> l s p k c", p=P)
        w_out_v = w_out.rearrange("l s (k p) c -> l s p k c", p=P)
        glu_v = w_glu.rearrange("a (k p) c -> (a p) k c", p=P)
        kv_v = w_kv.rearrange("(k p) c -> p k c", p=P)
        q_v = w_q.rearrange("a (k p) c -> (a p) k c", p=P)
        o_v = w_o.rearrange("a (k p) c -> (a p) k c", p=P)

        steps = [0]

        def link(eng, ins):
            steps[0] += 1
            ins.then_inc(step, 1)
            eng.wait_ge(step, steps[0])

        def tile(base, i, odd):
            return 2 * i + (base + odd), i + base // 2, odd

        def sp_stage(sp, base, count, view, a, b, k, between=None):
            def body(i):
                n = tile(base, i, 0)[0]
                wait(sp, w_lo, n)
                for s, col in enumerate((a, b)):
                    sp.dma_start(raw[s][:, 0:k, :], view[:, :, bass.ds(col(i), P)]).then_inc(w_loaded[s], 16)
                if between is not None and isinstance(i, int) and i == 0:
                    between(sp)
            pairs(sp, count, body, peel_first=base == 0 or between is not None)

        def sp_ffn(sp, base, l, s, between=None):
            for p in range(2):
                f0 = p * FH
                sp_stage(sp, base, FH,
                         w_in_v[l, s], lambda i: (i + f0) * P, lambda i: (i + (f0 + FT)) * P, DT,
                         between=None if p else between)
                base += 2 * FH
                sp_stage(sp, base, DT // 2,
                         w_out_v[l, s][:, f0:f0 + FH], lambda i: i * 2 * P, lambda i: i * 2 * P + P, FH)
                base += DT

        def sp_plain(sp, base, count, view, between=None):
            sp_stage(sp, base, count, view, lambda i: i * 2 * P, lambda i: i * 2 * P + P, DT, between=between)

        def act_hi(act, n, turn, s, k):
            act.wait_ge(w_loaded[s], 16 * turn + 16)
            wait(act, tile_done, n - 1)
            nc.scalar.copy(wh[s][:, 0:k, :], raw[s][:, 0:k, :]).then_inc(w_hi, 1)

        def dve_lo(dve, n, turn, s, k):
            wait(dve, w_hi, n + 1)
            nc.vector.tensor_tensor(wl[s][:, 0:k, :], raw[s][:, 0:k, :],
                                    wh[s][:, 0:k, :].bitcast(F32), ALU.subtract).then_inc(w_lo, 1)

        behind = {ln_: b for ln_, b in {1: N_FFN01, 2: N_KV, 3: N_Q, 4: N_FFN11}.items() if b < n_tiles}

        def ahead(split, eng, base, i, count, k, which):
            if isinstance(i, int) and (i, which) == (0, 0) and base in behind.values():
                return
            n, turn, s = tile(base, i, which + 1) if which == 0 else tile(base + 2, i, 0)
            if which == 1 and isinstance(i, int) and i == count - 1:
                if base + 2 * count >= n_tiles:
                    return
                k = unit_rows(base + 2 * count)
            split(eng, n, turn, s, k)

        def pe_tile(pe, n, turn, s, k, hi, lo, ready, have):
            wait(pe, w_lo, n + 1)
            if not (isinstance(turn, int) and turn == 0):
                pe.wait_ge(drained[s], turn)
            for kk in range(k):
                if ready is not None:
                    pe.wait_ge(ready, have + kk + 1)
                for hf_ in range(2):
                    cols = slice(hf_ * HALF, (hf_ + 1) * HALF)
                    o = ps[:, s, hf_, 0:HALF]
                    nc.tensor.matmul(o, wh[s][:, kk, :], hi[:, kk, cols], start=kk == 0, stop=False)
                    nc.tensor.matmul(o, wh[s][:, kk, :], lo[:, kk, cols], start=False, stop=False)
                    last = nc.tensor.matmul(o, wl[s][:, kk, :], hi[:, kk, cols], start=False,
                                            stop=kk == k - 1)
            last.then_inc(tile_done, 1)

        def pe_pair_by_halves(pe, base, have):
            e = [ln_ for ln_, b in behind.items() if b == base][0]
            for half in range(2):
                cols = slice(half * HALF, (half + 1) * HALF)
                for s in range(2):
                    n, turn, _ = tile(base, 0, s)
                    if half == 0:
                        pe.wait_ge(w_lo, n + 1)
                        pe.wait_ge(drained[s], turn)
                    o = ps[:, s, half, 0:HALF]
                    for kk in range(DT):
                        if s == 0 and half == 0:
                            pe.wait_ge(x_ready_a, DT * ln_halves(e) + kk + 1)
                        elif s == 0:
                            pe.wait_ge(x_ready, have + kk + 1)
                        nc.tensor.matmul(o, wh[s][:, kk, :], xh[:, kk, cols], start=kk == 0, stop=False)
                        nc.tensor.matmul(o, wh[s][:, kk, :], xl[:, kk, cols], start=False, stop=False)
                        last = nc.tensor.matmul(o, wl[s][:, kk, :], xh[:, kk, cols], start=False, stop=kk == DT - 1)
                    if half:
                        last.then_inc(tile_done, 1)

        def pe_stage(pe, base, count, k, hi, lo, ready, have, hooks={}, tables=False):
            def body(i):
                if isinstance(i, int) and i == 0 and base in behind.values():
                    pe_pair_by_halves(pe, base, have)
                    return
                for odd in range(2):
                    if odd:
                        dt = tables_of(0, tables, i, 1)
                        if dt is not None:
                            pe_tables(pe, dt)
                    pe_tile(pe, *tile(base, i, odd), k, hi, lo, ready, have)
                    if isinstance(i, int) and (i, odd) in hooks:
                        hooks[i, odd](pe)
            peeled(pe, count, body, beside(0, 1, "pe") if tables
                   else sorted({count - 1} | {i for i, _ in hooks}
                               | ({0} if base == 0 or base in behind.values() else set())))

        def ln_hooks(ln, units):
            centre = (NCEN, 1) if units == 2 else (NCEN // 2, NCEN % 2)
            last = (DT - 1, 1) if units == 2 else (DT // 2 - 1, 1)
            return {centre: lambda e: pe_centre(e, ln), last: lambda e: pe_stats(e, ln)}

        def pe_ffn(pe, base, ffn, have, ln):
            for p in range(2):
                pe_stage(pe, base, FH, DT, xh, xl, x_ready, have, tables=ffn == 0 and p == 1)
                base += 2 * FH
                pe_stage(pe, base, DT // 2, FH, hh, hl, hl_ready, (2 * ffn + p) * FH,
                         hooks=ln_hooks(ln, 1) if p else {})
                base += DT

        halves = [slice(0, HALF), slice(HALF, T)]

        def pe_centre(pe, ln):
            pe.wait_ge(ln_sum1, NCEN * (ln + 1))
            for q in range(2):
                mm = nc.tensor.matmul(misc[:, q, 0:HALF], ones[:], zc[:, halves[q]], start=True, stop=True)
            mm.then_inc(ln_centre_mm, 1)

        def pe_stats(pe, ln):
            def add(bank, src, ready, count, first):
                pe.wait_ge(ready, count)
                for q in range(2):
                    mm = nc.tensor.matmul(misc[:, bank + q, 0:HALF], ones[:], src[:, halves[q]],
                                          start=first, stop=not first)
                return mm
            add(0, zc, ln_sumc, (DT - 1) * (ln + 1), True)
            add(2, zq, ln_sumq, (DT - 1) * (ln + 1), True)
            add(0, r[:, DT - 1], ln_centred, DT * (ln + 1), False).then_inc(ln_mm1, 1)
            add(2, sq[(DT - 1) % 2], ln_sq, DT * (ln + 1), False).then_inc(ln_mm, 1)

        def two(t):
            return t[:, :].rearrange("p (h n) -> p h n", h=2)

        def z_ready(eng, d, z):
            eng.wait_ge(*z(d))

        def pool_ln(pool, ln, z, split):
            for d in range(NCEN):
                z_ready(pool, d, z)
                if d == 0:
                    if ln:
                        pool.wait_ge(ln_scaled, DT * ln)
                    nc.gpsimd.tensor_copy(zc[:, :], r[:, 0, :]).then_inc(ln_sum1, 1)
                else:
                    pool.wait_ge(ln_sum1, NCEN * ln + d)
                    nc.gpsimd.tensor_tensor(zc[:, :], zc[:, :], r[:, d, :], ALU.add).then_inc(ln_sum1, 1)
            for d in range(DT - 1):
                pool.wait_ge(ln_sq, DT * ln + d + 1)
                if d == 0:
                    nc.gpsimd.tensor_copy(zq[:, :], sq[0][:, :]).then_inc(ln_sumq, 1)
                else:
                    pool.wait_ge(ln_sumq, (DT - 1) * ln + d)
                    nc.gpsimd.tensor_tensor(zq[:, :], zq[:, :], sq[d % 2][:, :], ALU.add).then_inc(ln_sumq, 1)
            pool.wait_ge(ln_mean, ln + 1)
            for d in range(NSUB):
                nc.gpsimd.tensor_tensor(r[:, d, :], r[:, d, :], cb[:, :], ALU.subtract).then_inc(ln_sub, 1)
            if split is not None:
                for q in range(2):
                    h = halves[q]
                    for d in range(DT):
                        if q:
                            pool.wait_ge(xh_ready, split + d + 1)
                        else:
                            pool.wait_ge(xh_ready_a, DT * ln_halves(ln) + d + 1)
                        nc.gpsimd.tensor_tensor(xl[:, d, h], r[:, d, h], xh[:, d, h].bitcast(F32),
                                                ALU.subtract).then_inc((x_ready_a, x_ready)[q], 1)

        def pool_lo(pool, have):
            for d in range(DT):
                pool.wait_ge(xh_ready, have + d + 1)
                nc.gpsimd.tensor_tensor(xl[:, d, :], r[:, d, :], xh[:, d, :].bitcast(F32),
                                        ALU.subtract).then_inc(x_ready, 1)

        def dve_centre(dve, ln, d):
            if d == 0:
                dve.wait_ge(ln_centre, ln + 1)
            nc.vector.tensor_tensor(r[:, d, :], r[:, d, :], cb[:, :], ALU.subtract).then_inc(ln_centred, 1)
            dve.wait_ge(ln_centred, DT * ln + d + 1)
            if d == 0:
                nc.vector.tensor_copy(zc[:, :], r[:, 0, :]).then_inc(ln_sumc, 1)
            elif d < DT - 1:
                dve.wait_ge(ln_sumc, (DT - 1) * ln + d)
                nc.vector.tensor_tensor(zc[:, :], zc[:, :], r[:, d, :], ALU.add).then_inc(ln_sumc, 1)

        def ln_halves(ln):
            return max(0, ln - 1)

        def dve_ln(dve, ln):
            own = DT - NSUB

            def sub(d):
                nc.vector.tensor_tensor(r[:, d, :], r[:, d, :], cb[:, :], ALU.subtract).then_inc(ln_dsub, 1)

            def affine(d):
                dve.wait_ge(ln_scaled, DT * ln + d + 1)
                col, h = ln * DT + d, halves[1]
                nc.vector.tensor_scalar(r[:, d, h], r[:, d, h], vec[:, col:col + 1], vec[:, 48 + col:49 + col],
                                        ALU.mult, ALU.add).then_inc(ln_out, 1)

            if ln in behind:
                dve.wait_ge(ln_mm1, ln + 1)
                for q in range(2):
                    mean = nc.vector.tensor_scalar(cb[:, halves[q]], misc[:, q, 0:HALF], 1.0 / D, None, ALU.mult)
                mean.then_inc(ln_mean, 1)
                dve.wait_ge(ln_mean, ln + 1)
                link(dve, nc.vector.tensor_tensor(sq[0][:, :], cb[:, :], cb[:, :], ALU.mult))
                dve.wait_ge(ln_mm, ln + 1)
                for q in range(2):
                    h = halves[q]
                    nc.vector.scalar_tensor_tensor(out=sq[0][:, h], in0=misc[:, 2 + q, 0:HALF], scalar=1.0 / D,
                                                   in1=sq[0][:, h], op0=ALU.mult, op1=ALU.subtract).then_inc(ln_var, 1)
                sub(NSUB)
                for q in range(2):
                    h = halves[q]
                    if q == 0:
                        dve.wait_ge(ln_sd, ln + ln_halves(ln) + 1)
                        link(dve, nc.vector.reciprocal(rstd[:, h], sq[1][:, h]))
                    for d in range(DT):
                        if q == 0:
                            if d < NSUB:
                                dve.wait_ge(ln_sub, NSUB * ln + d + 1)
                            else:
                                if d > NSUB:
                                    sub(d)
                                dve.wait_ge(ln_dsub, own * ln + d - NSUB + 1)
                        nc.vector.tensor_tensor(r[:, d, h], r[:, d, h], rstd[:, h],
                                                ALU.mult).then_inc((ln_scaled_a, ln_scaled)[q], 1)
                        if q and d:
                            affine(d - 1)
                        if q == 0 and d == 5:
                            dve_lo(dve, *tile(behind[ln], 0, 1), DT)
                        if q == 0 and d == DT - 1:
                            dve.wait_ge(ln_sd, ln + ln_halves(ln) + 2)
                            link(dve, nc.vector.reciprocal(rstd[:, halves[1]], sq[1][:, halves[1]]))
                affine(DT - 1)
                return
            dve.wait_ge(ln_mm1, ln + 1)
            nc.vector.tensor_scalar(two(cb), misc[:, 0:2, 0:HALF], 1.0 / D, None, ALU.mult).then_inc(ln_mean, 1)
            dve.wait_ge(ln_mean, ln + 1)
            link(dve, nc.vector.tensor_tensor(sq[0][:, :], cb[:, :], cb[:, :], ALU.mult))
            dve.wait_ge(ln_mm, ln + 1)
            nc.vector.scalar_tensor_tensor(out=two(sq[0]), in0=misc[:, 2:4, 0:HALF], scalar=1.0 / D,
                                           in1=two(sq[0]), op0=ALU.mult, op1=ALU.subtract).then_inc(ln_var, 1)
            sub(NSUB)
            dve.wait_ge(ln_sd, ln + ln_halves(ln) + 1)
            link(dve, nc.vector.reciprocal(rstd[:, :], sq[1][:, :]))
            for d in range(DT):
                if d < NSUB:
                    dve.wait_ge(ln_sub, NSUB * ln + d + 1)
                else:
                    if d > NSUB:
                        sub(d)
                    dve.wait_ge(ln_dsub, own * ln + d - NSUB + 1)
                nc.vector.tensor_tensor(r[:, d, :], r[:, d, :], rstd[:, :], ALU.mult).then_inc(ln_scaled, 1)

        def act_centre(act, ln):
            act.wait_ge(ln_centre_mm, ln + 1)
            nc.scalar.activation(two(cb), misc[:, 0:2, 0:HALF], ACT.Copy, scale=1.0 / (NCEN * P)).then_inc(ln_centre, 1)

        def act_square(act, ln, d):
            act.wait_ge(ln_centred, DT * ln + d + 1)
            if d >= 2:
                act.wait_ge(ln_sumq, (DT - 1) * ln + d - 1)
            elif ln:
                act.wait_ge(ln_scaled, DT * ln)
            nc.scalar.activation(sq[d % 2][:, :], r[:, d, :], ACT.Square).then_inc(ln_sq, 1)

        def act_sums(act, ln, d):
            if d == NCEN:
                act_centre(act, ln)
            for c in CENTRED_AT.get(d, ()):
                act_square(act, ln, c)
            if d == DT - 1:
                nc.scalar.activation(small[:, 5:6], small[:, 0:1], ACT.Sqrt)

        def act_ln(act, ln):
            if ln in behind:
                for q in range(2):
                    act.wait_ge(ln_var, ln + ln_halves(ln) + q + 1)
                    nc.scalar.activation(sq[1][:, halves[q]], sq[0][:, halves[q]], ACT.Sqrt,
                                         bias=small[:, 0:1]).then_inc(ln_sd, 1)
                act_hi(act, *tile(behind[ln], 0, 1), DT)
                h, e = halves[0], ln_halves(ln)
                for d in range(DT + 1):
                    if d < DT:
                        act.wait_ge(ln_scaled_a, DT * e + d + 1)
                        col = ln * DT + d
                        nc.scalar.activation(r[:, d, h], r[:, d, h], ACT.Identity, scale=vec[:, col:col + 1],
                                             bias=vec[:, 48 + col:49 + col]).then_inc(ln_out_a, 1)
                    if d:
                        act.wait_ge(ln_out_a, DT * e + d)
                        nc.scalar.copy(xh[:, d - 1, h], r[:, d - 1, h]).then_inc(xh_ready_a, 1)
                h = halves[1]
                for d in range(DT):
                    act.wait_ge(ln_out, DT * ln + d + 1)
                    nc.scalar.copy(xh[:, d, h], r[:, d, h]).then_inc(xh_ready, 1)
                return
            act.wait_ge(ln_var, ln + ln_halves(ln) + 1)
            nc.scalar.activation(sq[1][:, :], sq[0][:, :], ACT.Sqrt, bias=small[:, 0:1]).then_inc(ln_sd, 1)
            for d in range(DT):
                act.wait_ge(ln_scaled, DT * ln + d + 1)
                col = ln * DT + d
                nc.scalar.activation(r[:, d, :], r[:, d, :], ACT.Identity, scale=vec[:, col:col + 1],
                                     bias=vec[:, 48 + col:49 + col]).then_inc(ln_out, 1)

        def act_out(act, base, k, ln):
            def body(i):
                for odd in range(2):
                    ahead(act_hi, act, base, i, DT // 2, k, odd)
                    if ln is not None and isinstance(i, int):
                        act_sums(act, ln, 2 * i + odd)
            peeled(act, DT // 2, body, [DT // 2 - 1] if ln is None else range(NCEN // 2, DT // 2))

        def dve_out(dve, base, k, alpha, ln):
            def body(i):
                for odd in range(2):
                    n, turn, s = tile(base, i, odd)
                    ahead(dve_lo, dve, base, i, DT // 2, k, odd)
                    dve.wait_ge(tile_done, n + 1)
                    rd = r[:, bass.ds(2 * i + odd, 1), :].rearrange("p a (h n) -> p (a h) n", h=2)
                    nc.vector.scalar_tensor_tensor(out=rd, in0=rd, scalar=alpha, in1=ps[:, s, :, 0:HALF],
                                                   op0=ALU.mult, op1=ALU.add).then_inc(drained[s], 1)
                    if ln is not None and isinstance(i, int) and 2 * i + odd in CENTRED_AT:
                        dve.wait_ge(drained[s], turn + 1)
                        for d in CENTRED_AT[2 * i + odd]:
                            dve_centre(dve, ln, d)
            peeled(dve, DT // 2, body, [DT // 2 - 1] if ln is None else range(NCEN // 2, DT // 2))

        N_PART = 10
        TRIG_PAIR = 5
        MADE_BY_LOOP = range(2, DT)

        def beside(ffn, p, eng):
            if ffn:
                return [FH - 1] if p else [0, FH - 1]
            if p:
                return [i for i in range(FH) if i not in MADE_BY_LOOP]
            return {"dve": range(FH), "act": [0, TRIG_PAIR, FH - 1]}.get(eng, [0, FH - 1])

        def tables_of(ffn, p, i, lag):
            if ffn or not p or (isinstance(i, int) and not lag <= i < DT + lag):
                return None
            return i - lag

        def act_ffn(act, base, ffn, ln, split):
            for p in range(2):
                def body_in(i, b=base, p=p):
                    n, turn, s = tile(b, i, 0)
                    ahead(act_hi, act, b, i, FH, DT, 0)
                    act.wait_ge(tile_done, n + 1)
                    wait(act, drained[1], turn)
                    nc.scalar.activation(two(sil), ps[:, 0, :, 0:HALF], ACT.Silu).then_inc(drained[0], 1)
                    dt = tables_of(ffn, p, i, 1)
                    if dt is not None:
                        act_input_tables(act, dt)
                    if ffn == 0 and p == 0 and isinstance(i, int) and i == TRIG_PAIR:
                        act_trig(act)
                    ahead(act_hi, act, b, i, FH, DT, 1)
                    if dt is not None:
                        act_toeplitz(act, dt)
                    act.wait_ge(drained[1], turn + 1)
                    nc.scalar.copy(hh[:, bass.ds(i, 1), :], hf[:, :].unsqueeze(1)).then_inc(hh_ready, 1)
                    if dt is not None:
                        act_store_toeplitz(act, dt)
                peeled(act, FH, body_in, beside(ffn, p, "act"))
                base += 2 * FH

                act_out(act, base, FH, ln if p else None)
                base += DT
            act_ln(act, ln)

        def dve_ffn(dve, base, ffn, ln):
            for p in range(2):
                def body_in(i, b=base, p=p, done=(2 * ffn + p) * FH):
                    n, turn, s = tile(b, i, 0)
                    ahead(dve_lo, dve, b, i, FH, DT, 0)
                    if ffn == 0 and p == 0 and isinstance(i, int) and i < N_PART:
                        dve_params(dve, i)
                    dt = tables_of(ffn, p, i, 0)
                    if dt is not None:
                        dve_tables(dve, dt)
                    ahead(dve_lo, dve, b, i, FH, DT, 1)
                    dve.wait_ge(tile_done, n + 2)
                    dve.wait_ge(drained[0], turn + 1)
                    wait(dve, hl_ready, i + done)
                    nc.vector.scalar_tensor_tensor(out=two(hf), in0=two(sil), scalar=0.5,
                                                   in1=ps[:, 1, :, 0:HALF], op0=ALU.mult,
                                                   op1=ALU.mult).then_inc(drained[1], 1)
                peeled(dve, FH, body_in, beside(ffn, p, "dve"))
                base += 2 * FH

                dve_out(dve, base, FH, 1.0 if p else ALPHA, ln if p else None)
                base += DT
            dve_ln(dve, ln)

        def pool_ffn(pool, base, ffn, ln, split):
            for p in range(2):
                def body_in(i, p=p, done=(2 * ffn + p) * FH):
                    dt = tables_of(ffn, p, i, 0)
                    if dt is not None:
                        pool_tables(pool, dt)
                    pool.wait_ge(hh_ready, i + (done + 1))
                    nc.gpsimd.tensor_tensor(hl[:, bass.ds(i, 1), :], hf[:, :].unsqueeze(1),
                                            hh[:, bass.ds(i, 1), :].bitcast(F32),
                                            ALU.subtract).then_inc(hl_ready, 1)
                peeled(pool, FH, body_in, beside(ffn, p, "pool"))
            first = base + 2 * (2 * FH) + DT
            pool_ln(pool, ln, lambda d: (drained[d % 2], (first + d) // 2 + 1), split)

        def sp_setup(sp):
            for i in range(4):
                sp.dma_start(xtok[:, i, :], x_prompt[0, i * P:(i + 1) * P, :]).then_inc(s_x, 16)
            sp.dma_start(xtok[0:DEC, 4, :], x_sample[0]).then_inc(s_x, 16)
            loads = [
                (rows[0:48, 0, :], ln_g.rearrange("l s (d p) -> (l s d) p", p=P)),
                (rows[48:96, 0, :], ln_b.rearrange("l s (d p) -> (l s d) p", p=P)),
                (rows[96:104, 0, :], ssm_d.rearrange("a (d p) -> (a d) p", p=P)),
                (rows[104:105, 0, :], subln_g),
                (rows[0:32, 1, :], a_re[0].rearrange("(a b) p -> a (b p)", b=2)),
                (rows[32:64, 1, :], a_im[0].rearrange("(a b) p -> a (b p)", b=2)),
                (rows[96:128, 1, :], state_re[0, 0].rearrange("(a b) p -> a (b p)", b=2)),
                (rows2[0:32, :], state_im[0, 0].rearrange("(a b) p -> a (b p)", b=2)),
                (dtrow[:, :], log_dt[0].rearrange("(a b) -> a b", b=2)),
                (cosT[:, :], rope_cos), (sinT[:, :], rope_sin),
                (braw[:, 0], b_re[0].rearrange("(a b) p c -> (b p) a c", b=2)),
                (braw[:, 1], b_im[0].rearrange("(a b) p c -> (b p) a c", b=2)),
            ]
            for ri, c in enumerate((c_re, c_im)):
                cv = c[0].rearrange("(d g) c p -> (g c) d p", d=DT)
                for dup in range(2):
                    loads.append((craw[:, ri, :, dup, :], cv))
            sp.wait_ge(s_pad, 1)
            loads.append((lamv[:].rearrange("p a b -> p (a b)"),
                          attn_lam.rearrange("a b c -> a (b c)").broadcast_to([P, 4 * HD])))
            for dst, src in loads:
                sp.dma_start(dst, src).then_inc(s_small, 16)
            assert 16 * len(loads) == N_SMALL
        N_SMALL = 16 * 18

        def pool_setup(pool):
            nc.gpsimd.memset(ident[:, :], 0.0).then_inc(s_const, 1)
            pool.wait_ge(s_const, 1)
            nc.gpsimd.affine_select(out=ident[:, :], in_=ident[:, :], compare_op=ALU.not_equal, fill=1.0,
                                    base=0, pattern=[[-1, P]], channel_multiplier=1).then_inc(s_const, 1)
            pool_lo(pool, X_IN)

        def pe_setup(pe):
            pe.wait_ge(s_const, 2)
            pe.wait_ge(s_x, 80)
            for d in range(DT):
                if d >= 2:
                    pe.wait_ge(s_r, d - 1)
                for i, (t0, n) in enumerate(TT):
                    mm = nc.tensor.transpose(mflat[:, (d % 2) * 1024 + t0:(d % 2) * 1024 + t0 + n],
                                             xtok[0:n, i, d * P:(d + 1) * P], ident[0:n, 0:n])
                mm.then_inc(s_tp, 1)
            pe.wait_ge(s_small, N_SMALL)
            pe.wait_ge(s_r, DT)
            pe.wait_ge(s_tpc, 1)
            nc.tensor.transpose(mflat[:, 0:P], rows[:, 0, :], ident[:])
            nc.tensor.transpose(mflat[:, P:2 * P], rows[:, 1, :], ident[:])
            nc.tensor.transpose(mflat[:, 2 * P:2 * P + 32], rows2[0:32, :], ident[0:32, 0:32]).then_inc(s_tp, 1)
            for ri in range(2):
                for d in range(DT):
                    mm = nc.tensor.transpose(mflat[:, 1024 + d * P :1024 + (d + 1) * P],
                                             craw[:, ri, d].rearrange("p a b -> p (a b)"), ident[:])
                mm.then_inc(s_tp, 1)
                if ri == 0:
                    pe.wait_ge(s_cm, 2)

        s_cm = sem("c_copied")

        def act_setup(act):
            for d in range(DT):
                act.wait_ge(s_r, d + 1)
                nc.scalar.copy(xh[:, d, :], r[:, d, :]).then_inc(xh_ready, 1)

        def act_trig(act):
            act.wait_ge(s_ang, 1)
            nc.scalar.activation(tmp[:, 8, :], tmp[:, 6, :], ACT.Sin).then_inc(s_trig, 1)
            nc.scalar.activation(tmp[:, 9, :], tmp[:, 7, :], ACT.Sin).then_inc(s_trig, 1)

        s_ang = sem("angles_ready")
        s_trig = sem("trig_ready")
        s_params = sem("s5_params_ready")

        def v_exp(dve, out, x_, a, b, c, kint=kint[:, :]):
            V = nc.vector
            link(dve, V.tensor_scalar(c, x_, -87.0, 88.0, ALU.max, ALU.min))
            link(dve, V.tensor_scalar(a, c, 1.0 / math.log(2), ROUND, ALU.mult, ALU.add))
            link(dve, V.tensor_scalar(a, a, ROUND, None, ALU.subtract))
            link(dve, V.scalar_tensor_tensor(out=b, in0=a, scalar=-LN2_1, in1=c, op0=ALU.mult, op1=ALU.add))
            link(dve, V.scalar_tensor_tensor(out=b, in0=a, scalar=-LN2_2, in1=b, op0=ALU.mult, op1=ALU.add))
            link(dve, V.tensor_scalar(kint, a, 127.0, 2.0 ** 23, ALU.add, ALU.mult))
            co = [1.0 / math.factorial(i) for i in range(9)]
            link(dve, V.tensor_scalar(c, b, co[8], None, ALU.mult))
            for i in range(7, 0, -1):
                link(dve, V.scalar_tensor_tensor(out=c, in0=c, scalar=co[i], in1=b, op0=ALU.add, op1=ALU.mult))
            link(dve, V.scalar_tensor_tensor(out=out, in0=c, scalar=1.0, in1=kint.bitcast(F32), op0=ALU.add, op1=ALU.mult))

        def v_cmul(dve, orr, oi, ar, ai, br, bi, t0, t1):
            V = nc.vector
            link(dve, V.tensor_tensor(t0, ar, br, ALU.mult))
            link(dve, V.tensor_tensor(t1, ai, bi, ALU.mult))
            link(dve, V.tensor_tensor(orr, t0, t1, ALU.subtract))
            link(dve, V.tensor_tensor(t0, ar, bi, ALU.mult))
            link(dve, V.tensor_tensor(t1, ai, br, ALU.mult))
            link(dve, V.tensor_tensor(oi, t0, t1, ALU.add))

        def dve_setup(dve):
            V = nc.vector
            V.memset(ones[:, :], 1.0)
            V.memset(small[:, :], LN_EPS)
            V.memset(rows[96:128, 0, :], 0.0).then_inc(s_pad, 1)
            dve.wait_ge(s_pad, 1)
            for d in range(DT):
                dve.wait_ge(s_tp, d + 1)
                nc.vector.tensor_copy(r[:, d, :], mflat[:, (d % 2) * 1024:(d % 2) * 1024 + T]).then_inc(s_r, 1)
            dve.wait_ge(s_small, N_SMALL)
            V.tensor_copy(rows[64:96, 1, :].rearrange("a (b p) -> a b p", b=2),
                          dtrow[:, :].unsqueeze(2).broadcast_to([NPAIR, 2, PS])).then_inc(s_tpc, 1)
            dve.wait_ge(s_tp, DT + 1)
            link(dve, V.tensor_copy(vec[:, :], mflat[:, 0:P]))
            link(dve, V.tensor_copy(vs[:].rearrange("p a b -> p (a b)"), mflat[:, P:P + 160]))
            link(dve, V.tensor_scalar(small[:, 3:4], vec[:, 104:105], 1.0 - LAM_INIT, None, ALU.mult))
            for ri in range(2):
                dve.wait_ge(s_tp, DT + 2 + ri)
                src = mflat[:, 1024:2048].rearrange("p (a g c) -> p a g c", g=2, c=GC)
                for g in range(2):
                    V.tensor_copy(cmat[64 * g:64 * g + 64, ri], src[64 * g:64 * g + 64, :, g, :]).then_inc(s_cm, 1)
            dve.wait_ge(s_cm, 4)
            link(dve, V.tensor_scalar(cmat[:, 2], cmat[:, 1], -1.0, None, ALU.mult))
            link(dve, V.memset(maskrow[:, 0:CHUNK], 1.0))
            link(dve, V.memset(maskrow[:, CHUNK:P], 0.0))
            V.memset(maskrow[:, P:P + CHUNK], -1e30).then_inc(s_pad, 1)

        def dve_params(dve, part):
            V = nc.vector
            X = [tmp[:, i, :] for i in range(20)]
            lr, li = X[0], vs[:, 1, :]
            lbr, lbi = lp[:, 0, :, 1], lp[:, 1, :, 1]
            if part == 0:
                for k in range(2):
                    link(dve, V.tensor_tensor(lamv[:, 2 * k], lamv[:, 2 * k], lamv[:, 2 * k + 1], ALU.mult))
                    link(dve, V.reduce_sum(X[15][:, k:k + 1], lamv[:, 2 * k], axis=AX.X))
                v_exp(dve, X[16][:, 0:2], X[15][:, 0:2], X[17][:, 0:2], X[18][:, 0:2], X[19][:, 0:2], kint[:, 0:2])
                link(dve, V.tensor_tensor(small[:, 1:2], X[16][:, 1:2], X[16][:, 0:1], ALU.subtract))
                link(dve, V.tensor_scalar(small[:, 1:2], small[:, 1:2], -LAM_INIT, None, ALU.add))
                link(dve, V.memset(small[0:DEC, 4:5], 1.0))
                link(dve, V.tensor_copy(small[DEC:P, 4:5], small[DEC:P, 1:2]))
            elif part == 1:
                link(dve, V.tensor_scalar(lr, vs[:, 0, :], -1e-4, None, ALU.min))
                v_exp(dve, X[1], vs[:, 2, :], X[10], X[11], X[12])
                link(dve, V.tensor_tensor(X[2], lr, X[1], ALU.mult))
            elif part == 2:
                v_exp(dve, X[3], X[2], X[10], X[11], X[12])
            elif part == 3:
                link(dve, V.tensor_tensor(X[4], li, X[1], ALU.mult))
                for out, shift in ((X[6], 0.0), (X[7], 0.25)):
                    link(dve, V.tensor_scalar(X[10], X[4], 1 / (2 * math.pi), shift, ALU.mult, ALU.add))
                    link(dve, V.tensor_scalar(X[10], X[10], ROUND, ROUND, ALU.add, ALU.subtract))
                    for c in (TWO_PI_1, TWO_PI_2, TWO_PI_3):
                        link(dve, V.scalar_tensor_tensor(out=X[11], in0=X[10], scalar=-c,
                                                         in1=X[4] if c == TWO_PI_1 else X[11],
                                                         op0=ALU.mult, op1=ALU.add))
                    link(dve, V.tensor_scalar(X[11], X[11], shift * 2 * math.pi, math.pi, ALU.add, ALU.min))
                    if shift:
                        V.tensor_scalar(out, X[11], -math.pi, None, ALU.max).then_inc(s_ang, 1)
                    else:
                        link(dve, V.tensor_scalar(out, X[11], -math.pi, None, ALU.max))
            elif part == 4:
                link(dve, V.memset(lp[:, 0, :, 0], 1.0))
                link(dve, V.memset(lp[:, 1, :, 0], 0.0))
            elif part == TRIG_PAIR + 1:
                dve.wait_ge(s_trig, 2)
                link(dve, V.tensor_tensor(lbi, X[3], X[8], ALU.mult))
                link(dve, V.tensor_tensor(lbr, X[3], X[9], ALU.mult))
                link(dve, V.tensor_scalar(X[5], lbr, -1.0, None, ALU.add))
                link(dve, V.tensor_tensor(X[10], lr, lr, ALU.mult))
                link(dve, V.tensor_tensor(X[11], li, li, ALU.mult))
                link(dve, V.tensor_tensor(X[10], X[10], X[11], ALU.add))
                link(dve, V.reciprocal(X[12], X[10]))
                link(dve, V.tensor_tensor(X[10], X[5], lr, ALU.mult))
                link(dve, V.tensor_tensor(X[11], lbi, li, ALU.mult))
                link(dve, V.tensor_tensor(X[10], X[10], X[11], ALU.add))
                link(dve, V.tensor_tensor(X[13], X[10], X[12], ALU.mult))
                link(dve, V.tensor_tensor(X[10], lbi, lr, ALU.mult))
                link(dve, V.tensor_tensor(X[11], X[5], li, ALU.mult))
                link(dve, V.tensor_tensor(X[10], X[10], X[11], ALU.subtract))
                link(dve, V.tensor_tensor(X[14], X[10], X[12], ALU.mult))
            elif part == TRIG_PAIR + 2:
                cr = X[13].unsqueeze(2).broadcast_to([P, NPAIR, GC])
                ci = X[14].unsqueeze(2).broadcast_to([P, NPAIR, GC])
                w0, w1 = (t[:, 0:512].rearrange("p (a c) -> p a c", c=GC) for t in prod)
                v_cmul(dve, bbar[:, 0], bbar[:, 1], cr, ci, braw[:, 0], braw[:, 1], w0, w1)
            elif part == TRIG_PAIR + 3:
                for k in (1, 2, 4):
                    w0, w1 = (t[:, 0:NPAIR * k].rearrange("p (a j) -> p a j", j=k) for t in prod)
                    b0, b1 = (lp[:, ri, :, k:k + 1].broadcast_to([P, NPAIR, k]) for ri in range(2))
                    v_cmul(dve, lp[:, 0, :, k + 1:2 * k + 1], lp[:, 1, :, k + 1:2 * k + 1],
                           lp[:, 0, :, 1:k + 1], lp[:, 1, :, 1:k + 1], b0, b1, w0, w1)
            elif part == TRIG_PAIR + 4:
                for j in range(BLK):
                    V.tensor_copy(lpr[:, :, :, j], lp[:, :, :, BLK - 1 - j])
                V.memset(ebuf[:].rearrange("p a b c d e -> p (a b c d e)"), 0.0)
                V.memset(cp[:].rearrange("p a b c d e -> p (a b c d e)"), 0.0)
                V.memset(tt[:].rearrange("p a b c -> p (a b c)"), 0.0).then_inc(s_params, 1)
                dve.wait_ge(s_params, 1)

        s_pad = sem("padded")

        s_e = sem("input_powers")
        s_c = sem("output_powers")
        s_tb = sem("tables_multiplied")
        s_tw = sem("tables_copied")
        s_tdw, s_tdc, s_tdt = (sem(f"table_{k}_stored") for k in "wct")
        s_pv = sem("products")
        s_pp = sem("pool_products")

        def later(dt):
            return not (isinstance(dt, int) and dt == 0)

        def dve_tables(dve, dt):
            V = nc.vector
            br, bi = (bbar[:, ri, bass.ds(4 * dt, 4), :].unsqueeze(2).broadcast_to([P, 4, BLK, GC]) for ri in range(2))
            lr, li = (lpr[:, ri, bass.ds(4 * dt, 4), :].unsqueeze(3).broadcast_to([P, 4, BLK, GC]) for ri in range(2))
            pr = [t[:, 0:4 * BLK * GC].rearrange("p (q j c) -> p q j c", q=4, c=GC) for t in prod]
            for ri, op in ((0, ALU.subtract), (1, ALU.add)):
                if ri:
                    dve.wait_ge(s_e, 4 * dt + 2)
                elif later(dt):
                    dve.wait_ge(s_e, 4 * dt)
                for k, (a, b) in enumerate(((br, lr), (bi, li)) if ri == 0 else ((br, li), (bi, lr))):
                    V.tensor_tensor(pr[k], a, b, ALU.mult).then_inc(s_pv, 1)
                dve.wait_ge(s_pv, 4 * dt + (2 + 2 * ri))
                if ri == 0 and later(dt):
                    dve.wait_ge(s_tb, 3 * dt)
                for g in range(2):
                    h = slice(64 * g, 64 * g + 64)
                    V.tensor_tensor(ebuf[h, ri, :, :, g, :], pr[0][h], pr[1][h], op).then_inc(s_e, 1)

        def pool_tables(pool, dt):
            G = nc.gpsimd
            cr, ci, nci = (cmat[:, k, bass.ds(4 * dt, 4), :].unsqueeze(2).broadcast_to([P, 4, BLK + 1, GC]) for k in range(3))
            lr, li = (lp[:, ri, bass.ds(4 * dt, 4), :].unsqueeze(3).broadcast_to([P, 4, BLK + 1, GC]) for ri in range(2))
            pr = [t[:, :].rearrange("p (q j c) -> p q j c", q=4, c=GC) for t in prodc]
            if later(dt):
                pool.wait_ge(s_c, 4 * dt)
            else:
                pool.wait_ge(s_params, 1)
            for k, (a, b) in enumerate(((cr, lr), (ci, li), (nci, lr), (cr, li))):
                G.tensor_tensor(pr[k], a, b, ALU.mult).then_inc(s_pp, 1)
            pool.wait_ge(s_pp, 4 * dt + 4)
            if later(dt):
                pool.wait_ge(s_tb, 3 * dt)
                pool.wait_ge(s_tdc, 16 * dt)
            for ri in range(2):
                for g in range(2):
                    h = slice(64 * g, 64 * g + 64)
                    G.tensor_tensor(cp[h, ri, :, :, g, :], pr[2 * ri][h], pr[2 * ri + 1][h],
                                    ALU.subtract).then_inc(s_c, 1)
                    pool.wait_ge(s_c, 4 * dt + (2 * ri + g + 1))

        def pe_tables(pe, dt):
            pe.wait_ge(s_e, 4 * dt + 4)
            if later(dt):
                pe.wait_ge(s_tw, 6 * dt)
            for ri in range(2):
                for q in range(4):
                    for jh in range(2):
                        k = ri * 1024 + (q * 2 + jh) * P
                        mm = nc.tensor.transpose(
                            mflat[:, k:k + P],
                            ebuf[:, ri, q, 4 * jh:4 * jh + 4].rearrange("p j g c -> p (j g c)"), ident[:])
                mm.then_inc(s_tb, 1)
            pe.wait_ge(s_c, 4 * dt + 4)
            pe.wait_ge(s_tw, 6 * dt + 1)
            for q in range(4):
                for ri in range(2):
                    mm = nc.tensor.matmul(mflat[0:32, q * 256:(q + 1) * 256],
                                          ebuf[:, ri, q, BLK - 1].rearrange("p g c -> p (g c)"),
                                          cp[:, ri, q, 0:BLK].rearrange("p j g c -> p (j g c)"),
                                          start=ri == 0, stop=ri == 1, skip_group_check=True)
            mm.then_inc(s_tb, 1)

        def table_row(scr, dt):
            return scr[bass.ds(dt, 1)].rearrange("a p n -> (a p) n")

        def act_input_tables(act, dt):
            act.wait_ge(s_c, 4 * dt + 4)
            act.dma_start(table_row(scr_c, dt).rearrange("p (a b n) -> p a b n", a=2, b=4),
                          cp[:, :, :, 1:BLK + 1].rearrange("p a q j g c -> p a q (j g c)")).then_inc(s_tdc, 16)
            if later(dt):
                act.wait_ge(s_tdw, 16 * dt)
            for ri in range(2):
                act.wait_ge(s_tb, 3 * dt + (ri + 1))
                nc.scalar.copy(wt[:, ri].rearrange("p q j s -> p (q j s)"),
                               mflat[:, ri * 1024:(ri + 1) * 1024]).then_inc(s_tw, 1)

        def act_toeplitz(act, dt):
            act.wait_ge(s_tw, 6 * dt + 2)
            act.dma_start(table_row(scr_w, dt), wt[:].rearrange("p a q j s -> p (a q j s)")).then_inc(s_tdw, 16)
            act.wait_ge(s_tb, 3 * dt + 3)
            if later(dt):
                act.wait_ge(s_tdt, 16 * dt)
            src = mflat[0:32, 0:1024].rearrange("p (q j c) -> p q j c", q=4, c=32)
            for jj in range(4):
                nc.scalar.copy(tt[32 * jj:32 * jj + 32, :, jj:BLK, :], src[:, :, 0:BLK - jj, :]).then_inc(s_tw, 1)

        def act_store_toeplitz(act, dt):
            act.wait_ge(s_tw, 6 * dt + 6)
            act.dma_start(table_row(scr_t, dt), tt[:].rearrange("p q j c -> p (q j c)")).then_inc(s_tdt, 16)

        s_u4d = sem("u4_ready_dve")
        s_u4a = sem("u4_ready_act")
        s_wl = [sem(f"wt2_loaded{s}") for s in range(2)]
        s_bl = [sem(f"cp2_tt2_loaded{s}") for s in range(2)]
        s_wm = sem("block_inputs_multiplied")
        s_wc = sem("block_inputs_copied")
        s_init = sem("states_initial")
        s_sh = sem("block_states")
        s_fin = sem("final_states")
        s_ym = sem("y_multiplied")
        s_yd = sem("y_copied_dve")
        s_ya = sem("y_copied_act")
        s_ys = sem("y_with_skip")
        s_ge = sem("gelu_done")
        s_st = sem("states_transposed")
        s_so = sem("states_copied")
        s_out = sem("stored")

        def sp_s5(sp):
            for s_ in (s_tdw, s_tdc, s_tdt):
                sp.wait_ge(s_, 16 * DT)
            for dt in range(DT):
                s = dt % 2
                if dt >= 2:
                    sp.wait_ge(s_wm, dt - 1)
                sp.dma_start(wt2[s][:].rearrange("p a q j s -> p (a q j s)"), scr_w[dt]).then_inc(s_wl[s], 16)
            for dt in range(DT):
                s = dt % 2
                if dt >= 2:
                    sp.wait_ge(s_ym, dt - 1)
                sp.dma_start(cp2[s][:].rearrange("p a q j g c -> p (a q j g c)"), scr_c[dt]).then_inc(s_bl[s], 16)
                sp.dma_start(tt2[s][:].rearrange("p q j c -> p (q j c)"), scr_t[dt]).then_inc(s_bl[s], 16)

        def u4_copy(eng_copy, done, jj, half):
            ds = slice(half * DT // 2, (half + 1) * DT // 2)
            for q in range(4):
                src = r[32 * q:32 * q + 32, ds, jj::4].rearrange("p d (n j) -> p d j n", j=2)
                eng_copy(u4[32 * jj:32 * jj + 32, ds, q, :, :], src).then_inc(done, 1)

        def dve_s5(dve):
            V = nc.vector

            def advance(prs, left, right, k, done=None, of=hs):
                cur, nxt = hs[:, :, prs, left], of[:, :, prs, right]
                np_, n = cur.shape[2], cur.shape[3]
                t0, t1 = (t[:, 0:2 * np_ * n].rearrange("p (r q n) -> p r q n", r=2, q=np_) for t in (sa, sb2))
                lre = lamp[k][:, 0, :, prs].unsqueeze(3).broadcast_to([P, 2, np_, n])
                V.tensor_tensor(t0, cur, lre, ALU.mult)
                for ri in range(2):
                    lim = lamp[k][:, 1, ri, prs].unsqueeze(2).broadcast_to([P, np_, n])
                    ins = V.tensor_tensor(t1[:, ri], cur[:, 1 - ri], lim, ALU.mult)
                link(dve, ins)
                link(dve, V.tensor_tensor(nxt, nxt, t0, ALU.add))
                if done is None:
                    link(dve, V.tensor_tensor(nxt, nxt, t1, ALU.add))
                else:
                    V.tensor_tensor(nxt, nxt, t1, ALU.add).then_inc(done, 1)

            pre, pim = lp[:, 0, :, BLK], lp[:, 1, :, BLK]
            for k in range(4):
                lk = lamp[k]
                if k:
                    ar, ai = lamp[k - 1][:, 0, 0], lamp[k - 1][:, 1, 1]
                    w0, w1 = sa[:, 0:NPAIR], sb2[:, 0:NPAIR]
                    V.tensor_tensor(w0, ar, ar, ALU.mult)
                    link(dve, V.tensor_tensor(w1, ai, ai, ALU.mult))
                    link(dve, V.tensor_tensor(lk[:, 0, 0], w0, w1, ALU.subtract))
                    link(dve, V.tensor_tensor(w0, ar, ai, ALU.mult))
                    link(dve, V.tensor_tensor(lk[:, 1, 1], w0, w0, ALU.add))
                    link(dve, V.tensor_copy(lk[:, 0, 1], lk[:, 0, 0]))
                else:
                    for half in range(2):
                        V.tensor_copy(lk[:, 0, half], pre)
                    link(dve, V.tensor_copy(lk[:, 1, 1], pim))
                link(dve, V.tensor_scalar(lk[:, 1, 0], lk[:, 1, 1], -1.0, None, ALU.mult))
            V.memset(hs[:, :, :, 0], 0.0)
            for half in range(2):
                dve.wait_ge(ln_out, (half + 1) * DT // 2)
                for jj in (0, 1):
                    u4_copy(V.tensor_copy, s_u4d, jj, half)
            for dt in range(DT):
                dve.wait_ge(s_wm, dt + 1)
                b = dt % 2
                prs = slice(4 * dt, 4 * dt + 4)
                src = mflat[:, b * 1024:(b + 1) * 1024].rearrange("p (r n) -> p r n", r=2)[:, :, 0:4 * NB] \
                    .rearrange("p r (q n) -> p r q n", q=4)
                for ri in range(2):
                    V.tensor_copy(hs[:, ri, prs, 1:NB], src[:, ri, :, 0:NB - 1]).then_inc(s_wc, 1)
                    V.tensor_copy(hlast[:, ri, prs, :], src[:, ri, :, NBP - 1::DEC // BLK]).then_inc(s_wc, 1)
                dve.wait_ge(s_wc, 4 * dt + 4)
                advance(prs, slice(1, NB - 2, 2), slice(2, NB - 1, 2), 0)
                advance(prs, slice(2, NB - 5, 4), slice(4, NB - 3, 4), 1)
                advance(prs, slice(4, NB - 11, 8), slice(8, NB - 7, 8), 2)
            every = slice(0, NPAIR)
            V.tensor_copy(hs[:, :, :, NBP], vs[:, 3:5, :]).then_inc(s_init, 1)
            dve.wait_ge(s_init, 1)
            for m in range(8, NBP - 8, 8):
                advance(every, slice(m, m + 1), slice(m + 8, m + 9), 3)

            def states(dt):
                prs = slice(4 * dt, 4 * dt + 4)
                advance(prs, slice(0, NB - 7, 8), slice(4, NB - 3, 8), 2)
                advance(prs, slice(0, NB - 3, 4), slice(2, NB - 1, 4), 1)
                advance(prs, slice(0, NB - 1, 2), slice(1, NB, 2), 0, done=s_sh)
                dve.wait_ge(s_sh, dt + 1)
            states(0)
            for dt in range(DT):
                if dt + 1 < DT:
                    states(dt + 1)
                else:
                    advance(every, slice(NBP - 1, NB, DEC // BLK), slice(0, 2), 0, done=s_fin, of=hlast)
                b = dt % 2
                dve.wait_ge(s_ym, dt + 1)
                if dt:
                    dve.wait_ge(s_ge, dt)
                src = mflat[:, b * 1024:(b + 1) * 1024].rearrange("p (a n) -> p a n", a=2)[:, :, 0:4 * NB] \
                    .rearrange("p a (q j n) -> p a q j n", q=2, j=2)
                for jj in (0, 1):
                    for q in range(4):
                        dst = ysb[32 * q:32 * q + 32, jj::4].rearrange("p (n j) -> p j n", j=2)
                        V.tensor_copy(dst, src[32 * jj:32 * jj + 32, q // 2, q % 2]).then_inc(s_yd, 1)
                dve.wait_ge(s_yd, 8 * dt + 8)
                dve.wait_ge(s_ya, 8 * dt + 8)
                V.scalar_tensor_tensor(out=ysb[:, :], in0=r[:, dt, :], scalar=vec[:, 96 + dt:97 + dt],
                                       in1=ysb[:, :], op0=ALU.mult, op1=ALU.add).then_inc(s_ys, 1)

        def act_s5(act):
            for half in range(2):
                act.wait_ge(ln_out, (half + 1) * DT // 2)
                for jj in (2, 3):
                    u4_copy(nc.scalar.copy, s_u4a, jj, half)
            for dt in range(DT):
                b = dt % 2
                act.wait_ge(s_ym, dt + 1)
                if dt:
                    act.wait_ge(s_ge, dt)
                src = mflat[:, b * 1024:(b + 1) * 1024].rearrange("p (a n) -> p a n", a=2)[:, :, 0:4 * NB] \
                    .rearrange("p a (q j n) -> p a q j n", q=2, j=2)
                for jj in (2, 3):
                    for q in range(4):
                        dst = ysb[32 * q:32 * q + 32, jj::4].rearrange("p (n j) -> p j n", j=2)
                        nc.scalar.copy(dst, src[32 * jj:32 * jj + 32, q // 2, q % 2]).then_inc(s_ya, 1)
                act.wait_ge(s_ys, dt + 1)
                if dt:
                    act.wait_ge(x_ready, X_GELU + dt)
                nc.scalar.activation(gel[:, :], ysb[:, :], ACT.Gelu_apprx_tanh).then_inc(s_ge, 1)
                act.wait_ge(s_ge, dt + 1)
                nc.scalar.copy(xh[:, dt, :], gel[:, :]).then_inc(xh_ready, 1)
            act.wait_ge(s_st, 4)
            nc.scalar.copy(strow[:].rearrange("p a b -> p (a b)"), mflat[0:NPAIR, 0:512]).then_inc(s_so, 1)

        def pool_s5(pool):
            G = nc.gpsimd
            for d in range(DT):
                pool.wait_ge(xh_ready, X_GELU + d + 1)
                G.tensor_tensor(xl[:, d, :], gel[:, :], xh[:, d, :].bitcast(F32),
                                ALU.subtract).then_inc(x_ready, 1)

        assert am.at <= k_at, (am.at - k_at)

        def pe_s5(pe):
            for dt in range(DT):
                s = dt % 2
                if dt % (DT // 2) == 0:
                    for s_ in (s_u4d, s_u4a):
                        pe.wait_ge(s_, 8 * (2 * dt // DT + 1))
                pe.wait_ge(s_wl[s], 16 * (dt // 2 + 1))
                if dt >= 2:
                    pe.wait_ge(s_wc, 4 * (dt - 1))
                for ri in range(2):
                    for q in range(4):
                        o = misc[:, 2 * s + ri, q * NB:(q + 1) * NB]
                        for jh in range(2):
                            mm = nc.tensor.matmul(o, wt2[s][:, ri, q, jh, :], u4[:, dt, q, jh, :],
                                                  start=jh == 0, stop=jh == 1)
                mm.then_inc(s_wm, 1)
            pe.wait_ge(s_wc, 4 * DT)

            def block_out(dt, q):
                c0 = (q % 2) * 2 * NB
                return misc[:, 2 * (dt % 2) + q // 2, c0:c0 + 2 * NB]

            def within(dt):
                s = dt % 2
                pe.wait_ge(s_bl[s], 32 * (dt // 2 + 1))
                if dt >= 2:
                    pe.wait_ge(s_yd, 8 * (dt - 1))
                    pe.wait_ge(s_ya, 8 * (dt - 1))
                for q in range(4):
                    o = block_out(dt, q)
                    t2 = tt2[s][:, q].rearrange("p j c -> p (j c)")
                    nc.tensor.matmul(o, t2[:, 0:P], u4[:, dt, q].rearrange("p j n -> p (j n)"),
                                     start=q % 2 == 0, stop=False, skip_group_check=True)
                    nc.tensor.matmul(o[:, NB:2 * NB], t2[:, P:2 * P], u4[:, dt, q, 0, :],
                                     start=False, stop=False, skip_group_check=True)
            within(0)
            within(1)
            for dt in range(DT):
                s = dt % 2
                if dt >= 2:
                    within(dt)
                pe.wait_ge(s_sh, dt + 1)
                for q in range(4):
                    o = block_out(dt, q)
                    for jh in range(2):
                        for ri in range(2):
                            v = cp2[s][:, ri, q, 4 * jh:4 * jh + 4].rearrange("p j g c -> p (j g c)")
                            mm = nc.tensor.matmul(o[:, jh * NB:(jh + 1) * NB], v, hs[:, ri, 4 * dt + q, :],
                                                  start=False, stop=ri == 1 and jh == 1, skip_group_check=True)
                mm.then_inc(s_ym, 1)
            pe.wait_ge(s_fin, 1)
            pe.wait_ge(s_yd, 8 * (DT - 1))
            pe.wait_ge(s_ya, 8 * (DT - 1))
            for k in range(4):
                nc.tensor.transpose(misc[0:NPAIR, 0, k * P:(k + 1) * P],
                                    hlast[:, k % 2, :, k // 2], ident[:]).then_inc(s_st, 1)
            pe.wait_ge(s_so, 1)

        def sp_states(sp):
            sp.wait_ge(s_so, 1)
            for k, dst in enumerate((p_re, p_im, s_re, s_im)):
                sp.dma_start(dst[0, 0].rearrange("(a b) p -> a (b p)", b=2), strow[:, k, :]).then_inc(s_out, 16)

        def act_glu(act, base, ln):
            def body(i):
                n, turn, s = tile(base, i, 0)
                ahead(act_hi, act, base, i, DT, DT, 0)
                act.wait_ge(tile_done, n + 1)
                wait(act, drained[1], turn)
                nc.scalar.activation(two(sil), ps[:, 0, :, 0:HALF], ACT.Sigmoid).then_inc(drained[0], 1)
                ahead(act_hi, act, base, i, DT, DT, 1)
                if isinstance(i, int):
                    act_sums(act, ln, i)
            peeled(act, DT, body, range(NCEN, DT))
            act_ln(act, ln)

        glu_z = sem("glu_z")

        def dve_glu(dve, base, ln):
            def body(i):
                n, turn, s = tile(base, i, 0)
                ahead(dve_lo, dve, base, i, DT, DT, 0)
                ahead(dve_lo, dve, base, i, DT, DT, 1)
                dve.wait_ge(tile_done, n + 2)
                dve.wait_ge(drained[0], turn + 1)
                wait(dve, glu_z, i)
                nc.vector.tensor_tensor(two(hf), two(sil), ps[:, 1, :, 0:HALF], ALU.mult).then_inc(drained[1], 1)
                dve.wait_ge(drained[1], turn + 1)
                rd = r[:, bass.ds(i, 1), :].rearrange("p a n -> p (a n)")
                nc.vector.scalar_tensor_tensor(out=rd, in0=rd, scalar=ALPHA, in1=hf[:, :], op0=ALU.mult,
                                               op1=ALU.add).then_inc(glu_z, 1)
                if isinstance(i, int) and i in CENTRED_AT:
                    dve.wait_ge(glu_z, i + 1)
                    for d in CENTRED_AT[i]:
                        dve_centre(dve, ln, d)
            peeled(dve, DT, body, [0] + list(range(NCEN + 1, DT)))
            dve_ln(dve, ln)

        s_swap = sem("halves_swapped")
        s_rot = sem("sine_part")
        s_rope = sem("heads_rotated")
        s_kvt = sem("kv_transposed")
        s_kc = sem("k_rows_copied")
        s_vc = sem("v_rows_copied")
        s_kout = sem("k_stored")

        def act_rope(act, base, done):
            def body(i):
                for odd in range(2):
                    n, turn, s = tile(base, i, odd)
                    if not (isinstance(i, int) and i == 0 and odd):
                        ahead(act_hi, act, base, i, NH // 2, DT, odd)
                    if isinstance(i, int) and i == 0 and not odd:
                        ahead(act_hi, act, base, i, NH // 2, DT, 1)
                    act.wait_ge(tile_done, n + 1)
                    wait(act, s_rope, 2 * i + (done + odd))
                    for a, b in ((0, 32), (32, 0), (64, 96), (96, 64)):
                        nc.scalar.copy(two(sil)[a:a + 32], ps[b:b + 32, s, :, 0:HALF]).then_inc(s_swap, 1)
            pairs(act, NH // 2, body, peel_first=True)

        def dve_rope(dve, base, done, dst):
            def body(i):
                for odd in range(2):
                    n, turn, s = tile(base, i, odd)
                    h = 2 * i + (done + odd)
                    if not (isinstance(i, int) and i == 0 and odd):
                        ahead(dve_lo, dve, base, i, NH // 2, DT, odd)
                    if isinstance(i, int) and i == 0 and not odd:
                        ahead(dve_lo, dve, base, i, NH // 2, DT, 1)
                    dve.wait_ge(s_swap, 8 * i + (4 * (done + odd) + 4))
                    nc.vector.tensor_tensor(two(hf), ps[:, s, :, 0:HALF], two(cosT), ALU.mult).then_inc(drained[s], 1)
                    nc.vector.tensor_tensor(sil[:, :], sil[:, :], sinT[:, :], ALU.mult).then_inc(s_rot, 1)
                    dve.wait_ge(s_rot, h + 1)
                    nc.vector.tensor_tensor(dst[:, bass.ds(2 * i + odd, 1), :].rearrange("p a n -> p (a n)"),
                                            hf[:, :], sil[:, :], ALU.add).then_inc(s_rope, 1)
                    dve.wait_ge(s_rope, h + 1)
            pairs(dve, NH // 2, body, peel_first=True)

        def act_v(act, base):
            def body(i):
                for odd in range(2):
                    n, turn, s = tile(base, i, odd)
                    ahead(act_hi, act, base, i, NH // 2, DT, odd)
                    act.wait_ge(tile_done, n + 1)
                    nc.scalar.copy(vT[:, bass.ds(2 * i + odd, 1), :].rearrange("p a (h n) -> p (a h) n", h=2),
                                   ps[:, s, :, 0:HALF]).then_inc(drained[s], 1)
            pairs(act, NH // 2, body)

        def dve_v(dve, base):
            def body(i):
                for odd in range(2):
                    ahead(dve_lo, dve, base, i, NH // 2, DT, odd)
            pairs(dve, NH // 2, body)

        def pe_kv_rows(pe):
            pe.wait_ge(s_rope, NH)
            for s in range(2):
                pe.wait_ge(drained[s], N_FFN10 // 2)
            for i, (t0, n) in enumerate(TT):
                if i:
                    pe.wait_ge(s_kc, i)
                for h in range(NH):
                    mm = nc.tensor.transpose(mflat[0:n, h * P:(h + 1) * P], kT[:, h, t0:t0 + n], ident[:])
                mm.then_inc(s_kvt, 1)
                if i:
                    pe.wait_ge(s_vc, i)
                for h in range(NH):
                    mm = nc.tensor.transpose(mflat[0:n, 1024 + h * P:1024 + (h + 1) * P], vT[:, h, t0:t0 + n], ident[:])
                mm.then_inc(s_kvt, 1)

        def act_kv_rows(act):
            for i, (t0, n) in enumerate(TT):
                act.wait_ge(s_kvt, 2 * i + 1)
                if i >= 2:
                    act.wait_ge(s_kout, 16 * (i - 1))
                nc.scalar.copy(ktok[i % 2][0:n, :], mflat[0:n, 0:1024]).then_inc(s_kc, 1)

        def dve_kv_rows(dve):
            nc.vector.memset(vtok[DEC:P, 4, :], 0.0)
            for i, (t0, n) in enumerate(TT):
                dve.wait_ge(s_kvt, 2 * i + 2)
                nc.vector.tensor_copy(vtok[0:n, i, :], mflat[0:n, 1024:2048]).then_inc(s_vc, 1)

        def sp_kv_rows(sp):
            for i, (t0, n) in enumerate(TT):
                kd = (p_k[0, t0:t0 + n] if i < 4 else s_k[0]).rearrange("t h m d -> t (h m d)")
                vd = (p_v[0, t0:t0 + n] if i < 4 else s_v[0]).rearrange("t h e -> t (h e)")
                sp.wait_ge(s_kc, i + 1)
                if i:
                    sp.wait_ge(s_kout, 16 * i)
                sp.dma_start(kd, ktok[i % 2][0:n, :]).then_inc(s_kout, 16)
                sp.wait_ge(s_vc, i + 1)
                sp.dma_start(vd, vtok[0:n, i, :]).then_inc(s_out, 16)

        ITEMS = 4 * NH
        s_qs = sem("queries_staged")
        s_sc = sem("scores")
        s_max = sem("maxima")
        s_exp = sem("exponentials")
        s_pr = sem("probabilities")
        s_pt = sem("p_transposed")
        s_ptc = sem("p_copied")
        s_o = sem("pv_done")
        s_oe = sem("o_copied")
        s_zq = sem("qs_cleared")
        v_mx = sem("v_stats")
        z_qs = sem("sample_queries_staged")
        z_kt = sem("cached_k_transposed")
        z_ktc = sem("cached_k_copied")
        z_sc = sem("sample_scores")
        z_own = sem("sample_own_scores")
        z_big = sem("sample_cached_maxima")
        z_st = sem("sample_stats")
        z_max = sem("sample_maxima")
        z_exp = sem("sample_exponentials")
        z_sum = sem("sample_sums")
        z_w = sem("sample_weights")
        z_pt = sem("sample_p_transposed")
        z_ptc = sem("sample_p_copied")
        z_o = sem("sample_pv_done")
        z_ov = sem("sample_second_map")
        z_fin = sem("sample_heads")
        s_sq = sem("squared_outputs")
        s_nq = sem("squared_norms")
        s_ck = [sem(f"cached_k_loaded{s}") for s in range(2)]
        s_cv = [sem(f"cached_v_loaded{s}") for s in range(2)]
        s_on = sem("heads_normalised")
        s_ns = sem("norm_roots")
        s_ox = sem("o_scaled")
        s_ot = sem("o_transposed")

        def item(i, j, k):
            if isinstance(j, int):
                it = 2 * j + 8 * i + k
                return it // NH, it % NH, k % 2, it
            return i, 2 * j + k, k % 2, 2 * j + (8 * i + k)

        def at_end(i, j, k):
            return isinstance(j, int) and 8 * i + 2 * j + k >= ITEMS

        def prompt_pairs(eng, body):
            for i in range(4):
                peeled(eng, NH // 2, lambda j, i=i: body(i, j), [0, NH // 2 - 1] if i == 0 else [NH // 2 - 1])

        def head(t, h, cols):
            return t[:, bass.ds(h, 1), cols].rearrange("p a n -> p (a n)")

        def vhead(i, h, rows_=P):
            return vtok[0:rows_, i, bass.ds(h * P, P)]

        def pool_attn(pool):
            G = nc.gpsimd
            pool.wait_ge(tile_done, N_O)
            for b in range(2):
                G.memset(qs[b][:].rearrange("p a b -> p (a b)"), 0.0).then_inc(s_zq, 1)
                G.memset(qd[b][:, :], 0.0).then_inc(s_zq, 1)
            pool.wait_ge(s_zq, 4)
            pool.wait_ge(s_rope, 2 * NH)

            def body(i, j):
                for k in range(2):
                    _, h, b, it = item(i, j, k)
                    wait(pool, s_sc, it - 1)
                    for m in range(2):
                        G.tensor_copy(qs[b][64 * m:64 * m + 64, m, :],
                                      head(qT, h, slice(i * P, i * P + P))[64 * m:64 * m + 64]).then_inc(s_qs, 1)
            prompt_pairs(pool, body)

            def square(i, n):
                if i == 0:
                    pool.wait_ge(s_oe, ITEMS)
                wait(pool, s_nq, i)
                G.tensor_tensor(sqb[0:n, :], otok[0:n, i, :], otok[0:n, i, :], ALU.mult).then_inc(s_sq, 1)
            for h in range(NH):
                b = h % 2
                wait(pool, z_own, h - 1)
                for m in range(2):
                    G.tensor_copy(qd[b][64 * m:64 * m + 64, 64 * m:64 * m + 64],
                                  qT[64 * m:64 * m + 64, h, SEQ:T]).then_inc(z_qs, 1)
                if 2 <= h < 6:
                    pool.wait_ge(z_qs, 2 * h + 2)
                    square(h - 2, P)
                    pool.wait_ge(s_sq, h - 1)

        def pe_attn(pe):
            pe.wait_ge(drained[0], N_O // 2)
            pe.wait_ge(drained[1], N_O // 2)
            mask_q, mask_k = maskrow[0:1, 0:P], maskrow[0:1, P:P + CHUNK]

            def scores(i, h, b, it):
                pe.wait_ge(s_qs, 2 * it + 2)
                wait(pe, s_exp, 2 * it - 2)
                kn = (i + 1) * P
                for m in range(2):
                    nc.tensor.matmul(ps[:, b, m, 0:kn], qs[b][:, m, :], head(kT, h, slice(0, kn)),
                                     start=True, stop=False)
                    mm = nc.tensor.matmul(ps[:, b, m, kn - CHUNK:kn], mask_q, mask_k, start=False, stop=True)
                mm.then_inc(s_sc, 1)

            def transposes(i, h, b, it):
                pe.wait_ge(s_pr, it + 1)
                wait(pe, s_ptc, it - 1)
                for kt in range(i + 1):
                    mm = nc.tensor.transpose(misc[:, b, kt * P:(kt + 1) * P], ex[b][:, 0, kt * P:(kt + 1) * P],
                                             ident[:])
                mm.then_inc(s_pt, 1)

            def output(i, h, b, it):
                pe.wait_ge(s_ptc, it + 1)
                wait(pe, s_oe, it - 1)
                for kt in range(i + 1):
                    mm = nc.tensor.matmul(misc[:, 2 + b, 0:P], pT[b][:, kt * P:(kt + 1) * P], vhead(kt, h),
                                          start=kt == 0, stop=kt == i)
                mm.then_inc(s_o, 1)

            def body(i, j):
                for k in range(2):
                    transposes(*item(i, j, k))
                    if not at_end(i, j, k + 2):
                        scores(*item(i, j, k + 2))
                    output(*item(i, j, k))
            for k in range(2):
                scores(*item(0, 0, k))
            prompt_pairs(pe, body)


            def cached(h, b):
                pe.wait_ge(s_ck[b], 16 * (h // 2 + 1))
                if h == 0:
                    pe.wait_ge(s_ptc, ITEMS)
                    pe.wait_ge(s_oe, ITEMS)
                wait(pe, z_ktc, h)
                for kt in range(PAST // P):
                    mm = nc.tensor.transpose(mflat[:, kt * P:(kt + 1) * P], ck[b][:, kt, :], ident[:])
                mm.then_inc(z_kt, 1)

            def scores_s(h, b):
                pe.wait_ge(z_qs, 2 * h + 2)
                pe.wait_ge(z_ktc, h + 1)
                wait(pe, z_ptc, 2 * (h - 1))
                for c in range(2):
                    mm = nc.tensor.matmul(ps[:, b, c, :], qd[b][:, :], kTc[b][:, c * 512:(c + 1) * 512],
                                          start=True, stop=True)
                mm.then_inc(z_sc, 1)

            def scores_own(h, b):
                wait(pe, z_fin, h - 1)
                nc.tensor.matmul(misc[:, 2 + b, 0:DEC], qd[b][:, :], kT[:, h, SEQ:T], start=True, stop=True,
                                 skip_group_check=True).then_inc(z_own, 1)

            for h in range(2):
                cached(h, h)
                scores_s(h, h)
            scores_own(0, 0)
            for h in range(NH):
                b = h % 2
                pe.wait_ge(z_exp, 2 * h + 2)
                for kt in range(PAST // P):
                    nc.tensor.transpose(ps[:, b].rearrange("p c n -> p (c n)")[:, kt * P:(kt + 1) * P],
                                        exS[b][:, kt * P:(kt + 1) * P], ident[:])
                nc.tensor.transpose(misc[0:DEC, 2 + b, P:2 * P], exS[b][:, PAST:PAST + DEC], ident[:]).then_inc(z_pt, 1)
                if h + 1 < NH:
                    scores_own(h + 1, 1 - b)
                if h + 2 < NH:
                    cached(h + 2, b)
                pe.wait_ge(z_ptc, 2 * h + 2)
                pe.wait_ge(s_cv[b], 16 * (h // 2 + 1))
                for kt in range(PAST // P):
                    nc.tensor.matmul(misc[:, 2 + b, 2 * P:3 * P], pTS[b][:, kt * P:(kt + 1) * P],
                                     cv[b][:, kt, :], start=kt == 0, stop=False, skip_group_check=True)
                nc.tensor.matmul(misc[:, 2 + b, 2 * P:3 * P], pTS[b][0:DEC, PAST:PAST + P], vhead(4, h, DEC),
                                 start=False, stop=True, skip_group_check=True).then_inc(z_o, 1)
                if h + 2 < NH:
                    scores_s(h + 2, b)

            for h in range(NH):
                if h == 0:
                    pe.wait_ge(s_on, 4)
                if h >= 2:
                    pe.wait_ge(s_ox, h - 1)
                for i, (t0, n) in enumerate(TT):
                    if h == 0 and i == 4:
                        pe.wait_ge(s_on, 5)
                    mm = nc.tensor.transpose(mflat[:, (h % 2) * 1024 + t0:(h % 2) * 1024 + t0 + n],
                                             otok[0:n, i, h * P:(h + 1) * P], ident[0:n, 0:n])
                mm.then_inc(s_ot, 1)

        def dve_attn(dve):
            V = nc.vector

            def maxima(i, h, b, it):
                st = sts[:, b]
                dve.wait_ge(s_sc, it + 1)
                V.reduce_max(st[:, 0:2], ps[:, b, :, 0:(i + 1) * P], axis=AX.X).then_inc(v_mx, 1)
                dve.wait_ge(v_mx, it + 1)
                V.tensor_scalar(st[:, 2:4], st[:, 0:2], -SCALE, None, ALU.mult).then_inc(s_max, 1)

            def combine(i, h, b, it):
                st = sts[:, b]
                kn = (i + 1) * P
                dve.wait_ge(s_exp, 2 * it + 2)
                V.reciprocal(st[:, 6:8], st[:, 4:6]).then_inc(v_rc, 1)
                dve.wait_ge(v_rc, 2 * it + 1)
                V.scalar_tensor_tensor(out=st[:, 8:9], in0=st[:, 4:5], scalar=small[:, 1:2], in1=st[:, 7:8],
                                       op0=ALU.mult, op1=ALU.mult).then_inc(v_rc, 1)
                dve.wait_ge(v_rc, 2 * it + 2)
                V.scalar_tensor_tensor(out=ex[b][:, 0, 0:kn], in0=ex[b][:, 1, 0:kn], scalar=st[:, 8:9],
                                       in1=ex[b][:, 0, 0:kn], op0=ALU.mult, op1=ALU.add).then_inc(s_pr, 1)

            def body(i, j):
                for k in range(2):
                    if not at_end(i, j, k + 1):
                        combine(*item(i, j, k + 1))
                    if not at_end(i, j, k + 2):
                        maxima(*item(i, j, k + 2))
            for k in range(2):
                maxima(*item(0, 0, k))
            combine(*item(0, 0, 0))
            prompt_pairs(dve, body)

            def keys(h, b):
                dve.wait_ge(z_kt, h + 1)
                wait(dve, z_sc, h - 1)
                V.tensor_copy(kTc[b][:, :], mflat[:, 0:PAST]).then_inc(z_ktc, 1)

            def maxima_s(h, b):
                st = stz[:, b]
                dve.wait_ge(z_sc, h + 1)
                V.reduce_max(st[:, 0:1], ps[:, b].rearrange("p c n -> p (c n)"), axis=AX.X).then_inc(z_big, 1)

            def shift_s(h, b):
                st = stz[:, b]
                dve.wait_ge(z_own, h + 1)
                V.reduce_max(st[:, 1:2], misc[:, 2 + b, 0:DEC], axis=AX.X).then_inc(z_st, 1)
                dve.wait_ge(z_big, h + 1)
                dve.wait_ge(z_st, 2 * h + 1)
                V.tensor_tensor(st[:, 2:3], st[:, 0:1], st[:, 1:2], ALU.max).then_inc(z_st, 1)
                dve.wait_ge(z_st, 2 * h + 2)
                V.tensor_scalar(st[:, 3:4], st[:, 2:3], -SCALE, None, ALU.mult).then_inc(z_max, 1)

            def weights(h, b):
                st = stz[:, b]
                dve.wait_ge(z_exp, 2 * h + 2)
                V.tensor_tensor(st[:, 4:5], st[:, 4:5], st[:, 5:6], ALU.add).then_inc(z_sum, 1)
                dve.wait_ge(z_sum, 2 * h + 1)
                V.reciprocal(st[:, 7:8], st[:, 4:5]).then_inc(z_sum, 1)
                dve.wait_ge(z_sum, 2 * h + 2)
                V.tensor_tensor(st[:, 6:7], st[:, 7:8], small[:, 4:5], ALU.mult).then_inc(z_w, 1)

            def finish(h, b):
                dve.wait_ge(z_ov, h + 1)
                V.scalar_tensor_tensor(out=otok[0:DEC, 4, h * P:(h + 1) * P], in0=misc[0:DEC, 2 + b, 2 * P:3 * P],
                                       scalar=stz[0:DEC, b, 6:7], in1=ov[b][:, :],
                                       op0=ALU.mult, op1=ALU.add).then_inc(z_fin, 1)

            def squares(i, n):
                if i < 4:
                    dve.wait_ge(s_sq, i + 1)
                else:
                    dve.wait_ge(z_fin, NH)
                    link(dve, V.tensor_tensor(sqb[0:n, :], otok[0:n, i, :], otok[0:n, i, :], ALU.mult))
                V.reduce_sum(ssq[0:n, i * NH:(i + 1) * NH], sqb[0:n, :].rearrange("p (h e) -> p h e", h=NH),
                             axis=AX.X).then_inc(s_nq, 1)

            def normalise(i):
                n = TT[i][1]
                o3 = otok[0:n, i].rearrange("p (h e) -> p h e", h=NH)
                V.tensor_tensor(o3, o3, nrm[0:n, 1, i * NH:(i + 1) * NH].unsqueeze(2).broadcast_to([n, NH, P]),
                                ALU.mult).then_inc(s_on, 1)

            for h in range(2):
                keys(h, h)
                maxima_s(h, h)
            shift_s(0, 0)
            for h in range(NH):
                b = h % 2
                if h + 1 < NH:
                    shift_s(h + 1, 1 - b)
                weights(h, b)
                if h == NH - 1:
                    normalise(3)
                if h + 2 < NH:
                    keys(h + 2, b)
                finish(h, b)
                if h + 2 < NH:
                    maxima_s(h + 2, b)
                if 1 <= h < 5:
                    squares(h - 1, P)
                if h == NH - 2:
                    dve.wait_ge(s_ns, 1)
                    link(dve, V.reciprocal(nrm[:, 1, 0:32], nrm[:, 0, 0:32]))
                    normalise(0)
                    normalise(1)
                    normalise(2)
            squares(4, DEC)
            dve.wait_ge(s_ns, 2)
            link(dve, V.reciprocal(nrm[0:DEC, 1, 32:40], nrm[0:DEC, 0, 32:40]))
            normalise(4)

        v_rc = sem("v_reciprocals")

        def act_attn(act):
            A = nc.scalar

            def exps(i, h, b, it):
                kn = (i + 1) * P
                act.wait_ge(s_max, it + 1)
                wait(act, s_pt, it - 1)
                for m in range(2):
                    A.activation(ex[b][:, m, 0:kn], ps[:, b, m, 0:kn], ACT.Exp, scale=SCALE,
                                 bias=sts[:, b, 2 + m:3 + m], accum_out=sts[:, b, 4 + m:5 + m]).then_inc(s_exp, 1)

            def body(i, j):
                for k in range(2):
                    i_, h, b, it = item(i, j, k)
                    act.wait_ge(s_pt, it + 1)
                    wait(act, s_o, it - 1)
                    A.copy(pT[b][:, 0:(i + 1) * P], misc[:, b, 0:(i + 1) * P]).then_inc(s_ptc, 1)
                    act.wait_ge(s_o, it + 1)
                    A.activation(otok[:, i, bass.ds(h * P, P)], misc[:, 2 + b, 0:P], ACT.Copy,
                                 scale=sts[:, b, 6:7]).then_inc(s_oe, 1)
                    if not at_end(i, j, k + 2):
                        exps(*item(i, j, k + 2))
            for k in range(2):
                exps(*item(0, 0, k))
            prompt_pairs(act, body)

            def exps_s(h, b):
                st = stz[:, b]
                act.wait_ge(z_max, h + 1)
                wait(act, z_pt, h - 1)
                A.activation(exS[b][:, 0:PAST], ps[:, b].rearrange("p c n -> p (c n)"), ACT.Exp, scale=SCALE,
                             bias=st[:, 3:4], accum_out=st[:, 4:5]).then_inc(z_exp, 1)
                A.activation(exS[b][:, PAST:PAST + DEC], misc[:, 2 + b, 0:DEC], ACT.Exp, scale=SCALE,
                             bias=st[:, 3:4], accum_out=st[:, 5:6]).then_inc(z_exp, 1)
            exps_s(0, 0)
            for h in range(NH):
                b = h % 2
                act.wait_ge(z_pt, h + 1)
                wait(act, z_o, h - 1)
                A.copy(pTS[b][:, 0:PAST], ps[:, b].rearrange("p c n -> p (c n)")).then_inc(z_ptc, 1)
                A.copy(pTS[b][0:DEC, PAST:PAST + P], misc[0:DEC, 2 + b, P:2 * P]).then_inc(z_ptc, 1)
                if h + 1 < NH:
                    exps_s(h + 1, 1 - b)
                act.wait_ge(z_o, h + 1)
                act.wait_ge(z_w, h + 1)
                wait(act, z_fin, h - 1)
                A.activation(ov[b][:, :], misc[DEC:P, 2 + b, 2 * P:3 * P], ACT.Copy,
                             scale=stz[DEC:P, b, 6:7]).then_inc(z_ov, 1)
                if h == NH - 2:
                    act.wait_ge(s_nq, 4)
                    A.activation(nrm[:, 0, 0:32], ssq[:, 0:32], ACT.Sqrt, scale=1.0 / P,
                                 bias=small[:, 0:1]).then_inc(s_ns, 1)

            act.wait_ge(s_nq, 5)
            A.activation(nrm[0:DEC, 0, 32:40], ssq[0:DEC, 32:40], ACT.Sqrt, scale=1.0 / P,
                         bias=small[0:DEC, 0:1]).then_inc(s_ns, 1)
            for h in range(NH):
                buf = (sil, hf)[h % 2]
                act.wait_ge(s_ot, h + 1)
                if h >= 2:
                    act.wait_ge(x_ready, X_ATT + h - 1)
                A.activation(buf[:, :], mflat[:, (h % 2) * 1024:(h % 2) * 1024 + T], ACT.Copy,
                             scale=small[:, 3:4]).then_inc(s_ox, 1)
                act.wait_ge(s_ox, h + 1)
                A.copy(xh[:, h, :], buf[:, :]).then_inc(xh_ready, 1)

        def pool_attn_out(pool):
            for h in range(NH):
                pool.wait_ge(xh_ready, X_ATT + h + 1)
                nc.gpsimd.tensor_tensor(xl[:, h, :], (sil, hf)[h % 2][:, :], xh[:, h, :].bitcast(F32),
                                        ALU.subtract).then_inc(x_ready, 1)

        def sp_attn(sp):
            sp.wait_ge(tile_done, N_Q)
            for h in range(NH + 1):
                if h < NH:
                    wait(sp, z_kt, h - 1)
                    sp.dma_start(ck[h % 2][:], cache_k[0].rearrange("(a p) h m d -> p a h (m d)", p=P)[:, :, h]
                                 ).then_inc(s_ck[h % 2], 16)
                v = h - 1
                if v >= 0:
                    wait(sp, z_o, v - 1)
                    sp.dma_start(cv[v % 2][:], cache_v[0].rearrange("(a p) h e -> p a h e", p=P)[:, :, v]
                                 ).then_inc(s_cv[v % 2], 16)

        s_yt = sem("y_transposed")
        s_yca = sem("y_rows_copied_act")
        s_ycd = sem("y_rows_copied_dve")
        s_yo = sem("y_stored")
        ym = Map(h_at)
        ytok = [ym(f"ytok{i}", [P, D]) for i in range(5)]

        def y_psum(i):
            n = TT[i][1]
            bank = ps[0:n, i % 2] if i % 4 < 2 else misc[0:n, 2 * (i % 2):2 * (i % 2) + 2]
            return bank.rearrange("p c n -> p (c n)")

        def pe_y(pe):
            def put(i, d):
                t0, n = TT[i]
                return nc.tensor.transpose(y_psum(i)[:, d * P:(d + 1) * P], r[:, d, t0:t0 + n], ident[:])
            for d in range(DT):
                pe.wait_ge(ln_out, 5 * DT + d + 1)
                for i in range(4):
                    mm = put(i, d)
                    if d == DT - 1:
                        mm.then_inc(s_yt, 1)
            pe.wait_ge(s_yca, 1)
            for d in range(DT):
                mm = put(4, d)
            mm.then_inc(s_yt, 1)

        def y_copies(eng, copy, tiles, done):
            for i in tiles:
                eng.wait_ge(s_yt, i + 1)
                copy(ytok[i][0:TT[i][1], :], y_psum(i)).then_inc(done, 1)

        def sp_y(sp):
            for i, (t0, n) in enumerate(TT):
                sp.wait_ge((s_yca, s_ycd)[i % 2], i // 2 + 1)
                sp.dma_start(y_prompt[0, t0:t0 + n] if i < 4 else y_sample[0], ytok[i][0:n, :]).then_inc(s_yo, 16)
            sp.wait_ge(s_yo, 80)

        def dump_r(sp, sems):
            for s_, v in sems:
                sp.wait_ge(s_, v)
            sp.dma_start(dump.rearrange("p (a b) -> p a b", a=DT), r[:]).then_inc(s_out, 16)

        block = ctx.enter_context(nc.Block())

        @block.sync
        def _(sp):
            sp_setup(sp)
            sp_ffn(sp, N_FFN00, 0, 0)
            n_out = 0
            if stop > 1:
                sp_stage(sp, N_GLU, DT, glu_v, lambda i: i * P + D, lambda i: i * P, DT, between=sp_s5)
                n_out += 4
            if stop > 2:
                sp_ffn(sp, N_FFN01, 0, 1, between=sp_states)
            elif stop > 1:
                sp_states(sp)
            if stop > 3:
                sp_plain(sp, N_KV, DT, kv_v)
                sp_ffn(sp, N_FFN10, 1, 0, between=sp_kv_rows)
                n_out += 5
            if stop > 4:
                sp_plain(sp, N_Q, DT // 2, q_v)
                sp_plain(sp, N_O, DT // 2, o_v, between=sp_attn)
            if stop > 5:
                sp_ffn(sp, N_FFN11, 1, 1)
                sp_y(sp)
            if dump is not None:
                dump_r(sp, [(ln_out, DT * stop)])
                n_out += 1
            if stop > 3:
                sp.wait_ge(s_kout, 80)
            for s_ in (s_tdw, s_tdc, s_tdt):
                sp.wait_ge(s_, 16 * DT)
            sp.wait_ge(s_out, 16 * n_out)

        @block.scalar
        def _(act):
            act_setup(act)
            act_hi(act, 0, 0, 0, DT)
            act_ffn(act, N_FFN00, 0, 0, None)
            if stop > 1:
                act_s5(act)
                act_glu(act, N_GLU, 1)
            if stop > 2:
                act_ffn(act, N_FFN01, 1, 2, True)
            if stop > 3:
                act_rope(act, N_KV, 0)
                act_v(act, N_KV + NH)
                act_kv_rows(act)
                act.wait_ge(s_kout, 80)
                act_ffn(act, N_FFN10, 2, 3, True)
            if stop > 4:
                act_rope(act, N_Q, NH)
                act_attn(act)
                act_out(act, N_O, DT, 4)
                act_ln(act, 4)
            if stop > 5:
                act_ffn(act, N_FFN11, 3, 5, None)
                y_copies(act, nc.scalar.copy, (0, 2, 4), s_yca)

        @block.vector
        def _(dve):
            dve_setup(dve)
            dve_lo(dve, 0, 0, 0, DT)
            dve_ffn(dve, N_FFN00, 0, 0)
            if stop > 1:
                dve_s5(dve)
                dve_glu(dve, N_GLU, 1)
            if stop > 2:
                dve_ffn(dve, N_FFN01, 1, 2)
            if stop > 3:
                dve_rope(dve, N_KV, 0, kT)
                dve_v(dve, N_KV + NH)
                dve_kv_rows(dve)
                dve_ffn(dve, N_FFN10, 2, 3)
            if stop > 4:
                dve_rope(dve, N_Q, NH, qT)
                dve_attn(dve)
                dve_out(dve, N_O, DT, ALPHA, 4)
                dve_ln(dve, 4)
            if stop > 5:
                dve_ffn(dve, N_FFN11, 3, 5)
                y_copies(dve, nc.vector.tensor_copy, (1, 3), s_ycd)

        @block.gpsimd
        def _(pool):
            pool_setup(pool)
            pool_ffn(pool, N_FFN00, 0, 0, None)
            if stop > 1:
                pool_s5(pool)
                pool_ln(pool, 1, lambda d: (glu_z, d + 1), X_LN1)
            if stop > 2:
                pool_ffn(pool, N_FFN01, 1, 2, X_LN2)
            if stop > 3:
                pool_ffn(pool, N_FFN10, 2, 3, X_LN3)
            if stop > 4:
                pool_attn(pool)
                pool_attn_out(pool)
                pool_ln(pool, 4, lambda d: (drained[d % 2], (N_O + d) // 2 + 1), X_LN4)
            if stop > 5:
                pool_ffn(pool, N_FFN11, 3, 5, None)

        @block.tensor
        def _(pe):
            pe_setup(pe)
            pe_ffn(pe, N_FFN00, 0, X_IN, 0)
            if stop > 1:
                pe_s5(pe)
                pe_stage(pe, N_GLU, DT, DT, xh, xl, x_ready, X_GELU, hooks=ln_hooks(1, 2))
            if stop > 2:
                pe_ffn(pe, N_FFN01, 1, X_LN1, 2)
            if stop > 3:
                pe_stage(pe, N_KV, DT, DT, xh, xl, x_ready, X_LN2)
                pe_kv_rows(pe)
                pe_ffn(pe, N_FFN10, 2, X_LN2, 3)
            if stop > 4:
                pe_stage(pe, N_Q, DT // 2, DT, xh, xl, x_ready, X_LN3)
                pe_attn(pe)
                pe_stage(pe, N_O, DT // 2, DT, xh, xl, x_ready, X_ATT,
                         hooks=ln_hooks(4, 1))
            if stop > 5:
                pe_ffn(pe, N_FFN11, 3, X_LN4, 5)
                pe_y(pe)


def rope_tables():
    half = HD // 2
    inv = (10000.0 ** (-np.arange(half) / half)).astype(np.float32)
    pos = np.concatenate([np.arange(SEQ), PAST + np.arange(DEC)]).astype(np.float32)
    ang = (inv[:, None] * pos[None, :]).astype(np.float32)
    c, s = np.cos(ang).astype(np.float32), np.sin(ang).astype(np.float32)
    return {"rope_cos": np.concatenate([c, c, c, c]), "rope_sin": np.concatenate([-s, s, -s, s])}


_INS = ["x_prompt", "x_sample", "cache_k", "cache_v", "state_ssm_re", "state_ssm_im", "ln_g", "ln_b",
        "ffn_w_in", "ffn_w_out", "ssm_a_re", "ssm_a_im", "ssm_log_dt", "ssm_b_re", "ssm_b_im",
        "ssm_c_re", "ssm_c_im", "ssm_d", "ssm_w_glu", "attn_w_q", "attn_w_kv", "attn_lam",
        "attn_subln_g", "attn_w_o"]
_OUTS = [(1, SEQ, D), (1, DEC, D), (1, 1, GROUPS, PS), (1, 1, GROUPS, PS), (1, SEQ, NH, 2, HD),
         (1, SEQ, NH, 2 * HD), (1, 1, GROUPS, PS), (1, 1, GROUPS, PS), (1, DEC, NH, 2, HD),
         (1, DEC, NH, 2 * HD)]


def kernel(**inputs):
    import numpy as _np
    import concourse.bacc as _bacc
    from concourse import mybir as _mybir
    from concourse.bass_utils import run_bass_kernel_spmd as _run

    nc = _bacc.Bacc("TRN2", target_bir_lowering=False, num_devices=1)
    arrays, args = {}, []
    consts = rope_tables()
    for name in _INS + list(consts):
        a = _np.ascontiguousarray(inputs[name] if name in inputs else consts[name])
        arrays[f"in_{name}_dram"] = a
        args.append(nc.dram_tensor(f"in_{name}_dram", a.shape, _mybir.dt.from_np(a.dtype), kind="ExternalInput").ap())
    for i, shape in enumerate(_OUTS):
        args.append(nc.dram_tensor(f"out_{i}_dram", shape, F32, kind="ExternalOutput").ap())
    build(nc, *args)
    r = _run(nc, [arrays], core_ids=[0])
    return tuple(r.results[0][f"out_{i}_dram"] for i in range(len(_OUTS)))
```
